# Optimizing a Trainium2 kernel written in Bass

```python
import math
import jax, jax.numpy as jnp
from jax import lax
import numpy as np

D_MODEL = 1024
BATCH = 1
SEQ = 512
DEPTH = 1

A_HEADS = 8
A_HEAD_DIM = 64
A_WIDTH = A_HEADS * A_HEAD_DIM
DILATED_PATTERNS = ((128, 1), (512, 4), (2048, 16))
BAND_BLOCK = 128
REL_BUCKETS = 32
REL_MAX_DIST = 2048
M_HEADS = 8
M_NOPE = 64
M_ROPE = 32
M_V = 64
M_Q_LORA = 768
M_KV_LORA = 256
M_WIDTH = M_HEADS * M_V
ROPE_THETA = 10000.0
Q_BLOCK = 128
D_FF = -(-8 * D_MODEL // (3 * 256)) * 256
N_MOD = 6
EPS = 1e-6
NEG_INF = -1e30
IN_SIZES = (3 * A_WIDTH, M_Q_LORA, M_KV_LORA, M_ROPE, D_MODEL, D_MODEL)
IN_WIDTH = 3 * A_WIDTH + M_Q_LORA + M_KV_LORA + M_ROPE + 2 * D_MODEL
IN_SPLIT_POINTS = (3 * A_WIDTH,
                   3 * A_WIDTH + M_Q_LORA,
                   3 * A_WIDTH + M_Q_LORA + M_KV_LORA,
                   3 * A_WIDTH + M_Q_LORA + M_KV_LORA + M_ROPE,
                   3 * A_WIDTH + M_Q_LORA + M_KV_LORA + M_ROPE + D_MODEL)


def _rmsnorm(x, g):
    xf = x.astype(jnp.float32)
    inv = lax.rsqrt(jnp.mean(xf * xf, axis=-1, keepdims=True) + EPS)
    return (xf * inv).astype(x.dtype) * g

def _t5_bucket(dist):
    max_exact = REL_BUCKETS // 2
    d = jnp.maximum(dist, 1).astype(jnp.float32)
    log_b = max_exact + (jnp.log(d / max_exact) / math.log(REL_MAX_DIST / max_exact)
                         * (REL_BUCKETS - max_exact)).astype(jnp.int32)
    log_b = jnp.minimum(log_b, REL_BUCKETS - 1)
    return jnp.where(dist < max_exact, dist, log_b)

def _dilated_pattern(q, k, v, rel_bias, window, dilation):
    B, H, S, Dh = q.shape
    n_back = window // dilation
    blk = BAND_BLOCK
    L = S // dilation
    pad_end = (-L) % blk
    Lp = L + pad_end
    nb = Lp // blk

    def to_sub(t):
        t = t.reshape(B, H, L, dilation, Dh).transpose(0, 1, 3, 2, 4)
        return jnp.pad(t, ((0, 0), (0, 0), (0, 0), (0, pad_end), (0, 0)))

    def band(t):
        tp = jnp.pad(t, ((0, 0), (0, 0), (0, 0), (blk, 0), (0, 0)))
        prev = tp[:, :, :, :Lp].reshape(B, H, dilation, nb, blk, Dh)
        cur = t.reshape(B, H, dilation, nb, blk, Dh)
        return jnp.concatenate([prev, cur], axis=4)

    qb = to_sub(q).reshape(B, H, dilation, nb, blk, Dh)
    kb = band(to_sub(k))
    vb = band(to_sub(v))
    s = jnp.einsum('bhrnqd,bhrnkd->bhrnqk', qb, kb).astype(jnp.float32) * (Dh ** -0.5)
    sub_dist = (jnp.arange(blk)[:, None] + blk) - jnp.arange(2 * blk)[None, :]
    in_band = (sub_dist >= 0) & (sub_dist <= n_back)
    bucket = _t5_bucket(jnp.clip(sub_dist, 0, n_back) * dilation)
    bias = rel_bias[:, bucket].astype(jnp.float32)
    key_idx = jnp.arange(nb)[:, None] * blk + jnp.arange(2 * blk)[None, :] - blk
    mask = in_band[None] & (key_idx >= 0)[:, None, :]
    s = jnp.where(mask, s + bias[None, :, None, None], NEG_INF)
    lse = jax.nn.logsumexp(s, axis=-1)
    p = jnp.exp(s - lse[..., None])
    o = jnp.einsum('bhrnqk,bhrnkd->bhrnqd', p.astype(v.dtype), vb)
    o = o.reshape(B, H, dilation, Lp, Dh)[:, :, :, :L].transpose(0, 1, 3, 2, 4).reshape(B, H, S, Dh)
    lse = lse.reshape(B, H, dilation, Lp)[:, :, :, :L].transpose(0, 1, 3, 2).reshape(B, H, S)
    return o, lse

def _dilated_attention(a_qkv, rel_bias):
    B, S, _ = a_qkv.shape
    qkv = a_qkv.reshape(B, S, 3, A_HEADS, A_HEAD_DIM).transpose(2, 0, 3, 1, 4)
    q, k, v = qkv[0], qkv[1], qkv[2]
    outs, lses = [], []
    for window, dilation in DILATED_PATTERNS:
        o, l = _dilated_pattern(q, k, v, rel_bias, window, dilation)
        outs.append(o)
        lses.append(l)
    w = jax.nn.softmax(jnp.stack(lses), axis=0)
    o = jnp.einsum('gbhs,gbhsd->bhsd', w.astype(v.dtype), jnp.stack(outs))
    return o.transpose(0, 2, 1, 3).reshape(B, S, A_WIDTH)

def _rope(x, pos):
    half = x.shape[-1] // 2
    freqs = ROPE_THETA ** (-jnp.arange(half, dtype=jnp.float32) / half)
    ang = pos.astype(jnp.float32)[..., None] * freqs
    ang = ang.reshape(ang.shape[:2] + (1,) * (x.ndim - 3) + (half,))
    cos, sin = jnp.cos(ang), jnp.sin(ang)
    x1 = x[..., :half].astype(jnp.float32)
    x2 = x[..., half:].astype(jnp.float32)
    return jnp.concatenate([x1 * cos - x2 * sin, x1 * sin + x2 * cos], axis=-1).astype(x.dtype)

def _mla(c_q, c_kv, k_r, positions, g_q_lora, w_uq, g_kv_lora, w_ukv):
    B, S, _ = c_q.shape
    q = jnp.einsum('bsl,lhd->bshd', _rmsnorm(c_q, g_q_lora), w_uq)
    kv = jnp.einsum('bsl,lhd->bshd', _rmsnorm(c_kv, g_kv_lora), w_ukv)
    q_nope, q_rope = q[..., :M_NOPE], _rope(q[..., M_NOPE:], positions)
    k_nope, v = kv[..., :M_NOPE], kv[..., M_NOPE:]
    k_rope = _rope(k_r, positions)
    scale = (M_NOPE + M_ROPE) ** -0.5
    nq = S // Q_BLOCK
    qn_b = jnp.moveaxis(q_nope.reshape(B, nq, Q_BLOCK, M_HEADS, M_NOPE), 1, 0)
    qr_b = jnp.moveaxis(q_rope.reshape(B, nq, Q_BLOCK, M_HEADS, M_ROPE), 1, 0)
    kpos = jnp.arange(S)

    def block(args):
        qn, qr, i = args
        s = (jnp.einsum('bqhd,bkhd->bhqk', qn, k_nope)
             + jnp.einsum('bqhr,bkr->bhqk', qr, k_rope)).astype(jnp.float32) * scale
        qpos = i * Q_BLOCK + jnp.arange(Q_BLOCK)
        s = jnp.where(kpos[None, :] <= qpos[:, None], s, NEG_INF)
        p = jax.nn.softmax(s, axis=-1)
        return jnp.einsum('bhqk,bkhd->bqhd', p.astype(v.dtype), v)

    o = lax.map(block, (qn_b, qr_b, jnp.arange(nq)))
    return jnp.moveaxis(o, 0, 1).reshape(B, S, M_WIDTH)

def _hybrid_mixer(h, positions, rel_bias, w_in, g_q_lora, w_uq, g_kv_lora, w_ukv,
                  w_up_a, w_up_b, w_o):
    proj = h @ w_in
    a_qkv, c_q, c_kv, k_r, gate_a, gate_b = jnp.split(proj, IN_SPLIT_POINTS, axis=-1)
    y_a = _dilated_attention(a_qkv, rel_bias) @ w_up_a
    y_b = _mla(c_q, c_kv, k_r, positions, g_q_lora, w_uq, g_kv_lora, w_ukv) @ w_up_b
    merged = jax.nn.sigmoid(gate_a) * y_a + jax.nn.sigmoid(gate_b) * y_b
    return merged @ w_o

def _swiglu(h, w_gate, w_up, w_down):
    return (jax.nn.silu(h @ w_gate) * (h @ w_up)) @ w_down

def first_inputs(seed: int = 0) -> dict:
    key = jax.random.key(seed)
    ks = jax.random.split(key, 20)
    f32 = jnp.float32

    def nrm(k, shape, fan_in, mult=1.0):
        return jax.random.normal(k, shape, f32) * (mult * fan_in ** -0.5)

    def gain(k, shape):
        return 1.0 + 0.05 * jax.random.normal(k, shape, f32)

    x = jax.random.normal(ks[0], (BATCH, SEQ, D_MODEL), f32)
    c = jax.random.normal(ks[1], (BATCH, D_MODEL), f32)
    offsets = jax.random.randint(ks[2], (BATCH, 1), 0, 4096, dtype=jnp.int32)
    positions = offsets + jnp.arange(SEQ, dtype=jnp.int32)[None, :]
    return {
        "x": x,
        "c": c,
        "positions": positions,
        "rel_bias": 0.5 * jax.random.normal(ks[3], (A_HEADS, REL_BUCKETS), f32),
        "w_ada": nrm(ks[4], (DEPTH, D_MODEL, N_MOD * D_MODEL), D_MODEL, 0.5),
        "b_ada": 0.02 * jax.random.normal(ks[5], (DEPTH, N_MOD * D_MODEL), f32),
        "g_mix": gain(ks[6], (DEPTH, D_MODEL)),
        "w_in": nrm(ks[7], (DEPTH, D_MODEL, IN_WIDTH), D_MODEL),
        "g_q_lora": gain(ks[8], (DEPTH, M_Q_LORA)),
        "w_uq": nrm(ks[9], (DEPTH, M_Q_LORA, M_HEADS, M_NOPE + M_ROPE), M_Q_LORA),
        "g_kv_lora": gain(ks[10], (DEPTH, M_KV_LORA)),
        "w_ukv": nrm(ks[11], (DEPTH, M_KV_LORA, M_HEADS, M_NOPE + M_V), M_KV_LORA),
        "w_up_a": nrm(ks[12], (DEPTH, A_WIDTH, D_MODEL), A_WIDTH),
        "w_up_b": nrm(ks[13], (DEPTH, M_WIDTH, D_MODEL), M_WIDTH),
        "w_o": nrm(ks[14], (DEPTH, D_MODEL, D_MODEL), D_MODEL),
        "g_ffn": gain(ks[15], (DEPTH, D_MODEL)),
        "w_gate": nrm(ks[16], (DEPTH, D_MODEL, D_FF), D_MODEL),
        "w_up": nrm(ks[17], (DEPTH, D_MODEL, D_FF), D_MODEL),
        "w_down": nrm(ks[18], (DEPTH, D_FF, D_MODEL), D_FF),
        "g_final": gain(ks[19], (D_MODEL,)),
    }

def first_block(x, c, positions, rel_bias, w_ada, b_ada, g_mix, w_in, g_q_lora, w_uq,
              g_kv_lora, w_ukv, w_up_a, w_up_b, w_o, g_ffn, w_gate, w_up, w_down, g_final):
    cond = jax.nn.silu(c)
    for layer in range(DEPTH):
        mod = (cond @ w_ada[layer] + b_ada[layer])[:, None, :]
        sh1, sc1, gt1, sh2, sc2, gt2 = jnp.split(mod, N_MOD, axis=-1)
        h = _rmsnorm(x, g_mix[layer]) * (1.0 + sc1) + sh1
        x = x + gt1 * _hybrid_mixer(h, positions, rel_bias, w_in[layer], g_q_lora[layer],
                                    w_uq[layer], g_kv_lora[layer], w_ukv[layer],
                                    w_up_a[layer], w_up_b[layer], w_o[layer])
        h = _rmsnorm(x, g_ffn[layer]) * (1.0 + sc2) + sh2
        x = x + gt2 * _swiglu(h, w_gate[layer], w_up[layer], w_down[layer])
    return _rmsnorm(x, g_final)


DEPTH_2 = 2

GRID_W = 64
CTX_LEN = 256

MIX_WIDTH = D_MODEL
FOURIER_WIDTH = MIX_WIDTH // 4
N_FOURIER_HEADS = 4
FOURIER_HEAD_DIM = FOURIER_WIDTH // N_FOURIER_HEADS
POOL_WIDTH = MIX_WIDTH // 4
POOL_WINDOWS = (2, 4, 8, 16)
POOL_GROUP_DIM = POOL_WIDTH // len(POOL_WINDOWS)
ATTN_WIDTH = MIX_WIDTH // 2
HEAD_DIM = 128
N_Q_HEADS = ATTN_WIDTH // HEAD_DIM
N_KV_HEADS = 2
Q_PER_KV = N_Q_HEADS // N_KV_HEADS
KV_WIDTH = N_KV_HEADS * HEAD_DIM
ROPE_HALF = HEAD_DIM // 2

F_OFF = 0
P_OFF = F_OFF + FOURIER_WIDTH
Q_OFF = P_OFF + POOL_WIDTH
K_OFF = Q_OFF + ATTN_WIDTH
V_OFF = K_OFF + KV_WIDTH
IN_WIDTH_2 = V_OFF + KV_WIDTH

N_EXPERTS = 16
EC_CAPACITY_FACTOR = 2
EXPERT_FF = D_MODEL


def rms_norm(x, g):
    xf = x.astype(jnp.float32)
    y = xf * lax.rsqrt(jnp.mean(xf * xf, axis=-1, keepdims=True) + EPS)
    return (y * g.astype(jnp.float32)).astype(x.dtype)

def modulate(x, g, shift, scale):
    xf = x.astype(jnp.float32)
    y = xf * lax.rsqrt(jnp.mean(xf * xf, axis=-1, keepdims=True) + EPS) * g.astype(jnp.float32)
    y = y * (1.0 + scale.astype(jnp.float32)) + shift.astype(jnp.float32)
    return y.astype(x.dtype)

def axial_angles(n):
    rows = n // GRID_W
    row = jnp.repeat(jnp.arange(rows, dtype=jnp.float32), GRID_W)
    col = jnp.tile(jnp.arange(GRID_W, dtype=jnp.float32), rows)
    inv = ROPE_THETA ** (-jnp.arange(0, ROPE_HALF, 2, dtype=jnp.float32) / ROPE_HALF)
    return row[:, None] * inv[None, :], col[:, None] * inv[None, :]

def rope_half(x, ang):
    cos = jnp.cos(ang)[None, :, None, :]
    sin = jnp.sin(ang)[None, :, None, :]
    xf = x.astype(jnp.float32)
    x1, x2 = xf[..., : ROPE_HALF // 2], xf[..., ROPE_HALF // 2:]
    return jnp.concatenate([x1 * cos - x2 * sin, x2 * cos + x1 * sin], axis=-1).astype(x.dtype)

def axial_rope(x, ang_row, ang_col):
    return jnp.concatenate([rope_half(x[..., :ROPE_HALF], ang_row),
                            rope_half(x[..., ROPE_HALF:], ang_col)], axis=-1)

def attend(q, k, v):
    s = jnp.einsum('bqhgd,bkhd->bhgqk', q, k).astype(jnp.float32) * (HEAD_DIM ** -0.5)
    p = jax.nn.softmax(s, axis=-1).astype(v.dtype)
    return jnp.einsum('bhgqk,bkhd->bqhgd', p, v)

def blocked_attention(q, k, v):
    B, L = q.shape[0], q.shape[1]
    nb = L // Q_BLOCK
    qb = q.reshape(B, nb, Q_BLOCK, N_KV_HEADS, Q_PER_KV, HEAD_DIM).transpose(1, 0, 2, 3, 4, 5)
    ob = lax.map(lambda qi: attend(qi, k, v), qb)
    return ob.transpose(1, 0, 2, 3, 4, 5).reshape(B, L, ATTN_WIDTH)

def fourier_mix(f, w):
    B, n, _ = f.shape
    fh = f.astype(jnp.float32).reshape(B, n, N_FOURIER_HEADS, FOURIER_HEAD_DIM).transpose(0, 2, 1, 3)
    fr = jnp.real(jnp.fft.fft2(fh, axes=(-2, -1), norm="ortho"))
    fr = fr.transpose(0, 2, 1, 3).reshape(B, n, FOURIER_WIDTH).astype(f.dtype)
    return fr @ w

def pool_mix(p, w, scale):
    B, n, _ = p.shape
    pf = p.astype(jnp.float32)
    cs = jnp.concatenate([jnp.zeros((B, 1, POOL_WIDTH), jnp.float32), jnp.cumsum(pf, axis=1)], axis=1)
    t = jnp.arange(n)
    outs = []
    for gi, win in enumerate(POOL_WINDOWS):
        lo = jnp.clip(t - win // 2, 0, n)
        hi = jnp.clip(t + win // 2, 0, n)
        sl = slice(gi * POOL_GROUP_DIM, (gi + 1) * POOL_GROUP_DIM)
        csg = cs[..., sl]
        s = jnp.take(csg, hi, axis=1) - jnp.take(csg, lo, axis=1)
        cnt = (hi - lo).astype(jnp.float32)[None, :, None]
        outs.append(s / cnt - pf[..., sl])
    d = jnp.stack(outs, axis=2).astype(p.dtype)
    y = jnp.einsum('bngc,gcd->bngd', d, w).reshape(B, n, POOL_WIDTH)
    return y * scale

def expert_choice_ffn(h, w_router, w_gate, w_up, w_down):
    B, n, D = h.shape
    cap = EC_CAPACITY_FACTOR * n // N_EXPERTS
    logits = jnp.einsum('bnd,de->bne', h, w_router).astype(jnp.float32)
    aff = jax.nn.softmax(logits, axis=-1)
    g, idx = lax.top_k(aff.transpose(0, 2, 1), cap)
    xs = jax.vmap(lambda hb, ib: hb[ib])(h, idx)
    a = jnp.einsum('becd,edf->becf', xs, w_gate)
    u = jnp.einsum('becd,edf->becf', xs, w_up)
    y = jnp.einsum('becf,efd->becd', jax.nn.silu(a) * u, w_down)
    y = y * g[..., None].astype(y.dtype)
    return jax.vmap(lambda yb, ib: jnp.zeros((n, D), yb.dtype).at[ib.reshape(-1)].add(yb.reshape(-1, D)))(y, idx)

def second_inputs(seed: int = 0) -> dict:
    key = jax.random.key(seed)
    ks = jax.random.split(key, 20)
    nrm = jax.random.normal
    f32 = jnp.float32
    D = D_MODEL
    return {
        "x": nrm(ks[0], (BATCH, SEQ, D), f32),
        "c": nrm(ks[1], (BATCH, D), f32),
        "ctx": nrm(ks[2], (BATCH, CTX_LEN, D), f32),
        "c_ctx": nrm(ks[3], (D,), f32),
        "ada_w": nrm(ks[4], (DEPTH_2, D, 6 * D), f32) * (0.5 * D ** -0.5),
        "ada_b": nrm(ks[5], (DEPTH_2, 6 * D), f32) * 0.02,
        "norm1_g": 1.0 + 0.02 * nrm(ks[6], (DEPTH_2, D), f32),
        "norm2_g": 1.0 + 0.02 * nrm(ks[7], (DEPTH_2, D), f32),
        "w_in": nrm(ks[8], (DEPTH_2, D, IN_WIDTH_2), f32) * D ** -0.5,
        "w_fourier": nrm(ks[9], (DEPTH_2, FOURIER_WIDTH, FOURIER_WIDTH), f32) * FOURIER_WIDTH ** -0.5,
        "w_pool": nrm(ks[10], (DEPTH_2, len(POOL_WINDOWS), POOL_GROUP_DIM, POOL_GROUP_DIM), f32) * POOL_GROUP_DIM ** -0.5,
        "pool_scale": 1.0 + 0.1 * nrm(ks[11], (DEPTH_2, POOL_WIDTH), f32),
        "q_norm_g": 1.0 + 0.02 * nrm(ks[12], (DEPTH_2, HEAD_DIM), f32),
        "k_norm_g": 1.0 + 0.02 * nrm(ks[13], (DEPTH_2, HEAD_DIM), f32),
        "w_out": nrm(ks[14], (DEPTH_2, MIX_WIDTH, D), f32) * MIX_WIDTH ** -0.5,
        "w_router": nrm(ks[15], (DEPTH_2, D, N_EXPERTS), f32) * D ** -0.5,
        "w_gate": nrm(ks[16], (DEPTH_2, N_EXPERTS, D, EXPERT_FF), f32) * D ** -0.5,
        "w_up": nrm(ks[17], (DEPTH_2, N_EXPERTS, D, EXPERT_FF), f32) * D ** -0.5,
        "w_down": nrm(ks[18], (DEPTH_2, N_EXPERTS, EXPERT_FF, D), f32) * EXPERT_FF ** -0.5,
    }

def second_block(x, c, ctx, c_ctx, ada_w, ada_b, norm1_g, norm2_g, w_in, w_fourier, w_pool, pool_scale,
              q_norm_g, k_norm_g, w_out, w_router, w_gate, w_up, w_down):
    B, L, D = x.shape
    Lc = ctx.shape[1]
    ang_row, ang_col = axial_angles(L)
    sc = jax.nn.silu(c)
    scc = jax.nn.silu(c_ctx)
    for i in range(DEPTH_2):
        last = i == DEPTH_2 - 1
        sh1, sc1, g1, sh2, sc2, g2 = jnp.split((sc @ ada_w[i] + ada_b[i])[:, None, :], 6, axis=-1)
        csh1, csc1, cg1, csh2, csc2, cg2 = jnp.split((scc @ ada_w[i] + ada_b[i])[None, None, :], 6, axis=-1)

        hx = modulate(x, norm1_g[i], sh1, sc1)
        hc = modulate(ctx, norm1_g[i], csh1, csc1)
        px_all = hx @ w_in[i]
        kvc = hc @ w_in[i][:, K_OFF:]
        kc = rms_norm(kvc[..., :KV_WIDTH].reshape(B, Lc, N_KV_HEADS, HEAD_DIM), k_norm_g[i])
        vc = kvc[..., KV_WIDTH:].reshape(B, Lc, N_KV_HEADS, HEAD_DIM)

        qx = rms_norm(px_all[..., Q_OFF:K_OFF].reshape(B, L, N_Q_HEADS, HEAD_DIM), q_norm_g[i])
        kx = rms_norm(px_all[..., K_OFF:V_OFF].reshape(B, L, N_KV_HEADS, HEAD_DIM), k_norm_g[i])
        vx = px_all[..., V_OFF:].reshape(B, L, N_KV_HEADS, HEAD_DIM)
        qx = axial_rope(qx, ang_row, ang_col)
        kx = axial_rope(kx, ang_row, ang_col)
        k_all = jnp.concatenate([kx, kc], axis=1)
        v_all = jnp.concatenate([vx, vc], axis=1)
        ax = blocked_attention(qx, k_all, v_all)
        ox = jnp.concatenate([fourier_mix(px_all[..., F_OFF:P_OFF], w_fourier[i]),
                              pool_mix(px_all[..., P_OFF:Q_OFF], w_pool[i], pool_scale[i]),
                              ax], axis=-1) @ w_out[i]
        x_new = x + g1 * ox

        x_new = x_new + g2 * expert_choice_ffn(modulate(x_new, norm2_g[i], sh2, sc2),
                                               w_router[i], w_gate[i], w_up[i], w_down[i])

        if not last:
            pc_all = hc @ w_in[i][:, :K_OFF]
            qc = rms_norm(pc_all[..., Q_OFF:K_OFF].reshape(B, Lc, N_KV_HEADS, Q_PER_KV, HEAD_DIM), q_norm_g[i])
            ac = attend(qc, kc, vc).reshape(B, Lc, ATTN_WIDTH)
            oc = jnp.concatenate([fourier_mix(pc_all[..., F_OFF:P_OFF], w_fourier[i]),
                                  pool_mix(pc_all[..., P_OFF:Q_OFF], w_pool[i], pool_scale[i]),
                                  ac], axis=-1) @ w_out[i]
            ctx = ctx + cg1 * oc
            ctx = ctx + cg2 * expert_choice_ffn(modulate(ctx, norm2_g[i], csh2, csc2),
                                                w_router[i], w_gate[i], w_up[i], w_down[i])
        x = x_new
    return x


def setup_inputs(seed=0):
    out = dict(first_inputs(seed))
    for name, value in second_inputs(seed + 1).items():
        if name != "x":
            out[name + "_2"] = value
    return out


def reference(
    x, c, positions, rel_bias, w_ada, b_ada, g_mix, w_in, g_q_lora, w_uq, g_kv_lora, w_ukv,
    w_up_a, w_up_b, w_o, g_ffn, w_gate, w_up, w_down, g_final, c_2, ctx_2, c_ctx_2, ada_w_2,
    ada_b_2, norm1_g_2, norm2_g_2, w_in_2, w_fourier_2, w_pool_2, pool_scale_2, q_norm_g_2,
    k_norm_g_2, w_out_2, w_router_2, w_gate_2, w_up_2, w_down_2,
):
    x = first_block(
        x, c, positions, rel_bias, w_ada, b_ada, g_mix, w_in, g_q_lora, w_uq, g_kv_lora, w_ukv,
        w_up_a, w_up_b, w_o, g_ffn, w_gate, w_up, w_down, g_final,
    )
    return second_block(
        x, c_2, ctx_2, c_ctx_2, ada_w_2, ada_b_2, norm1_g_2, norm2_g_2, w_in_2, w_fourier_2,
        w_pool_2, pool_scale_2, q_norm_g_2, k_norm_g_2, w_out_2, w_router_2, w_gate_2, w_up_2,
        w_down_2,
    )


_drawn_inputs = setup_inputs


def setup_inputs(seed=0):
    import zlib

    import numpy as np

    out = dict(_drawn_inputs(seed))
    spreads = {}
    factors = {'rel_bias': 3.728,
     'b_ada': 2.903,
     'g_mix': 8.0,
     'g_q_lora': 8.0,
     'g_kv_lora': 8.0,
     'g_ffn': 3.269,
     'ctx_2': 4.459,
     'norm1_g_2': 8.0,
     'norm2_g_2': 6.864,
     'q_norm_g_2': 8.0,
     'k_norm_g_2': 8.0}
    for name, (base, spread) in spreads.items():
        noise = np.random.default_rng([zlib.crc32(name.encode()), seed]).standard_normal(out[name].shape)
        drawn = base * np.exp(spread * noise) if base else spread * noise
        out[name] = __import__('jax').numpy.asarray(drawn.astype(out[name].dtype))
    for name, factor in factors.items():
        out[name] = (out[name] * factor).astype(out[name].dtype)
    return out
```

```python
from contextlib import ExitStack

import numpy as np

import concourse.bass as bass
from concourse import mybir

NCONST = 11
P = 128
D = 1024
DC = D // P
T, TC = 512, 4
C, CC = 256, 2
A = T + C
AC = TC + CC
EPS = 1e-6
NEG = -1e30
HA, HD = 8, 64
HM, NOPE, ROPE, MV = 8, 64, 32, 64
QK = NOPE + ROPE
QL, KVL = 768, 256
FF = 2816
FC = FF // P
BUCKETS = 32
RL = 640
LAYERS = 2
HQ, HKV, HB = 4, 2, 128
NE = 16
CAPX, CAPC = 2 * T // NE, 2 * C // NE
SLOTS = 6
SLOT = 2048
BANKS = 8

F32 = mybir.dt.float32
I32 = mybir.dt.int32
ALU = mybir.AluOpType
ACT = mybir.ActivationFunctionType
AX = mybir.AxisListType.X

PCOL = {}
ROWS = []
for _name, _n in (("g_mix", 8), ("g_q_lora", 6), ("g_kv_lora", 2), ("g_ffn", 8), ("g_final", 8),
                  ("norm1_g_2", 16), ("norm2_g_2", 16), ("pool_scale_2", 4), ("q_norm_g_2", 2), ("k_norm_g_2", 2),
                  ("b_ada", 48), ("c", 8), ("ada_b_2", 96), ("c_2", 8), ("c_ctx_2", 8)):
    PCOL[_name] = sum(n for _, n in ROWS)
    ROWS.append((_name, _n))
NPAR = sum(n for _, n in ROWS)

VECTORS = [("b1", v, 1) for v in range(2, 6)] + [(0, v, 2) for v in range(6)] \
    + [(1, v, 2 if v < 2 else 1) for v in range(6)]
SIDE = [(n, j) for n in range(len(VECTORS)) for j in range(4)]
SIDE_AT = {}


def _place_sides():
    left = list(range(len(SIDE)))
    for stage, tiles, each in (("qk", 4, 1), ("va", 2, 1), ("cq", 3, 1), ("ckv", 1, 1), ("kr", 1, 1),
                               ("uq", 4, 1), ("ukv", 1, 1), ("wo", 4, 1), ("ffn", 22, 2)):
        for t in range(tiles):
            SIDE_AT[(stage, t)] = [left.pop(0) for _ in range(each) if left]
    assert not left


_place_sides()


class Ring:

    def __init__(self, slots):
        self.slots, self.at, self.pos = slots, {}, 0
        self.used = [0] * slots
        self.body = None

    def add(self, stage, n=1):
        for i in range(n):
            s = self.pos % self.slots
            self.at[(stage, i)] = [s, self.used[s], 0]
            if self.body is not None:
                self.body.append((stage, i))
            self.used[s] += 1
            self.pos += 1

    def loop(self):
        self.body, self.before = [], list(self.used)

    def end(self, trips):
        per = [u - b for u, b in zip(self.used, self.before)]
        for key in self.body:
            self.at[key][2] = per[self.at[key][0]]
        self.used = [b + trips * p for b, p in zip(self.before, per)]
        self.body = None


SETS = {0: ("x", "c"), 1: ("x",)}
SET = {"x": dict(n=CAPX, parts=P // CAPX, w=D * CAPX // P, tok=T, tc=TC, t0=0, at=0),
       "c": dict(n=CAPC, parts=P // CAPC, w=D * CAPC // P, tok=C, tc=CC, t0=TC, at=T)}


def plan():
    b, r = Ring(BANKS), Ring(SLOTS)

    def side(stage, t):
        for s in SIDE_AT.get((stage, t), ()):
            n, j = SIDE[s]
            if j == 0 and n > 0:
                b.add(("mod", n - 1))
            r.add(("side", s))

    b.add("par", 2)
    b.add("xin", 2 * DC)
    b.add("rel", 2)
    for v in (0, 1):
        r.add(("ada", v), 4)
        b.add(("adamod", v))
    b.add("n1")
    for t in range(4):
        r.add(("qk", t)); b.add(("qk", t), 2); side("qk", t)
    for t in range(2):
        r.add(("va", t)); b.add(("va", t), TC); side("va", t)

    def attn(tag, heads, qi, segs, kc):
        b.add((tag, "S", 0), qi * segs)
        for h in range(heads):
            if h + 1 < heads:
                b.add((tag, "S", h + 1), qi * segs)
            b.add((tag, "T", h), kc)
            b.add((tag, "O", h))

    attn("A", HA, TC, 1, TC)
    for t in range(3):
        r.add(("cq", t)); b.add(("cq", t), 2); side("cq", t)
    r.add(("ckv", 0)); b.add(("ckv", 0), 2); side("ckv", 0)
    r.add(("kr", 0)); b.add(("kr", 0)); side("kr", 0)
    b.add("nq"); b.add("nkv")
    b.add("krr")
    for t in range(4):
        r.add(("uq", t)); b.add(("uq", t), 2); side("uq", t)
    b.add("qr", HM)
    r.add(("ukv", 0)); b.add("kn", HM); b.add("vm", TC); side("ukv", 0)
    attn("M", HM, TC, 1, TC)
    for half in range(2):
        r.add(("upa", half)); r.add(("upb", half))
        for t in (2 * half, 2 * half + 1):
            r.add(("ga", t)); r.add(("gb", t))
            b.add(("merge", t), 8)
    for t in range(4):
        r.add(("wo", t)); b.add(("wo", t), 2); side("wo", t)
    b.add("n2")
    for t in range(FC // 2):
        for k in range(2):
            r.add(("ffn", 2 * t + k))
            side("ffn", 2 * t + k)
        b.add(("ffn", t), 4)
    b.add(("mod", len(VECTORS) - 1))
    r.add("down", FC // 2); b.add("down", DC)
    b.add("nf")
    for i in range(LAYERS):
        sets = SETS[i]
        b.add((i, "n1x")); b.add((i, "n1c"))
        for t in range(6):
            r.add((i, "in", t))
            b.add((i, "in", t), 6 if t == 5 else 4 if (i == 0 or t == 4) else 2)
        b.add((i, "qkn"), len(qk_units(i)))
        b.add((i, "rot"), HQ + HKV)
        for s in sets:
            b.add((i, "f1", s), SET[s]["tc"])
            r.add((i, "dft", s), 2 if s == "x" else 1)
            b.add((i, "f2", s), 2)
            b.add((i, "f3", s), 2)
            b.add((i, "pw", s), 2)
        for s in sets:
            nk = A if s == "x" else C
            attn((i, s), HQ, SET[s]["tc"], 2 if s == "x" else 1, nk // P)
        for t in range(4):
            r.add((i, "out", t)); b.add((i, "out", t), 2 * len(sets))
        for s in sets:
            b.add((i, "n2" + s))
        b.add((i, "lg"))
        b.add((i, "ht"), 2 * (AC if i == 0 else TC))
        b.add((i, "aT"), len(sets)); b.add((i, "posT"))

        def gather(e):
            for s in sets:
                b.add((i, e, "XG", s))

        def turn(e):
            for s in sets:
                b.add((i, e, "XT", s))

        gather("first"); turn("first")
        b.loop(); r.loop()
        for e in range(2):
            r.add((i, e, "w"), 12)
            for m in ("G", "U"):
                for s in sets:
                    b.add((i, e, m, s))
            gather(e)
            turn(e)
            for s in sets:
                b.add((i, e, "T", s))
            for s in sets:
                b.add((i, e, "S", s), DC)
            for s in sets:
                b.add((i, e, "Y", s))
            for s in sets:
                b.add((i, e, "PT", s))
        b.end(NE // 2); r.end(NE // 2)
        for s in sets:
            b.add((i, "last", "S", s), DC)
    b.add("yout", 2 * TC)
    return b, r


def qk_units(i):
    u = [(ch, 0, T) for ch in range(HQ + HKV)]
    return u + [(ch, T, C) for ch in (range(HQ + HKV) if i == 0 else range(HQ, HQ + HKV))]


def constants():
    k = {}
    k["ident"] = np.eye(P, dtype=np.float32)
    k["flip"] = np.eye(P, dtype=np.float32)[::-1].copy()
    r = np.arange(RL)
    delta = 511 - r
    dist = np.maximum(delta, 0)
    logb = 16 + np.floor(np.maximum(np.log(np.maximum(dist, 1) / 16) / np.log(128) * 16, 0) + 1e-9).astype(int)
    bucket = np.where(dist < 16, dist, np.minimum(logb, BUCKETS - 1))
    k["onehot"] = (bucket[None, :] == np.arange(BUCKETS)[:, None]).astype(np.float32)
    count = (delta >= 0) * ((delta <= 128) * 1 + (delta % 4 == 0) * 1 + (delta % 16 == 0) * 1)
    lnc = np.where(count > 0, np.log(np.maximum(count, 1)), NEG).astype(np.float32)
    k["lncount"] = np.broadcast_to(lnc, (HA, RL)).copy()
    u = np.arange(512)
    k["causal"] = np.where(np.arange(P)[:, None] - u[None, :] + 384 >= 0, 0.0, NEG).astype(np.float32)
    half = ROPE // 2
    f = (10000.0 ** (-np.arange(half) / half)).astype(np.float32)
    k["ropecol"] = np.stack([np.concatenate([f, f]), np.concatenate([-np.ones(half), np.ones(half)])], 1)\
        .astype(np.float32)
    perm = np.zeros((P, P), np.float32)
    for p in range(NOPE, QK):
        j = p - NOPE
        perm[NOPE + (j + half) % ROPE, p] = 1
    k["perm1"] = perm
    perm = np.zeros((P, P), np.float32)
    for p in range(P):
        perm[(p // 64) * 64 + (p + 32) % 64, p] = 1
    k["perm2"] = perm
    inv = (10000.0 ** (-np.arange(0, 64, 2) / 64)).astype(np.float32)
    n = np.arange(T)
    row, col = (n // 64).astype(np.float32), (n % 64).astype(np.float32)
    ar, ac = inv[:, None] * row[None], inv[:, None] * col[None]
    ang = np.concatenate([ar, ar, ac, ac], 0).astype(np.float32).astype(np.float64)
    sign = np.where(np.arange(P) % 64 < 32, -1.0, 1.0)[:, None]
    k["axial"] = np.concatenate([np.cos(ang), np.sin(ang) * sign], 1).astype(np.float32)
    d = np.arange(64)
    a = 2 * np.pi * (np.outer(d, d) % 64) / 64
    blk = np.zeros((P, 2, P), np.float64)
    for g in range(2):
        blk[64 * g:64 * g + 64, 0, 64 * g:64 * g + 64] = np.cos(a)
        blk[64 * g:64 * g + 64, 1, 64 * g:64 * g + 64] = np.sin(a)
    k["dft64"] = blk.reshape(P, 2 * P).astype(np.float32)
    for name, m in (("x", T), ("c", C)):
        t = np.arange(m)
        a = 2 * np.pi * (np.outer(t, t) % m) / m
        s = 1 / np.sqrt(m * 64)
        k["dft" + name] = np.concatenate([np.cos(a) * s, -np.sin(a) * s], 0).astype(np.float32)
    ic = np.zeros((P, 2, A), np.float64)
    for g, win in enumerate((2, 4, 8, 16)):
        for m, at in ((T, 0), (C, T)):
            t = np.arange(m)
            cnt = np.clip(t + win // 2, 0, m) - np.clip(t - win // 2, 0, m)
            ic[64 * (g % 2):64 * (g % 2) + 64, g // 2, at:at + m] = 1.0 / cnt
    k["invcount"] = ic.reshape(P, 2 * A).astype(np.float32)
    k["iota"] = np.broadcast_to(np.arange(CAPX, dtype=np.float32), (P, CAPX)).copy()
    return k


def build(nc, I, out):
    bank_plan, ring_plan = plan()
    with ExitStack() as ctx:
        def sb(name, shape, dt=F32):
            return ctx.enter_context(nc.sbuf_tensor(name, shape, dt))

        def sem(name):
            return ctx.enter_context(nc.semaphore(name))

        ps = [ctx.enter_context(nc.psum_tensor(f"ps{i}", [P, 512], F32)) for i in range(BANKS)]
        ring = sb("ring", [P, SLOTS, SLOT])
        XC = sb("XC", [P, DC, A])
        HT = sb("HT", [P, DC, A])
        WN = 22016
        W = sb("W", [P, WN])
        acc = sb("acc", [P, 2, D])
        inv = sb("inv", [P, 512])
        ident, ones = sb("ident", [P, P]), sb("ones", [P, 512])
        iota = sb("iota", [P, CAPX])
        perm, flip = sb("perm", [P, P]), sb("flip", [P, P])
        rope = sb("rope", [P, 2, T])
        dft64 = sb("dft64", [P, 2 * P])
        wp = sb("wp", [P, LAYERS, 2, 64])
        wr = sb("wr", [P, LAYERS, DC, NE])
        prow = sb("prow", [P, 2, P])
        pcol = sb("pcol", [P, NPAR])
        cond = sb("cond", [P, 24])
        mod1 = sb("mod1", [P, 6, DC])
        mod2 = sb("mod2", [P, LAYERS, 2, 6, DC])
        acol = sb("acol", [P, 2, DC])
        ac2 = sb("ac2", [P, LAYERS, 2, 2, DC])
        stat = sb("stat", [P, 3, 2, TC])
        freq = sb("freq", [P, 2])
        relT = sb("relT", [P, HA])
        rev_dram = nc.dram_tensor("rev_bias", (HA, RL), F32).ap()

        full = [sem(f"bank_full{i}") for i in range(BANKS)]
        free = [sem(f"bank_free{i}") for i in range(BANKS)]
        loaded = [sem(f"tile_loaded{i}") for i in range(SLOTS)]
        used = [sem(f"tile_used{i}") for i in range(SLOTS)]
        names = ("rows_loaded tok_loaded consts_loaded pos_loaded axial_loaded rev_stored bias_loaded0 "
                 "bias_loaded1 mask_loaded ones_ready pcol_ready cond_ready x_ready rev_ready ang_ready sincos_ready "
                 "sq_ready lat_ready ms_ready inv_ready scaled h_ready acol_ready proj_ready qn_ready "
                 "q_ready smax_ready exp_ready p_ready merged x_new pd_ready lg_ready ex_ready aff_ready "
                 "a_ready tok_ready sel_ready fin_ready out_stored dve_step kb_ready").split()
        S = {n: sem(n) for n in names}

        xtok = HT[:, :, :].rearrange("p c t -> p (c t)").rearrange("p (t d) -> p t d", d=D)

        class Counts:

            def __init__(self, own=None):
                self.own, self.n = own, 0
                self.seen, self.it, self.per, self.given = {}, None, {}, {}

            def grown(self, value, per):
                return value if self.it is None else self.it * per + value

            def next(self, name, k=1):
                self.seen[name] = self.seen.get(name, 0) + k
                return S[name], self.grown(self.seen[name], self.per.get(name, 0))

            def stepped(self):
                self.n += 1
                return S[self.own]

            def steps(self):
                return S[self.own], self.grown(self.n, self.per.get(self.own, 0))

            def signs(self, name):
                self.given[name] = self.given.get(name, 0) + 1
                return S[name]

            def own_signs(self, name):
                return S[name], self.given[name]

            def begin(self, it, per):
                self.it, self.per = it, per
                self.base, self.base_n = dict(self.seen), self.n

            def end(self, trips):
                for name, value in self.seen.items():
                    base = self.base.get(name, 0)
                    assert value - base == self.per.get(name, 0), (name, value - base)
                    self.seen[name] = base + trips * (value - base)
                if self.own is not None:
                    assert self.n - self.base_n == self.per.get(self.own, 0), self.n - self.base_n
                    self.n = self.base_n + trips * (self.n - self.base_n)
                self.it = None

            def bank(self, stage, i=0):
                return ps[bank_plan.at[(stage, i)][0]]

            def fills(self, stage, i=0):
                return full[bank_plan.at[(stage, i)][0]]

            def freed(self, stage, i=0):
                return free[bank_plan.at[(stage, i)][0]]

            def full(self, stage, i=0):
                s, u, per = bank_plan.at[(stage, i)]
                return full[s], self.grown(u + 1, per)

            def read(self, stage, i=0, before=False, after=0):
                s, u, per = bank_plan.at[(stage, i)]
                v = u + 1 - (per if before else 0) + (per * (after - 1) if after else 0)
                assert v > 0
                return free[s], self.grown(v, per)

            def free(self, stage, i=0, after=()):
                s, u, per = bank_plan.at[(stage, i)]
                want = {s: (u, per)}
                for stage2, i2, before in after:
                    s2, u2, per2 = bank_plan.at[(stage2, i2)]
                    u2 += 1 - (per2 if before else 0)
                    want[s2] = (max(u2, want.get(s2, (0, 0))[0]), per2)
                return [(free[s2], self.grown(u2, per2)) for s2, (u2, per2) in want.items() if u2 > 0]

            def landed(self, stage, i=0):
                s, u, per = ring_plan.at[(stage, i)]
                return loaded[s], self.grown(u, per) * 16 + 16

            def slot(self, stage, i=0):
                return ring[:, ring_plan.at[(stage, i)][0], :]

            def vacant(self, stage, i=0):
                s, u, per = ring_plan.at[(stage, i)]
                return [(used[s], self.grown(u, per))] if u > 0 else []

            def used_up(self, stage, i=0):
                return used[ring_plan.at[(stage, i)][0]]

            def spent(self, stage, i=0):
                s, u, per = ring_plan.at[(stage, i)]
                return used[s], self.grown(u + 1, per)

        block = ctx.enter_context(nc.Block())

        def wv(at, n, m):
            return W[:, at:at + n * m].rearrange("p (n m) -> p n m", n=n)

        OA, OB = wv(0, 4, T), wv(2048, 4, T)
        QKA, VA = wv(4096, 8, T), wv(8192, TC, 512)
        QM, KM, VM = wv(4096, HM, T), wv(8192, HM, T), wv(12288, TC, 512)
        CQ, CKV = wv(14336, 6, T), wv(17408, 2, T)
        P1 = wv(14336, 8, 512)
        PT1 = wv(18432, 4, 512)
        MB = wv(20480, 2, 512)
        MASK = MB[:, 0:1, :]
        MERGED = wv(4096, DC, T)
        GS = wv(14336, 4, 512)
        ACTF = wv(0, FC, T)
        SG = wv(11264, 4, T)
        ONEHOT, REV = W[0:BUCKETS, 0:RL], W[0:HA, RL:2 * RL]
        LNC = W[0:HA, 2 * RL:3 * RL]
        ctok = W[:, 4096:4096 + 2 * D].rearrange("p (t d) -> p t d", d=D)
        POSI = W[:, 8192:8192 + T].bitcast(I32)
        ANG = wv(8704, 4, T)
        SQ6, KRT = wv(4096, 6, T), wv(18432, 2, T)
        RTMP = wv(19456, 2, T)
        invcount = wv(20480, 2, A)
        wf = W[:, 18432:19456].rearrange("p (l k n) -> p l k n", l=LAYERS, k=2)
        FB, PB = wv(0, 2, A), wv(1536, 2, A)
        QKB = wv(3072, 6, A)
        VB = wv(7680, AC, 256)
        UB = wv(9216, AC, 512)
        FR = wv(12288, 2, A)
        ZX, ZC = 8 + T + 1 + 8, 8 + C + 1 + 8
        Z = wv(13824, 2, ZX + ZC)
        PD = wv(13824 + 2 * (ZX + ZC), 2, A)
        P2 = wv(9216, 2 * TC, A)
        PT2 = wv(15360, AC, 512)
        HTOK = wv(0, AC, D)
        LG = wv(6144, AC, NE)
        L1 = W[:, 6240:6240 + 3 * AC].rearrange("p (a b) -> p a b", a=3)
        PA = W[:, 6300:6300 + 18 * 2 * AC].rearrange("p (e k) -> p e k", e=18)
        CUR = W[:, 6520:6520 + 2 * 2 * AC].rearrange("p (e k) -> p e k", e=2)
        TOP = W[0:NE, 6560:6568]
        AT = W[0:NE, 6656:6656 + A]
        MK = W[0:NE, 7424:7424 + A]
        RK = W[0:NE, 8192:8192 + A]
        at = 9472
        E = {}
        for s, o in SET.items():
            n, w, tc = o["n"], o["w"], o["tc"]
            blocks = w // P
            for key, size in (("P", tc * n), ("Pg", 2 * tc * P), ("XG", w), ("XS", 2 * w), ("SG", w), ("ACT", w),
                              ("AT", w), ("Y", w), ("PT", 2 * tc * P)):
                E[key + s] = W[:, at:at + size]
                at += size
        assert at <= WN, at
        SBX = {s: SET[s]["w"] // P for s in SET}

        def sect(name, v, n=DC):
            return pcol[:, PCOL[name] + v * n:PCOL[name] + (v + 1) * n]

        @block.sync
        def _(sp):
            me = Counts()

            def put(stage, i, src, dst):
                for tile_used, count in me.vacant(stage, i):
                    sp.wait_ge(tile_used, count)
                sp.dma_start(dst(me.slot(stage, i)), src).then_inc(me.landed(stage, i)[0], 16)

            def cols(w, c0, n, k=DC):
                return w[:, c0:c0 + n].rearrange("(k p) n -> p k n", p=P), \
                    (lambda t: t[:, 0:k * n].rearrange("p (k n) -> p k n", k=k))

            def rows(w, k0, c0=0, n=D):
                return w[k0 * P:(k0 + 2) * P, c0:c0 + n].rearrange("(k p) n -> p k n", p=P), \
                    (lambda t: t[:, 0:2 * n].rearrange("p (k n) -> p k n", k=2))

            def side(stage, t):
                for s in SIDE_AT.get((stage, t), ()):
                    n, j = SIDE[s]
                    blk, v, _ = VECTORS[n]
                    w = I["w_ada"][0] if blk == "b1" else I["ada_w_2"][blk]
                    put(("side", s), 0, *rows(w, 2 * j, v * D))

            for v in (0, 1):
                for j in range(4):
                    put(("ada", v), j, *rows(I["w_ada"][0], 2 * j, v * D))
            w_in = I["w_in"][0]
            for t in range(4):
                put(("qk", t), 0, *cols(w_in, t * 256, 256)); side("qk", t)
            for t in range(2):
                put(("va", t), 0, *cols(w_in, 1024 + t * 256, 256)); side("va", t)
            for t in range(3):
                put(("cq", t), 0, *cols(w_in, 1536 + t * 256, 256)); side("cq", t)
            put(("ckv", 0), 0, *cols(w_in, 1536 + QL, 256)); side("ckv", 0)
            g0 = 1536 + QL + KVL
            put(("kr", 0), 0, *cols(w_in, g0, ROPE)); side("kr", 0)
            w_uq = I["w_uq"][0].rearrange("l h d -> l (h d)")
            for t in range(4):
                put(("uq", t), 0, *cols(w_uq, t * 2 * QK, 2 * QK, 6)); side("uq", t)
            put(("ukv", 0), 0, *cols(I["w_ukv"][0].rearrange("l h d -> l (h d)"), 0, 1024, 2)); side("ukv", 0)
            for half in range(2):
                put(("upa", half), 0, *cols(I["w_up_a"][0], 512 * half, 512, 4))
                put(("upb", half), 0, *cols(I["w_up_b"][0], 512 * half, 512, 4))
                for t in (2 * half, 2 * half + 1):
                    put(("ga", t), 0, *cols(w_in, g0 + ROPE + 256 * t, 256))
                    put(("gb", t), 0, *cols(w_in, g0 + ROPE + D + 256 * t, 256))
            for t in range(4):
                put(("wo", t), 0, *cols(I["w_o"][0], 256 * t, 256)); side("wo", t)
            for t in range(FC // 2):
                for k, name in enumerate(("w_gate", "w_up")):
                    put(("ffn", 2 * t + k), 0, *cols(I[name][0], 256 * t, 256)); side("ffn", 2 * t + k)
            for t in range(FC // 2):
                put("down", t, *rows(I["w_down"][0], 2 * t))
            for i in range(LAYERS):
                for t in range(6):
                    put((i, "in", t), 0, *cols(I["w_in_2"][i], 256 * t, 256))
                for s in SETS[i]:
                    k = SET[s]["tok"]
                    if s == "x":
                        for j in range(2):
                            put((i, "dft", s), j, *cols(I["dftx"][j * T:(j + 1) * T, :], 0, T, TC))
                    else:
                        put((i, "dft", s), 0, *cols(I["dftc"], 0, C, 4))
                for t in range(4):
                    put((i, "out", t), 0, *cols(I["w_out_2"][i], 256 * t, 256))
                flat = {m: I[m][i].rearrange("e k n -> (e k) n") for m in ("w_gate_2", "w_up_2", "w_down_2")}
                with sp.Fori(0, NE // 2) as it:
                    me.it = it
                    for e in range(2):
                        for m, name in enumerate(("w_gate_2", "w_up_2", "w_down_2")):
                            for j in range(4):
                                src = flat[name][bass.ds(it * (2 * D) + (e * D + 2 * j * P), 2 * P), :]
                                put((i, e, "w"), 4 * m + j, src.rearrange("(k p) n -> p k n", p=P),
                                    lambda t: t[:, 0:2 * D].rearrange("p (k n) -> p k n", k=2))
                    me.it = None
            for t in range(TC):
                sp.wait_ge(*me.next("fin_ready", 1))
                sp.dma_start(out[0, t * P:(t + 1) * P, :], HTOK[:, t, :]).then_inc(S["out_stored"], 16)
            sp.wait_ge(S["out_stored"], 16 * TC)

        @block.gpsimd
        def _(pool):
            me = Counts()
            k = 0
            for t in range(TC):
                pool.dma_start(xtok[:, t, :], I["x"][0, t * P:(t + 1) * P, :]).then_inc(S["tok_loaded"], 16)
            for t in range(CC):
                pool.dma_start(ctok[:, t, :], I["ctx_2"][0, t * P:(t + 1) * P, :]).then_inc(S["tok_loaded"], 16)
            for dst, src in ((perm[:, :], I["perm1"]), (iota[:, :], I["iota"]), (flip[:, :], I["flip"]), (ONEHOT, I["onehot"]),
                             (LNC, I["lncount"]), (freq[NOPE:QK, :], I["ropecol"]), 
                             (dft64[:, :], I["dft64"]),
                             (wp[:, 0], I["w_pool_2"][0].rearrange("(g h) c d -> (h c) g d", h=2)),
                             (wp[:, 1], I["w_pool_2"][1].rearrange("(g h) c d -> (h c) g d", h=2)),
                             (wr[:, 0], I["w_router_2"][0].rearrange("(k p) n -> p k n", p=P)),
                             (wr[:, 1], I["w_router_2"][1].rearrange("(k p) n -> p k n", p=P))):
                pool.dma_start(dst, src).then_inc(S["consts_loaded"], 16)
                k += 1
            assert k == NCONST
            pool.wait_ge(*me.next("rev_ready"))
            pool.dma_start(rev_dram, REV).then_inc(S["rev_stored"], 16)
            pool.wait_ge(S["rev_stored"], 16)
            for h in range(HA):
                if h >= 2:
                    pool.wait_ge(S["smax_ready"], TC * (h - 1))
                src = bass.AP(rev_dram.tensor, h * RL, [[1, P], [1, 512]])
                pool.dma_start(MB[:, h % 2, :], src).then_inc(S[f"bias_loaded{h % 2}"], 16)
            pool.wait_ge(S["smax_ready"], TC * HA)
            pool.dma_start(MASK[:, 0, :], I["causal"]).then_inc(S["mask_loaded"], 16)
            pool.wait_ge(S["merged"], 1)
            pool.dma_start(rope[:, :, :].rearrange("p a b -> p (a b)"), I["axial"]).then_inc(S["axial_loaded"], 16)
            pool.dma_start(perm[:, :], I["perm2"]).then_inc(S["axial_loaded"], 16)
            pool.dma_start(invcount[:, :, :].rearrange("p a b -> p (a b)"), I["invcount"])\
                .then_inc(S["axial_loaded"], 16)
            for i in range(LAYERS):
                pool.dma_start(wf[:, i], I["w_fourier_2"][i].rearrange("(k p) n -> p k n", p=P))\
                    .then_inc(S["axial_loaded"], 16)

        NROWS = len(ROWS)

        @block.scalar
        def _(act):
            me = Counts()
            act.dma_start(ident[:, :], I["ident"]).then_inc(S["rows_loaded"], 16)
            r = 0
            for name, n in ROWS:
                src = I[name]
                dst = prow[r % P:r % P + n, r // P, :]
                act.dma_start(dst, src).then_inc(S["rows_loaded"], 16)
                r += n
            act.dma_start(POSI[NOPE:QK, :], I["positions"].to_broadcast([ROPE, T])).then_inc(S["pos_loaded"], 16)
            act.dma_start(relT[0:BUCKETS, :], I["rel_bias"].rearrange("h b -> b h"),
                          allow_slow_non_contiguous=True).then_inc(S["pos_loaded"], 16)

            def norm(bankname, n, cnt, src, sq, b=None, dst=None, waits=()):
                for name, k in waits:
                    act.wait_ge(*me.next(name, k))
                for c in range(cnt):
                    act.activation(sq(c), src(c), ACT.Square).then_inc(S["sq_ready"], 1)
                act.wait_ge(*me.next("ms_ready"))
                act.activation(inv[:, 0:n], inv[:, 0:n], ACT.Sqrt).then_inc(S["inv_ready"], 1)
                if b is not None:
                    for c in range(cnt):
                        act.wait_ge(*me.next("scaled"))
                        act.activation(dst(c), dst(c), ACT.Identity, bias=b(c)).then_inc(S["h_ready"], 1)

            def attn(tag, heads, qi_n, nk, kc_n, pbuf, ptbuf, causal):
                def exps(h):
                    for qi in range(qi_n):
                        act.wait_ge(*me.next("smax_ready"))
                        n = P * (qi + 1) if causal else nk
                        row = pbuf[:, TC * (h % 2) + qi, 0:n]
                        act.activation(row, row, ACT.Exp, bias=stat[:, 0, h % 2, qi:qi + 1],
                                       accum_out=stat[:, 1, h % 2, qi:qi + 1]).then_inc(S["exp_ready"], 1)

                exps(0)
                for h in range(heads):
                    if h + 1 < heads:
                        exps(h + 1)
                    for kc in range(kc_n):
                        q0 = P * kc if causal else 0
                        act.wait_ge(*me.full((tag, "T", h), kc))
                        b = me.bank((tag, "T", h), kc)
                        act.activation(ptbuf[:, kc, q0:P * qi_n], b[:, q0:P * qi_n], ACT.Copy).then_inc(
                            me.freed((tag, "T", h), kc), 1)

            act.wait_ge(*me.next("pcol_ready"))
            act.activation(cond[:, 0:8], sect("c", 0), ACT.Silu).then_inc(S["cond_ready"], 1)
            act.activation(cond[:, 8:24], pcol[:, PCOL["c_2"]:PCOL["c_2"] + 16], ACT.Silu)\
                .then_inc(S["cond_ready"], 1)
            act.wait_ge(*me.next("ang_ready"))
            act.activation(rope[NOPE:QK, 1, :], ANG[NOPE:QK, 2, :], ACT.Sin).then_inc(S["sincos_ready"], 1)
            act.wait_ge(*me.next("ang_ready"))
            act.activation(rope[NOPE:QK, 0, :], ANG[NOPE:QK, 3, :], ACT.Sin).then_inc(S["sincos_ready"], 1)
            h1 = lambda c: HT[:, c, 0:T]
            x1 = lambda c: XC[:, c, 0:T]
            norm("n1", T, DC, x1, h1, lambda c: mod1[:, 0, c:c + 1], h1, [("x_ready", 1), ("acol_ready", 1)])
            attn("A", HA, TC, T, TC, P1, PT1, True)
            norm("nq", T, 6, lambda c: CQ[:, c, :], lambda c: SQ6[:, c, :], waits=[("proj_ready", 1)])
            norm("nkv", T, 2, lambda c: CKV[:, c, :], lambda c: SQ6[:, c, :], waits=[("proj_ready", 1)])
            for t in range(4):
                for j in range(2):
                    act.wait_ge(*me.full(("uq", t), j))
                    b = me.bank(("uq", t), j)
                    act.activation(QM[0:QK, 2 * t + j, :], b[0:QK, :], ACT.Copy,
                                              scale=float(np.float32(QK ** -0.5)))\
                        .then_inc(me.freed(("uq", t), j), 1)
            attn("M", HM, TC, T, TC, P1, PT1, True)
            for t in range(4):
                for j in range(2):
                    if t or j:
                        act.wait_ge(*me.next("merged"))
                    for k in range(2):
                        act.wait_ge(*me.full(("merge", t), 4 * j + 2 * k + 1))
                        b = me.bank(("merge", t), 4 * j + 2 * k + 1)
                        act.activation(GS[:, k, :], b[:, :], ACT.Sigmoid).then_inc(
                            me.freed(("merge", t), 4 * j + 2 * k + 1), 1)
            act.wait_ge(*me.next("merged"))
            norm("n2", T, DC, x1, h1, lambda c: mod1[:, 3, c:c + 1], h1, [("x_new", 1)])
            for t in range(FC // 2):
                for j in range(2):
                    if t:
                        act.wait_ge(*me.read(("ffn", t - 1), 2 + j))
                    act.wait_ge(*me.full(("ffn", t), j))
                    b = me.bank(("ffn", t), j)
                    act.activation(SG[:, j, :], b[:, :], ACT.Silu).then_inc(me.freed(("ffn", t), j), 1)
            norm("nf", T, DC, x1, h1, waits=[("x_new", 1)])

            for i in range(LAYERS):
                sets = SETS[i]
                hx = lambda c: HT[:, c, 0:T]
                hc = lambda c: HT[:, c, T:A]
                xc = lambda c: XC[:, c, T:A]
                norm("n1x", T, DC, x1, hx, lambda c: mod2[:, i, 0, 0, c:c + 1], hx, [("x_ready", 1)])
                norm("n1c", C, DC, xc, hc, lambda c: mod2[:, i, 1, 0, c:c + 1], hc)
                for k, (ch, a0, n) in enumerate(qk_units(i)):
                    if k == 0:
                        act.wait_ge(*me.next("proj_ready"))
                    act.activation(RTMP[:, 0, 0:n], QKB[:, ch, a0:a0 + n], ACT.Square).then_inc(S["sq_ready"], 1)
                    act.wait_ge(*me.next("ms_ready"))
                    act.activation(inv[:, 0:n], inv[:, 0:n], ACT.Sqrt).then_inc(S["inv_ready"], 1)
                for s in sets:
                    attn((i, s), HQ, SET[s]["tc"], A if s == "x" else C, (A if s == "x" else C) // P, P2, PT2, False)
                norm("n2x", T, DC, x1, hx, lambda c: mod2[:, i, 0, 3, c:c + 1], hx, [("x_new", 1)])
                if "c" in sets:
                    norm("n2c", C, DC, xc, hc, lambda c: mod2[:, i, 1, 3, c:c + 1], hc)
                act.wait_ge(*me.next("lg_ready"))
                na = AC if i == 0 else TC
                lg = LG[:, 0:na, :].rearrange("p a b -> p (a b)")
                act.activation(lg, lg, ACT.Exp).then_inc(S["ex_ready"], 1)

                def turn(e, par):
                    for s in sets:
                        act.wait_ge(*me.full((i, e, "XT", s)))
                        b = me.bank((i, e, "XT", s))
                        w = SET[s]["w"]
                        act.activation(E["XS" + s][:, par * w:(par + 1) * w], b[:, 0:w], ACT.Copy).then_inc(
                            me.freed((i, e, "XT", s)), 1)

                turn("first", 0)
                with act.Fori(0, NE // 2) as it:
                    me.begin(it, {})
                    for e in range(2):
                        for s in sets:
                            w = SET[s]["w"]
                            act.wait_ge(*me.full((i, e, "G", s)))
                            b = me.bank((i, e, "G", s))
                            act.activation(E["SG" + s], b[:, 0:w], ACT.Silu).then_inc(me.freed((i, e, "G", s)), 1)
                        turn(e, (e + 1) % 2)
                        for s in sets:
                            w = SET[s]["w"]
                            act.wait_ge(*me.full((i, e, "T", s)))
                            b = me.bank((i, e, "T", s))
                            act.activation(E["AT" + s], b[:, 0:w], ACT.Copy).then_inc(me.freed((i, e, "T", s)), 1)
                        for s in sets:
                            w = SET[s]["w"]
                            act.wait_ge(*me.full((i, e, "Y", s)))
                            b = me.bank((i, e, "Y", s))
                            act.activation(E["Y" + s], b[:, 0:w], ACT.Copy).then_inc(me.freed((i, e, "Y", s)), 1)
                    me.end(NE // 2)

        @block.vector
        def _(dve):
            v = nc.vector
            me = Counts("dve_step")
            v.memset(ones[:, :], 1.0).then_inc(S["ones_ready"], 1)
            v.memset(rope[0:NOPE, 0, :], 1.0).then_inc(me.stepped(), 1)
            v.memset(rope[0:NOPE, 1, :], 0.0).then_inc(me.stepped(), 1)
            for k in range(2):
                n = min(P, NPAR - P * k)
                dve.wait_ge(*me.full("par", k))
                b = me.bank("par", k)
                v.tensor_copy(pcol[:, P * k:P * k + n], b[:, 0:n]).then_inc(me.freed("par", k), 1)
            dve.wait_ge(*me.read("par", 0))
            dve.wait_ge(*me.read("par", 1))
            dve.sem_inc(S["pcol_ready"], 1)

            def mod_take(n):
                blk, vec, sets = VECTORS[n]
                dve.wait_ge(*me.full(("mod", n)))
                b = me.bank(("mod", n))
                if blk == "b1":
                    last = v.tensor_tensor(mod1[:, vec, :], b[:, 0:DC], sect("b_ada", vec), ALU.add)
                else:
                    for s in range(sets):
                        last = v.tensor_tensor(mod2[:, blk, s, vec, :], b[:, s * DC:(s + 1) * DC],
                                               sect("ada_b_2", 6 * blk + vec), ALU.add)
                last.then_inc(me.freed(("mod", n)), 1)
                if vec in (1, 4):
                    dve.wait_ge(*me.read(("mod", n)))
                    base = PCOL["norm1_g_2" if vec == 1 else "norm2_g_2"]
                    if blk == "b1":
                        v.scalar_tensor_tensor(acol[:, 1, :], mod1[:, 4, :], 1.0, sect("g_ffn", 0),
                                                       ALU.add, ALU.mult).then_inc(me.stepped(), 1)
                    else:
                        for s in range(sets):
                            g = pcol[:, base + blk * DC:base + (blk + 1) * DC]
                            v.scalar_tensor_tensor(ac2[:, blk, s, vec // 4, :], mod2[:, blk, s, vec, :], 1.0,
                                                           g, ALU.add, ALU.mult).then_inc(me.stepped(), 1)

            def ada(stage, j_tile, j, csets):
                dve.wait_ge(*me.landed(stage, j_tile))
                tile = me.slot(stage, j_tile).rearrange("p (k n) -> p k n", k=2)
                for kk in range(2):
                    kc = 2 * j + kk
                    for s, c0 in enumerate(csets):
                        col = cond[:, c0 + kc:c0 + kc + 1]
                        if kc == 0:
                            ins = v.tensor_scalar(acc[:, s, :], tile[:, kk, :], col, None, ALU.mult)
                        else:
                            dve.wait_ge(*me.steps())
                            ins = v.scalar_tensor_tensor(acc[:, s, :], tile[:, kk, :], col, acc[:, s, :],
                                                         ALU.mult, ALU.add)
                        if kk == 1 and s == len(csets) - 1:
                            ins.then_inc(me.used_up(stage, j_tile), 1)
                        else:
                            ins.then_inc(me.stepped(), 1)
                dve.wait_ge(*me.spent(stage, j_tile))

            def side(stage, t):
                for sd in SIDE_AT.get((stage, t), ()):
                    n, j = SIDE[sd]
                    if j == 0 and n > 0:
                        mod_take(n - 1)
                    blk, vec, sets = VECTORS[n]
                    ada(("side", sd), 0, j, (0,) if blk == "b1" else (8, 16)[:sets])

            for c in range(DC):
                dve.wait_ge(*me.full("xin", 2 * c))
                b = me.bank("xin", 2 * c)
                v.tensor_copy(XC[:, c, 0:T], b[:, :]).then_inc(me.freed("xin", 2 * c), 1)
                dve.wait_ge(*me.full("xin", 2 * c + 1))
                b = me.bank("xin", 2 * c + 1)
                v.tensor_copy(XC[:, c, T:A], b[:, 0:C]).then_inc(me.freed("xin", 2 * c + 1), 1)
            for c in range(DC):
                dve.wait_ge(*me.read("xin", 2 * c))
                dve.wait_ge(*me.read("xin", 2 * c + 1))
            dve.sem_inc(S["x_ready"], 1)
            dve.wait_ge(S["consts_loaded"], 16 * NCONST)
            dve.wait_ge(*me.full("rel", 0))
            b = me.bank("rel", 0)
            v.tensor_tensor(REV[:, 0:512], b[0:HA, :], LNC[:, 0:512], ALU.add).then_inc(me.freed("rel", 0), 1)
            dve.wait_ge(*me.full("rel", 1))
            b = me.bank("rel", 1)
            v.tensor_tensor(REV[:, 512:RL], b[0:HA, 0:RL - 512], LNC[:, 512:RL], ALU.add).then_inc(
                me.freed("rel", 1), 1)
            dve.wait_ge(*me.read("rel", 0))
            dve.wait_ge(*me.read("rel", 1))
            dve.sem_inc(S["rev_ready"], 1)
            R_ = slice(NOPE, QK)
            dve.wait_ge(S["pos_loaded"], 32)
            v.tensor_copy(ANG[R_, 1, :], POSI[R_, :]).then_inc(me.stepped(), 1)
            dve.wait_ge(*me.steps())
            v.tensor_scalar(ANG[R_, 0, :], ANG[R_, 1, :], freq[R_, 0:1], None, ALU.mult).then_inc(me.stepped(), 1)
            dve.wait_ge(*me.steps())
            C1, C2 = 6.28125, float(np.float32(2 * np.pi - 6.28125) )
            C2 = float(np.float32(int((2 * np.pi - 6.28125) * 2 ** 20) / 2 ** 20))
            C3 = float(2 * np.pi - C1 - C2)
            MAGIC = float(1.5 * 2 ** 23)
            for dst, turn_, shift in ((2, 0.0, 0.0), (3, 0.25, float(np.pi / 2))):
                v.tensor_scalar(ANG[R_, 1, :], ANG[R_, 0, :], float(1 / (2 * np.pi)), turn_,
                                         ALU.mult, ALU.add).then_inc(me.stepped(), 1)
                dve.wait_ge(*me.steps())
                v.tensor_scalar(ANG[R_, 1, :], ANG[R_, 1, :], MAGIC, None, ALU.add).then_inc(me.stepped(), 1)
                dve.wait_ge(*me.steps())
                v.tensor_scalar(ANG[R_, 1, :], ANG[R_, 1, :], MAGIC, None, ALU.subtract).then_inc(me.stepped(), 1)
                dve.wait_ge(*me.steps())
                v.scalar_tensor_tensor(ANG[R_, dst, :], ANG[R_, 1, :], -C1, ANG[R_, 0, :],
                                                ALU.mult, ALU.add).then_inc(me.stepped(), 1)
                dve.wait_ge(*me.steps())
                v.scalar_tensor_tensor(ANG[R_, dst, :], ANG[R_, 1, :], -C2, ANG[R_, dst, :],
                                                ALU.mult, ALU.add).then_inc(me.stepped(), 1)
                dve.wait_ge(*me.steps())
                v.scalar_tensor_tensor(ANG[R_, dst, :], ANG[R_, 1, :], -C3, ANG[R_, dst, :],
                                                ALU.mult, ALU.add).then_inc(me.stepped(), 1)
                dve.wait_ge(*me.steps())
                v.tensor_scalar(ANG[R_, dst, :], ANG[R_, dst, :], shift, 3.1415925, ALU.add, ALU.min).then_inc(me.stepped(), 1)
                dve.wait_ge(*me.steps())
                v.tensor_scalar(ANG[R_, dst, :], ANG[R_, dst, :], -3.1415925, None, ALU.max)\
                    .then_inc(S["ang_ready"], 1)
            dve.wait_ge(*me.next("sincos_ready", 2))
            v.tensor_scalar(rope[R_, 1, :], rope[R_, 1, :], freq[R_, 1:2], None, ALU.mult).then_inc(me.stepped(), 1)
            dve.wait_ge(*me.next("cond_ready", 2))
            for vec in (0, 1):
                for j in range(4):
                    ada(("ada", vec), j, j, (0,))
                dve.wait_ge(*me.full(("adamod", vec)))
                b = me.bank(("adamod", vec))
                v.tensor_tensor(mod1[:, vec, :], b[:, 0:DC], sect("b_ada", vec), ALU.add).then_inc(
                    me.freed(("adamod", vec)), 1)
                dve.wait_ge(*me.read(("adamod", vec)))
            v.scalar_tensor_tensor(acol[:, 0, :], mod1[:, 1, :], 1.0, sect("g_mix", 0), ALU.add, ALU.mult)\
                .then_inc(S["acol_ready"], 1)
            dve.wait_ge(S["acol_ready"], 1)

            def norm(bankname, n, cnt, width, src, a, dst, sig):
                dve.wait_ge(*me.full(bankname))
                b = me.bank(bankname)
                v.tensor_scalar(inv[:, 0:n], b[:, 0:n], 1.0 / width, EPS, ALU.mult, ALU.add).then_inc(
                    me.freed(bankname), 1)
                dve.wait_ge(*me.read(bankname))
                v.reciprocal(inv[:, 0:n], inv[:, 0:n]).then_inc(S["ms_ready"], 1)
                dve.wait_ge(*me.next("inv_ready"))
                dve.wait_ge(*me.steps())
                for c in range(cnt):
                    v.scalar_tensor_tensor(dst(c), src(c), a(c), inv[:, 0:n], ALU.mult, ALU.mult).then_inc(
                        me.signs(sig), 1)

            h1 = lambda c: HT[:, c, 0:T]
            x1 = lambda c: XC[:, c, 0:T]
            norm("n1", T, DC, D, x1, lambda c: acol[:, 0, c:c + 1], h1, "scaled")
            for t in range(4):
                for j in range(2):
                    dve.wait_ge(*me.full(("qk", t), j))
                    b = me.bank(("qk", t), j)
                    ins = v.tensor_scalar(QKA[:, 2 * t + j, :], b[:, :], HD ** -0.5, None, ALU.mult) if t < 2 \
                        else v.tensor_copy(QKA[:, 2 * t + j, :], b[:, :])
                    ins.then_inc(me.freed(("qk", t), j), 1)
                side("qk", t)
            for t in range(2):
                for k in range(TC):
                    dve.wait_ge(*me.full(("va", t), k))
                    b = me.bank(("va", t), k)
                    v.tensor_copy(VA[:, k, 256 * t:256 * t + 256], b[:, 0:256]).then_inc(me.freed(("va", t), k), 1)
                side("va", t)

            def attn(tag, heads, qi_n, nk, kc_n, pbuf, causal, addtile, scale, dst):
                segs = 2 if nk > 512 else 1

                def rows(h):
                    for qi in range(qi_n):
                        n = P * (qi + 1) if causal else nk
                        row = pbuf[:, TC * (h % 2) + qi, :]
                        for sg in range(segs):
                            k0, k1 = 512 * sg, min(n, 512 * sg + 512)
                            dve.wait_ge(*me.full((tag, "S", h), qi * segs + sg))
                            b = me.bank((tag, "S", h), qi * segs + sg)
                            if addtile is not None:
                                ins = v.tensor_tensor(row[:, k0:k1], b[:, 0:k1 - k0],
                                                      addtile(h)[:, 512 - n:512], ALU.add)
                            else:
                                ins = v.tensor_scalar(row[:, k0:k1], b[:, 0:k1 - k0], scale, None, ALU.mult)
                            ins.then_inc(me.freed((tag, "S", h), qi * segs + sg), 1)
                        for sg in range(segs):
                            dve.wait_ge(*me.read((tag, "S", h), qi * segs + sg))
                        v.reduce_max(stat[:, 0, h % 2, qi:qi + 1], row[:, 0:n], AX, negate=True)\
                            .then_inc(S["smax_ready"], 1)
                    for qi in range(qi_n):
                        n = P * (qi + 1) if causal else nk
                        row = pbuf[:, TC * (h % 2) + qi, 0:n]
                        dve.wait_ge(*me.next("exp_ready"))
                        v.reciprocal(stat[:, 2, h % 2, qi:qi + 1], stat[:, 1, h % 2, qi:qi + 1]).then_inc(me.stepped(), 1)
                        dve.wait_ge(*me.steps())
                        v.tensor_scalar(row, row, stat[:, 2, h % 2, qi:qi + 1], None, ALU.mult)\
                            .then_inc(S["p_ready"], 1)

                rows(0)
                for h in range(heads):
                    if h + 1 < heads:
                        rows(h + 1)
                    dve.wait_ge(*me.full((tag, "O", h)))
                    b = me.bank((tag, "O", h))
                    d, p0, pn = dst(h)
                    v.tensor_copy(d, b[p0:p0 + pn, 0:P * qi_n]).then_inc(me.freed((tag, "O", h)), 1)

            attn("A", HA, TC, T, TC, P1, True, None, 1.0,
                 lambda h: (OA[(h % 2) * 64:(h % 2) * 64 + 64, h // 2, :], (h % 2) * 64, 64))
            for t in range(3):
                for j in range(2):
                    dve.wait_ge(*me.full(("cq", t), j))
                    b = me.bank(("cq", t), j)
                    v.tensor_copy(CQ[:, 2 * t + j, :], b[:, :]).then_inc(me.freed(("cq", t), j), 1)
                side("cq", t)
            for t in range(3):
                for j in range(2):
                    dve.wait_ge(*me.read(("cq", t), j))
            dve.sem_inc(S["proj_ready"], 1)
            for j in range(2):
                dve.wait_ge(*me.full(("ckv", 0), j))
                b = me.bank(("ckv", 0), j)
                v.tensor_copy(CKV[:, j, :], b[:, :]).then_inc(me.freed(("ckv", 0), j), 1)
            side("ckv", 0)
            for j in range(2):
                dve.wait_ge(*me.read(("ckv", 0), j))
            dve.sem_inc(S["proj_ready"], 1)
            dve.wait_ge(*me.full(("kr", 0)))
            b = me.bank(("kr", 0))
            v.tensor_copy(KRT[NOPE:QK, 0, :], b[NOPE:QK, :]).then_inc(me.freed(("kr", 0)), 1)
            side("kr", 0)
            norm("nq", T, 6, QL, lambda c: CQ[:, c, :], lambda c: pcol[:, PCOL["g_q_lora"] + c:PCOL["g_q_lora"] + c + 1],
                 lambda c: CQ[:, c, :], "lat_ready")
            dve.wait_ge(*me.own_signs("lat_ready"))
            norm("nkv", T, 2, KVL, lambda c: CKV[:, c, :],
                 lambda c: pcol[:, PCOL["g_kv_lora"] + c:PCOL["g_kv_lora"] + c + 1], lambda c: CKV[:, c, :], "lat_ready")

            def rotate(rng, src, dst, bankname, i, n, sig):
                dve.wait_ge(*me.full(bankname, i))
                b = me.bank(bankname, i)
                v.tensor_tensor(RTMP[rng, 0, 0:n], src, rope[rng, 0, 0:n], ALU.mult).then_inc(me.stepped(), 1)
                v.tensor_tensor(RTMP[rng, 1, 0:n], b[rng, 0:n], rope[rng, 1, 0:n], ALU.mult).then_inc(
                    me.freed(bankname, i), 1)
                dve.wait_ge(*me.steps())
                dve.wait_ge(*me.read(bankname, i))
                ins = v.tensor_tensor(dst, RTMP[rng, 0, 0:n], RTMP[rng, 1, 0:n], ALU.add)
                if sig is None:
                    ins.then_inc(me.stepped(), 1)
                    dve.wait_ge(*me.steps())
                else:
                    ins.then_inc(me.signs(sig), 1)
                    dve.wait_ge(*me.own_signs(sig))

            dve.wait_ge(*me.read(("kr", 0)))
            rotate(slice(NOPE, QK), KRT[NOPE:QK, 0, :], KRT[NOPE:QK, 1, :], "krr", 0, T, None)
            v.tensor_copy(KM[NOPE:QK, :, :], KRT[NOPE:QK, 1:2, :].to_broadcast([ROPE, HM, T]))\
                .then_inc(S["kb_ready"], 1)
            for t in range(4):
                side("uq", t)
            for h in range(HM):
                rotate(slice(0, QK), QM[0:QK, h, :], QM[0:QK, h, :], "qr", h, T, "q_ready")
            for h in range(HM):
                dve.wait_ge(*me.full("kn", h))
                b = me.bank("kn", h)
                v.tensor_copy(KM[0:NOPE, h, :], b[0:NOPE, :]).then_inc(me.freed("kn", h), 1)
            for k in range(TC):
                dve.wait_ge(*me.full("vm", k))
                b = me.bank("vm", k)
                v.tensor_copy(VM[:, k, :], b[:, :]).then_inc(me.freed("vm", k), 1)
            side("ukv", 0)
            dve.wait_ge(S["mask_loaded"], 16)
            attn("M", HM, TC, T, TC, P1, True, lambda h: MASK[:, 0, :], None,
                 lambda h: (OB[(h % 2) * 64:(h % 2) * 64 + 64, h // 2, :], (h % 2) * 64, 64))
            for t in range(4):
                for j in range(2):
                    for k in range(2):
                        dve.wait_ge(*me.full(("merge", t), 4 * j + 2 * k))
                        b = me.bank(("merge", t), 4 * j + 2 * k)
                        dve.wait_ge(*me.read(("merge", t), 4 * j + 2 * k + 1))
                        v.tensor_tensor(GS[:, 2 + k, :], b[:, :], GS[:, k, :], ALU.mult).then_inc(
                            me.freed(("merge", t), 4 * j + 2 * k), 1)
                    for k in range(2):
                        dve.wait_ge(*me.read(("merge", t), 4 * j + 2 * k))
                    v.tensor_tensor(MERGED[:, 2 * t + j, :], GS[:, 2, :], GS[:, 3, :], ALU.add)\
                        .then_inc(S["merged"], 1)
                    dve.wait_ge(S["merged"], 2 * t + j + 1)

            def add_back(stage, i, c, gate, s):
                o = SET[s]
                xs = XC[:, c, o["at"]:o["at"] + o["tok"]]
                dve.wait_ge(*me.full(stage, i))
                b = me.bank(stage, i)
                v.scalar_tensor_tensor(xs, b[:, 0:o["tok"]], gate[:, c:c + 1], xs, ALU.mult, ALU.add).then_inc(
                    me.freed(stage, i), 1)

            for t in range(4):
                for j in range(2):
                    add_back(("wo", t), j, 2 * t + j, mod1[:, 2, :], "x")
                side("wo", t)
            for t in range(4):
                for j in range(2):
                    dve.wait_ge(*me.read(("wo", t), j))
            dve.wait_ge(*me.steps())
            dve.sem_inc(S["x_new"], 1)
            norm("n2", T, DC, D, x1, lambda c: acol[:, 1, c:c + 1], h1, "scaled")
            for t in range(FC // 2):
                side("ffn", 2 * t)
                side("ffn", 2 * t + 1)
                for j in range(2):
                    dve.wait_ge(*me.read(("ffn", t), j))
                    dve.wait_ge(*me.full(("ffn", t), 2 + j))
                    b = me.bank(("ffn", t), 2 + j)
                    v.tensor_tensor(ACTF[:, 2 * t + j, :], b[:, :], SG[:, j, :], ALU.mult).then_inc(
                        me.freed(("ffn", t), 2 + j), 1)
            mod_take(len(VECTORS) - 1)
            for c in range(DC):
                add_back("down", c, c, mod1[:, 5, :], "x")
            for c in range(DC):
                dve.wait_ge(*me.read("down", c))
            dve.sem_inc(S["x_new"], 1)
            norm("nf", T, DC, D, x1, lambda c: pcol[:, PCOL["g_final"] + c:PCOL["g_final"] + c + 1], x1, "dve_step")
            me.n += DC
            dve.wait_ge(*me.steps())
            dve.sem_inc(S["x_ready"], 1)

            for i in range(LAYERS):
                sets = SETS[i]
                hx = lambda c: HT[:, c, 0:T]
                hc = lambda c: HT[:, c, T:A]
                xc = lambda c: XC[:, c, T:A]
                norm((i, "n1x"), T, DC, D, x1, lambda c: ac2[:, i, 0, 0, c:c + 1], hx, "scaled")
                norm((i, "n1c"), C, DC, D, xc, lambda c: ac2[:, i, 1, 0, c:c + 1], hc, "scaled")
                for t in range(5):
                    both = i == 0 or t == 4
                    for j in range(2):
                        dst = (FB, PB, QKB, QKB, QKB)[t][:, (0, 0, 0, 2, 4)[t] + j, :]
                        dve.wait_ge(*me.full((i, "in", t), (2 if both else 1) * j))
                        b = me.bank((i, "in", t), (2 if both else 1) * j)
                        v.tensor_copy(dst[:, 0:T], b[:, :]).then_inc(me.freed((i, "in", t), (2 if both else 1) * j), 1)
                        if both:
                            dve.wait_ge(*me.full((i, "in", t), 2 * j + 1))
                            b = me.bank((i, "in", t), 2 * j + 1)
                            v.tensor_copy(dst[:, T:A], b[:, 0:C]).then_inc(me.freed((i, "in", t), 2 * j + 1), 1)
                for k in range(AC):
                    dve.wait_ge(*me.full((i, "in", 5), k))
                    b = me.bank((i, "in", 5), k)
                    v.tensor_copy(VB[:, k, :], b[:, 0:256]).then_inc(me.freed((i, "in", 5), k), 1)
                for t in range(6):
                    for k in range(6 if t == 5 else 4 if (i == 0 or t == 4) else 2):
                        dve.wait_ge(*me.read((i, "in", t), k))
                if i == 0:
                    dve.wait_ge(S["axial_loaded"], 80)
                dve.sem_inc(S["proj_ready"], 1)
                for k, (ch, a0, n) in enumerate(qk_units(i)):
                    if k:
                        dve.wait_ge(*me.own_signs("qn_ready"))
                    g = pcol[:, PCOL["q_norm_g_2" if ch < HQ else "k_norm_g_2"] + i:][:, 0:1]
                    view = QKB[:, ch, a0:a0 + n]
                    dve.wait_ge(*me.full((i, "qkn"), k))
                    b = me.bank((i, "qkn"), k)
                    v.tensor_scalar(inv[:, 0:n], b[:, 0:n], 1.0 / HB, EPS, ALU.mult, ALU.add).then_inc(
                        me.freed((i, "qkn"), k), 1)
                    dve.wait_ge(*me.read((i, "qkn"), k))
                    v.reciprocal(inv[:, 0:n], inv[:, 0:n]).then_inc(S["ms_ready"], 1)
                    dve.wait_ge(*me.next("inv_ready"))
                    v.scalar_tensor_tensor(view, view, g, inv[:, 0:n], ALU.mult, ALU.mult).then_inc(
                        me.signs("qn_ready"), 1)
                dve.wait_ge(*me.own_signs("qn_ready"))
                for ch in range(HQ + HKV):
                    rotate(slice(0, P), QKB[:, ch, 0:T], QKB[:, ch, 0:T], (i, "rot"), ch, T, "q_ready")
                for s in sets:
                    o = SET[s]
                    n, a0 = o["tok"], o["at"]
                    for k in range(o["tc"]):
                        dve.wait_ge(*me.full((i, "f1", s), k))
                        b = me.bank((i, "f1", s), k)
                        v.tensor_copy(UB[:, k, :], b[:, :]).then_inc(me.freed((i, "f1", s), k), 1)
                    for f in range(2):
                        dve.wait_ge(*me.full((i, "f2", s), f))
                        b = me.bank((i, "f2", s), f)
                        v.tensor_copy(FR[:, f, a0:a0 + n], b[:, 0:n]).then_inc(me.freed((i, "f2", s), f), 1)
                    for f in range(2):
                        dve.wait_ge(*me.full((i, "f3", s), f))
                        b = me.bank((i, "f3", s), f)
                        v.tensor_copy(HT[:, f, a0:a0 + n], b[:, 0:n]).then_inc(me.freed((i, "f3", s), f), 1)
                    zat = 0 if s == "x" else ZX
                    zl = ZX if s == "x" else ZC
                    for g in range(2):
                        z = Z[:, g, zat:zat + zl]
                        v.memset(z[:, 0:9], 0.0).then_inc(me.stepped(), 1)
                        dve.wait_ge(*me.steps())
                        v.tensor_tensor_scan(z[:, 9:9 + n], ones[:, 0:n], PB[:, g, a0:a0 + n], 0.0,
                                                      ALU.mult, ALU.add).then_inc(me.stepped(), 1)
                        dve.wait_ge(*me.steps())
                        v.tensor_copy(z[:, 9 + n:zl], z[:, 8 + n:9 + n].to_broadcast([P, zl - 9 - n])).then_inc(me.stepped(), 1)
                        dve.wait_ge(*me.steps())
                        d = PD[:, g, a0:a0 + n]
                        for k in range(2):
                            hw = (2, 4, 8, 16)[2 * g + k] // 2
                            r = slice(64 * k, 64 * k + 64)
                            v.tensor_tensor(d[r, :], z[r, 8 + hw:8 + hw + n], z[r, 8 - hw:8 - hw + n],
                                                    ALU.subtract).then_inc(me.stepped(), 1)
                        dve.wait_ge(*me.steps())
                        v.tensor_tensor(d, d, invcount[:, g, a0:a0 + n], ALU.mult).then_inc(me.stepped(), 1)
                        dve.wait_ge(*me.steps())
                        v.tensor_tensor(d, d, PB[:, g, a0:a0 + n], ALU.subtract).then_inc(S["pd_ready"], 1)
                    for g in range(2):
                        dve.wait_ge(*me.full((i, "pw", s), g))
                        b = me.bank((i, "pw", s), g)
                        c0 = PCOL["pool_scale_2"] + 2 * i + g
                        v.tensor_scalar(HT[:, 2 + g, a0:a0 + n], b[:, 0:n], pcol[:, c0:c0 + 1], None,
                                                   ALU.mult)\
                            .then_inc(me.freed((i, "pw", s), g), 1)
                for s in sets:
                    for g in range(2):
                        dve.wait_ge(*me.read((i, "pw", s), g))
                        dve.wait_ge(*me.read((i, "f3", s), g))
                        dve.wait_ge(*me.read((i, "f2", s), g))
                for s in sets:
                    o = SET[s]
                    attn((i, s), HQ, o["tc"], A if s == "x" else C, (A if s == "x" else C) // P, P2, False, None,
                         float(np.float32(HB ** -0.5)),
                         lambda h, a0=o["at"], n=o["tok"]: (HT[:, 4 + h, a0:a0 + n], 0, P))
                for t in range(4):
                    for j in range(2):
                        for k, s in enumerate(sets):
                            add_back((i, "out", t), len(sets) * j + k, 2 * t + j, mod2[:, i, k, 2, :], s)
                for t in range(4):
                    for k in range(2 * len(sets)):
                        dve.wait_ge(*me.read((i, "out", t), k))
                dve.sem_inc(S["x_new"], 1)
                norm((i, "n2x"), T, DC, D, x1, lambda c: ac2[:, i, 0, 1, c:c + 1], hx, "scaled")
                if "c" in sets:
                    norm((i, "n2c"), C, DC, D, xc, lambda c: ac2[:, i, 1, 1, c:c + 1], hc, "scaled")
                na = AC if i == 0 else TC
                dve.wait_ge(*me.full((i, "lg")))
                b = me.bank((i, "lg"))
                v.tensor_copy(LG[:, 0:na, :], b[:, 0:na * NE].rearrange("p (a b) -> p a b", a=na)).then_inc(
                    me.freed((i, "lg")), 1)
                dve.wait_ge(*me.read((i, "lg")))
                v.reduce_max(L1[:, 0, 0:na], LG[:, 0:na, :], AX).then_inc(me.stepped(), 1)
                dve.wait_ge(*me.steps())
                bc = lambda k: L1[:, k, 0:na].unsqueeze(2).to_broadcast([P, na, NE])
                v.tensor_tensor(LG[:, 0:na, :], LG[:, 0:na, :], bc(0), ALU.subtract).then_inc(S["lg_ready"], 1)
                for k in range(2 * na):
                    dve.wait_ge(*me.full((i, "ht"), k))
                    b = me.bank((i, "ht"), k)
                    v.tensor_copy(HTOK[:, k // 2, 512 * (k % 2):512 * (k % 2) + 512], b[:, :]).then_inc(
                        me.freed((i, "ht"), k), 1)
                dve.wait_ge(*me.next("ex_ready"))
                v.reduce_sum(L1[:, 1, 0:na], LG[:, 0:na, :], AX).then_inc(me.stepped(), 1)
                dve.wait_ge(*me.steps())
                v.reciprocal(L1[:, 2, 0:na], L1[:, 1, 0:na]).then_inc(me.stepped(), 1)
                dve.wait_ge(*me.steps())
                v.memset(PA[:, :, :], -1.0).then_inc(me.stepped(), 1)
                v.tensor_tensor(LG[:, 0:na, :], LG[:, 0:na, :], bc(2), ALU.mult).then_inc(me.stepped(), 1)
                dve.wait_ge(*me.steps())
                v.tensor_copy(PA[:, 0:NE, AC:AC + na], LG[:, 0:na, :].rearrange("p a e -> p e a"))\
                    .then_inc(S["aff_ready"], 1)
                for k, s in enumerate(sets):
                    o = SET[s]
                    a0, n = o["at"], o["tok"]
                    dve.wait_ge(*me.full((i, "aT"), k))
                    b = me.bank((i, "aT"), k)
                    v.tensor_copy(AT[:, a0:a0 + n], b[0:NE, 0:n]).then_inc(me.freed((i, "aT"), k), 1)
                    dve.wait_ge(*me.read((i, "aT"), k))
                    for _ in range(o["n"] // 8):
                        v.max(TOP, AT[:, a0:a0 + n]).then_inc(me.stepped(), 1)
                        dve.wait_ge(*me.steps())
                        v.match_replace(AT[:, a0:a0 + n], TOP, AT[:, a0:a0 + n], -1.0).then_inc(me.stepped(), 1)
                        dve.wait_ge(*me.steps())
                    v.tensor_scalar(MK[:, a0:a0 + n], AT[:, a0:a0 + n], 0.0, None, ALU.is_lt).then_inc(me.stepped(), 1)
                    dve.wait_ge(*me.steps())
                    v.tensor_tensor_scan(RK[:, a0:a0 + n], ones[0:NE, 0:n], MK[:, a0:a0 + n], 0.0,
                                                  ALU.mult, ALU.add).then_inc(me.stepped(), 1)
                    dve.wait_ge(*me.steps())
                    v.tensor_tensor(RK[:, a0:a0 + n], RK[:, a0:a0 + n], MK[:, a0:a0 + n], ALU.mult).then_inc(me.stepped(), 1)
                    dve.wait_ge(*me.steps())
                    v.tensor_scalar(RK[:, a0:a0 + n], RK[:, a0:a0 + n], 1.0, None, ALU.subtract)\
                        .then_inc(S["a_ready"], 1)
                dve.wait_ge(*me.full((i, "posT")))
                b = me.bank((i, "posT"))
                v.tensor_copy(PA[:, 0:NE, 0:na],
                                         b[:, 0:na * NE].rearrange("p (a e) -> p e a", a=na))\
                    .then_inc(me.freed((i, "posT")), 1)
                dve.wait_ge(*me.read((i, "posT")))
                dve.wait_ge(S["aff_ready"], i + 1)
                for k in range(2 * na):
                    dve.wait_ge(*me.read((i, "ht"), k))
                for s in sets:
                    v.memset(E["Y" + s], 0.0).then_inc(me.stepped(), 1)
                    v.memset(E["PT" + s], 0.0).then_inc(me.stepped(), 1)
                dve.wait_ge(*me.steps())
                dve.sem_inc(S["tok_ready"], 1)

                def select(e_expr, par):
                    v.tensor_copy(CUR[:, par:par + 1, :], PA[:, e_expr, :]).then_inc(me.stepped(), 1)
                    dve.wait_ge(*me.steps())
                    for k, s in enumerate(sets):
                        o = SET[s]
                        n, tc, q = o["n"], o["tc"], o["parts"]
                        pos = CUR[:, par, o["t0"]:o["t0"] + tc]
                        aff = CUR[:, par, AC + o["t0"]:AC + o["t0"] + tc]
                        pt = E["P" + s].rearrange("p (t c) -> p t c", t=tc)
                        io = iota[:, 0:n].unsqueeze(1).to_broadcast([P, tc, n])
                        v.tensor_tensor(pt, io, pos.unsqueeze(2).to_broadcast([P, tc, n]), ALU.is_equal).then_inc(me.stepped(), 1)
                        dve.wait_ge(*me.steps())
                        pg = E["Pg" + s][:, par * tc * P:(par + 1) * tc * P].rearrange("p (t q c) -> p t q c",
                                                                                      t=tc, q=q)
                        for r in range(q):
                            last = v.tensor_tensor(pg[:, :, r, :], pt, aff.unsqueeze(2).to_broadcast([P, tc, n]),
                                                   ALU.mult)
                            if r == q - 1:
                                last.then_inc(S["sel_ready"], 1)

                def take_gather(e):
                    for s in sets:
                        w = SET[s]["w"]
                        dve.wait_ge(*me.full((i, e, "XG", s)))
                        b = me.bank((i, e, "XG", s))
                        v.tensor_copy(E["XG" + s], b[:, 0:w]).then_inc(me.freed((i, e, "XG", s)), 1)

                def add_experts(e):
                    for k, s in enumerate(sets):
                        for c in range(DC):
                            ch = (c % SET[s]["parts"]) * SBX[s] + c // SET[s]["parts"]
                            add_back((i, e, "S", s), c, ch, mod2[:, i, k, 5, :], s)

                select(slice(0, 1), 0)
                take_gather("first")
                per = (2 * (1 + len(sets)))
                with dve.Fori(0, NE // 2) as it:
                    me.begin(it, {"dve_step": per})
                    for e in range(2):
                        select(bass.ds(it * 2 + (e + 1), 1), (e + 1) % 2)
                        for s in sets:
                            w = SET[s]["w"]
                            dve.wait_ge(*me.read((i, e, "G", s)))
                            dve.wait_ge(*me.full((i, e, "U", s)))
                            b = me.bank((i, e, "U", s))
                            v.tensor_tensor(E["ACT" + s], b[:, 0:w], E["SG" + s], ALU.mult).then_inc(
                                me.freed((i, e, "U", s)), 1)
                        take_gather(e)
                        dve.wait_ge(*me.read((i, 1 - e, "S", sets[-1]), DC - 1, before=(e == 0)))
                        add_experts(e)
                        for s in sets:
                            w = SET[s]["tc"] * P
                            dve.wait_ge(*me.full((i, e, "PT", s)))
                            b = me.bank((i, e, "PT", s))
                            v.tensor_copy(E["PT" + s][:, e * w:(e + 1) * w], b[:, 0:w]).then_inc(
                                me.freed((i, e, "PT", s)), 1)
                    me.end(NE // 2)
                dve.wait_ge(*me.read((i, 1, "S", sets[-1]), DC - 1, after=NE // 2))
                add_experts("last")
                for s in sets:
                    for c in range(DC):
                        dve.wait_ge(*me.read((i, "last", "S", s), c))
                dve.sem_inc(S["x_ready"], 1)
            for t in range(TC):
                for k in range(2):
                    dve.wait_ge(*me.full("yout", 2 * t + k))
                    b = me.bank("yout", 2 * t + k)
                    v.tensor_copy(HTOK[:, t, 512 * k:512 * k + 512], b[:, :]).then_inc(me.freed("yout", 2 * t + k), 1)
                dve.wait_ge(*me.read("yout", 2 * t))
                dve.wait_ge(*me.read("yout", 2 * t + 1))
                dve.sem_inc(S["fin_ready"], 1)

        @block.tensor
        def _(pe):
            me = Counts()

            spent = []

            def mm(o, l, r, start, stop):
                ins = nc.tensor.matmul(o, l, r, start=start, stop=stop)
                if spent and not stop:
                    ins.then_inc(me.used_up(*spent.pop(0)), 1)
                return ins

            def tr(o, src, idt, inner=False):
                ins = nc.tensor.transpose(o, src, idt)
                if spent and inner:
                    ins.then_inc(me.used_up(*spent.pop(0)), 1)
                return ins

            pe.wait_ge(S["rows_loaded"], 16 * (NROWS + 1))
            for k in range(2):
                n = min(P, NPAR - P * k)
                for bank_free, count in me.free("par", k):
                    pe.wait_ge(bank_free, count)
                b = me.bank("par", k)
                nc.tensor.transpose(b[:, 0:n], prow[0:n, k, :], ident[0:n, 0:n]).then_inc(me.fills("par", k), 1)
            pe.wait_ge(S["tok_loaded"], 16 * AC)
            for c in range(DC):
                for bank_free, count in me.free("xin", 2 * c):
                    pe.wait_ge(bank_free, count)
                b = me.bank("xin", 2 * c)
                for t in range(TC):
                    last = nc.tensor.transpose(b[:, t * P:(t + 1) * P], xtok[:, t, c * P:(c + 1) * P], ident[:, :])
                last.then_inc(me.fills("xin", 2 * c), 1)
                for bank_free, count in me.free("xin", 2 * c + 1):
                    pe.wait_ge(bank_free, count)
                b = me.bank("xin", 2 * c + 1)
                for t in range(CC):
                    last = nc.tensor.transpose(b[:, t * P:(t + 1) * P], ctok[:, t, c * P:(c + 1) * P], ident[:, :])
                last.then_inc(me.fills("xin", 2 * c + 1), 1)
            pe.wait_ge(S["consts_loaded"], 16 * NCONST)
            pe.wait_ge(S["pos_loaded"], 32)
            for k, (c0, n) in enumerate(((0, 512), (512, RL - 512))):
                for bank_free, count in me.free("rel", k):
                    pe.wait_ge(bank_free, count)
                b = me.bank("rel", k)
                mm(b[0:HA, 0:n], relT[0:BUCKETS, :], ONEHOT[:, c0:c0 + n], True, True).then_inc(me.fills("rel", k), 1)
            pe.wait_ge(*me.next("ones_ready"))

            def mod_mm(stage, sets):
                for bank_free, count in me.free(stage):
                    pe.wait_ge(bank_free, count)
                b = me.bank(stage)
                for s in range(sets):
                    for c in range(DC):
                        last = mm(b[:, s * DC + c:s * DC + c + 1], acc[:, s, c * P:(c + 1) * P], ones[:, 0:1],
                                  True, True)
                last.then_inc(me.fills(stage), 1)

            def side(stage, t):
                for sd in SIDE_AT.get((stage, t), ()):
                    n, j = SIDE[sd]
                    if j == 0 and n > 0:
                        pe.wait_ge(*me.spent(("side", 4 * n - 1)))
                        mod_mm(("mod", n - 1), VECTORS[n - 1][2])

            def norm(stage, n, cnt, sq):
                for bank_free, count in me.free(stage):
                    pe.wait_ge(bank_free, count)
                b = me.bank(stage)
                for c in range(cnt):
                    pe.wait_ge(*me.next("sq_ready"))
                    last = mm(b[:, 0:n], ones[:, 0:P], sq(c), c == 0, c == cnt - 1)
                last.then_inc(me.fills(stage), 1)

            def tile(stage, k, n, i=0):
                pe.wait_ge(*me.landed(stage, i))
                return me.slot(stage, i)[:, 0:k * n].rearrange("p (k n) -> p k n", k=k)

            def dense(stage, t, c0, m, rhs, k=DC, width=None, o=None):
                for bank_free, count in me.free(*stage):
                    pe.wait_ge(bank_free, count)
                b = me.bank(*stage)
                width = width or T
                for kc in range(k):
                    r = rhs(kc)
                    oo = b[0:m, 0:width] if o is None else o(b)
                    last = mm(oo, t[:, kc, c0:c0 + m], r, kc == 0, kc == k - 1)
                last.then_inc(me.fills(*stage), 1)
                return last

            for vec in (0, 1):
                pe.wait_ge(*me.spent(("ada", vec), 3))
                mod_mm(("adamod", vec), 1)
            h1 = lambda c: HT[:, c, 0:T]
            norm("n1", T, DC, h1)
            pe.wait_ge(*me.next("h_ready", DC))

            for t in range(4):
                w = tile(("qk", t), DC, 256)
                for j in range(2):
                    dense((("qk", t), j), w, P * j, P, h1)
                spent.append((("qk", t),))
                side("qk", t)
            for t in range(2):
                w = tile(("va", t), DC, 256)
                for k in range(TC):
                    for bank_free, count in me.free(("va", t), k):
                        pe.wait_ge(bank_free, count)
                    b = me.bank(("va", t), k)
                    for kc in range(DC):
                        last = mm(b[:, 0:256], HT[:, kc, k * P:(k + 1) * P], w[:, kc, :], kc == 0, kc == DC - 1)
                    last.then_inc(me.fills(("va", t), k), 1)
                spent.append((("va", t),))
                side("va", t)

            def attn(tag, heads, qi_n, nk, kc_n, pbuf, ptbuf, causal, q, k, v_, o, bias=None):
                segs = 2 if nk > 512 else 1

                def scores(h):
                    if bias is not None:
                        pe.wait_ge(S[f"bias_loaded{h % 2}"], 16 * (h // 2 + 1))
                    for qi in range(qi_n):
                        n = P * (qi + 1) if causal else nk
                        for sg in range(segs):
                            k0, k1 = 512 * sg, min(n, 512 * sg + 512)
                            for bank_free, count in me.free((tag, "S", h), qi * segs + sg):
                                pe.wait_ge(bank_free, count)
                            b = me.bank((tag, "S", h), qi * segs + sg)
                            last = mm(b[:, 0:k1 - k0], q(h, qi), k(h, k0, k1), True, bias is None)
                            if bias is not None:
                                last = mm(b[:, 0:n], flip[:, :], bias(h)[:, 512 - n:512], False, True)
                            last.then_inc(me.fills((tag, "S", h), qi * segs + sg), 1)

                scores(0)
                for h in range(heads):
                    if h + 1 < heads:
                        scores(h + 1)
                    pe.wait_ge(*me.next("p_ready", qi_n))
                    for kc in range(kc_n):
                        for bank_free, count in me.free((tag, "T", h), kc):
                            pe.wait_ge(bank_free, count)
                        b = me.bank((tag, "T", h), kc)
                        for qi in range(kc if causal else 0, qi_n):
                            last = nc.tensor.transpose(b[:, P * qi:P * qi + P],
                                                       pbuf[:, TC * (h % 2) + qi, P * kc:P * kc + P], ident[:, :])
                        last.then_inc(me.fills((tag, "T", h), kc), 1)
                    for bank_free, count in me.free((tag, "O", h)):
                        pe.wait_ge(bank_free, count)
                    b = me.bank((tag, "O", h))
                    for kc in range(kc_n):
                        q0 = P * kc if causal else 0
                        pe.wait_ge(*me.read((tag, "T", h), kc))
                        last = mm(o(b, h)[:, q0:P * qi_n], v_(h, kc), ptbuf[:, kc, q0:P * qi_n],
                                  kc == 0, kc == kc_n - 1)
                    last.then_inc(me.fills((tag, "O", h)), 1)

            def hp(h):
                return slice((h % 2) * 64, (h % 2) * 64 + 64)

            for t in range(4):
                for j in range(2):
                    pe.wait_ge(*me.read(("qk", t), j))
            for t in range(2):
                for k in range(TC):
                    pe.wait_ge(*me.read(("va", t), k))
            attn("A", HA, TC, T, TC, P1, PT1, True,
                 lambda h, qi: QKA[hp(h), h // 2, qi * P:(qi + 1) * P],
                 lambda h, k0, k1: QKA[hp(h), 4 + h // 2, k0:k1],
                 lambda h, kc: VA[:, kc, h * 64:h * 64 + 64],
                 lambda b, h: b[hp(h), :], lambda h: MB[:, h % 2, :])
            for t in range(3):
                w = tile(("cq", t), DC, 256)
                for j in range(2):
                    dense((("cq", t), j), w, P * j, P, h1)
                spent.append((("cq", t),))
                side("cq", t)
            w = tile(("ckv", 0), DC, 256)
            for j in range(2):
                dense((("ckv", 0), j), w, P * j, P, h1)
            spent.append((("ckv", 0),))
            side("ckv", 0)
            w = tile(("kr", 0), DC, ROPE)
            dense((("kr", 0), 0), w, 0, ROPE, h1, o=lambda b: b[NOPE:QK, :])
            spent.append((("kr", 0),))
            side("kr", 0)
            norm("nq", T, 6, lambda c: SQ6[:, c, :])
            norm("nkv", T, 2, lambda c: SQ6[:, c, :])
            pe.wait_ge(*me.read(("kr", 0)))
            for bank_free, count in me.free("krr"):
                pe.wait_ge(bank_free, count)
            b = me.bank("krr")
            mm(b[NOPE:QK, :], perm[NOPE:QK, NOPE:QK], KRT[NOPE:QK, 0, :], True, True).then_inc(me.fills("krr"), 1)
            pe.wait_ge(*me.next("lat_ready", 8))
            for t in range(4):
                w = tile(("uq", t), 6, 2 * QK)
                for j in range(2):
                    dense((("uq", t), j), w, QK * j, QK, lambda kc: CQ[:, kc, :], 6)
                spent.append((("uq", t),))
                side("uq", t)
            for h in range(HM):
                for bank_free, count in me.free("qr", h):
                    pe.wait_ge(bank_free, count)
                b = me.bank("qr", h)
                pe.wait_ge(*me.read(("uq", h // 2), h % 2))
                mm(b[0:QK, :], perm[0:QK, 0:QK], QM[0:QK, h, :], True, True).then_inc(me.fills("qr", h), 1)
            w = tile(("ukv", 0), 2, 1024)
            for h in range(HM):
                dense(("kn", h), w, P * h, NOPE, lambda kc: CKV[:, kc, :], 2)
            for k in range(TC):
                for bank_free, count in me.free("vm", k):
                    pe.wait_ge(bank_free, count)
                b = me.bank("vm", k)
                for kc in range(2):
                    last = mm(b[:, :], CKV[:, kc, k * P:(k + 1) * P],
                              w[:, kc, :].rearrange("p (h d) -> p h d", h=HM)[:, :, NOPE:P], kc == 0, kc == 1)
                last.then_inc(me.fills("vm", k), 1)
            spent.append((("ukv", 0),))
            side("ukv", 0)
            for h in range(HM):
                pe.wait_ge(*me.read("kn", h))
            for k in range(TC):
                pe.wait_ge(*me.read("vm", k))
            pe.wait_ge(*me.next("kb_ready"))
            pe.wait_ge(*me.next("q_ready", HM))
            attn("M", HM, TC, T, TC, P1, PT1, True,
                 lambda h, qi: QM[0:QK, h, qi * P:(qi + 1) * P],
                 lambda h, k0, k1: KM[0:QK, h, k0:k1],
                 lambda h, kc: VM[:, kc, h * 64:h * 64 + 64],
                 lambda b, h: b[hp(h), :])
            for h in range(HM):
                pe.wait_ge(*me.read(("A", "O", h)))
                pe.wait_ge(*me.read(("M", "O", h)))
            for half in range(2):
                ua, ub = tile(("upa", half), 4, 512), tile(("upb", half), 4, 512)
                for t in (2 * half, 2 * half + 1):
                    ga, gb = tile(("ga", t), DC, 256), tile(("gb", t), DC, 256)
                    for j in range(2):
                        c = 2 * (t % 2) + j
                        dense((("merge", t), 4 * j), ua, P * c, P, lambda kc: OA[:, kc, :], 4)
                        if c == 3:
                            spent.append((("upa", half),))
                        dense((("merge", t), 4 * j + 1), ga, P * j, P, h1)
                        if j == 1:
                            spent.append((("ga", t),))
                        dense((("merge", t), 4 * j + 2), ub, P * c, P, lambda kc: OB[:, kc, :], 4)
                        if c == 3:
                            spent.append((("upb", half),))
                        dense((("merge", t), 4 * j + 3), gb, P * j, P, h1)
                    spent.append((("gb", t),))
            pe.wait_ge(*me.next("merged", DC))
            for t in range(4):
                w = tile(("wo", t), DC, 256)
                for j in range(2):
                    dense((("wo", t), j), w, P * j, P, lambda kc: MERGED[:, kc, :])
                spent.append((("wo", t),))
                side("wo", t)
            norm("n2", T, DC, h1)
            pe.wait_ge(*me.next("h_ready", DC))
            for t in range(FC // 2):
                side("ffn", 2 * t)
                side("ffn", 2 * t + 1)
                g = tile(("ffn", 2 * t), DC, 256)
                for j in range(2):
                    dense((("ffn", t), j), g, P * j, P, h1)
                spent.append((("ffn", 2 * t),))
                u = tile(("ffn", 2 * t + 1), DC, 256)
                for j in range(2):
                    dense((("ffn", t), 2 + j), u, P * j, P, h1)
                spent.append((("ffn", 2 * t + 1),))
            pe.wait_ge(*me.spent(("side", len(SIDE) - 1)))
            mod_mm(("mod", len(VECTORS) - 1), VECTORS[-1][2])
            for c in range(DC):
                for bank_free, count in me.free("down", c):
                    pe.wait_ge(bank_free, count)
            banks = [me.bank("down", c) for c in range(DC)]
            for t in range(FC // 2):
                w = tile("down", 2, D, t)
                for kk in range(2):
                    pe.wait_ge(*me.read(("ffn", t), 2 + kk))
                    for c in range(DC):
                        last = mm(banks[c][:, :], w[:, kk, c * P:(c + 1) * P], ACTF[:, 2 * t + kk, :],
                                  t + kk == 0, 2 * t + kk == FC - 1)
                        if 2 * t + kk == FC - 1:
                            last.then_inc(me.fills("down", c), 1)
                spent.append(("down", t))
            norm("nf", T, DC, h1)

            for i in range(LAYERS):
                sets = SETS[i]
                hx = lambda c: HT[:, c, 0:T]
                hc = lambda c: HT[:, c, T:A]
                norm((i, "n1x"), T, DC, hx)
                norm((i, "n1c"), C, DC, hc)
                pe.wait_ge(*me.next("h_ready", 2 * DC))
                for t in range(5):
                    w = tile((i, "in", t), DC, 256)
                    both = i == 0 or t == 4
                    for j in range(2):
                        dense(((i, "in", t), (2 if both else 1) * j), w, P * j, P, hx)
                        if both:
                            dense(((i, "in", t), 2 * j + 1), w, P * j, P, hc, width=C)
                    spent.append(((i, "in", t),))
                w = tile((i, "in", 5), DC, 256)
                for k in range(AC):
                    for bank_free, count in me.free((i, "in", 5), k):
                        pe.wait_ge(bank_free, count)
                    b = me.bank((i, "in", 5), k)
                    for kc in range(DC):
                        last = mm(b[:, 0:256], HT[:, kc, k * P:(k + 1) * P], w[:, kc, :], kc == 0, kc == DC - 1)
                    last.then_inc(me.fills((i, "in", 5), k), 1)
                spent.append(((i, "in", 5),))
                for k, (ch, a0, n) in enumerate(qk_units(i)):
                    for bank_free, count in me.free((i, "qkn"), k):
                        pe.wait_ge(bank_free, count)
                    b = me.bank((i, "qkn"), k)
                    pe.wait_ge(*me.next("sq_ready"))
                    mm(b[:, 0:n], ones[:, 0:P], RTMP[:, 0, 0:n], True, True).then_inc(me.fills((i, "qkn"), k), 1)
                pe.wait_ge(*me.next("qn_ready", len(qk_units(i))))
                if i == 0:
                    pe.wait_ge(S["axial_loaded"], 80)
                for ch in range(HQ + HKV):
                    for bank_free, count in me.free((i, "rot"), ch):
                        pe.wait_ge(bank_free, count)
                    b = me.bank((i, "rot"), ch)
                    mm(b[:, :], perm[:, :], QKB[:, ch, 0:T], True, True).then_inc(me.fills((i, "rot"), ch), 1)
                for s in sets:
                    o = SET[s]
                    n, a0, tc = o["tok"], o["at"], o["tc"]
                    for k in range(tc):
                        for bank_free, count in me.free((i, "f1", s), k):
                            pe.wait_ge(bank_free, count)
                        b = me.bank((i, "f1", s), k)
                        for f in range(2):
                            last = mm(b[:, 256 * f:256 * f + 256], FB[:, f, a0 + k * P:a0 + (k + 1) * P],
                                      dft64[:, :], True, True)
                        last.then_inc(me.fills((i, "f1", s), k), 1)
                    for k in range(tc):
                        pe.wait_ge(*me.read((i, "f1", s), k))
                    if s == "x":
                        tabs = [tile((i, "dft", s), tc, n, j) for j in range(2)]
                    else:
                        tt = tile((i, "dft", s), 4, n)
                        tabs = [tt[:, 0:2, :], tt[:, 2:4, :]]
                    for f in range(2):
                        for bank_free, count in me.free((i, "f2", s), f):
                            pe.wait_ge(bank_free, count)
                        b = me.bank((i, "f2", s), f)
                        for m in range(2):
                            for k in range(tc):
                                last = mm(b[:, 0:n], UB[:, k, 256 * f + P * m:256 * f + P * m + P], tabs[m][:, k, :],
                                          m + k == 0, m == 1 and k == tc - 1)
                        last.then_inc(me.fills((i, "f2", s), f), 1)
                    for j in range(2 if s == "x" else 1):
                        spent.append(((i, "dft", s), j,))
                    for f in range(2):
                        pe.wait_ge(*me.read((i, "f2", s), f))
                    for f in range(2):
                        for bank_free, count in me.free((i, "f3", s), f):
                            pe.wait_ge(bank_free, count)
                        b = me.bank((i, "f3", s), f)
                        for k in range(2):
                            last = mm(b[:, 0:n], wf[:, i, k, P * f:P * f + P], FR[:, k, a0:a0 + n], k == 0, k == 1)
                        last.then_inc(me.fills((i, "f3", s), f), 1)
                    for g in range(2):
                        pe.wait_ge(*me.next("pd_ready"))
                        for bank_free, count in me.free((i, "pw", s), g):
                            pe.wait_ge(bank_free, count)
                        b = me.bank((i, "pw", s), g)
                        for k in range(2):
                            r = slice(64 * k, 64 * k + 64)
                            last = mm(b[r, 0:n], wp[r, i, g, :], PD[r, g, a0:a0 + n], True, True)
                        last.then_inc(me.fills((i, "pw", s), g), 1)
                pe.wait_ge(*me.next("q_ready", HQ + HKV))
                for s in sets:
                    o = SET[s]
                    a0 = o["at"]
                    kb = 0 if s == "x" else T
                    attn((i, s), HQ, o["tc"], A if s == "x" else C, (A if s == "x" else C) // P, P2, PT2, False,
                         lambda h, qi, a0=a0: QKB[:, h, a0 + qi * P:a0 + (qi + 1) * P],
                         lambda h, k0, k1, kb=kb: QKB[:, HQ + h // 2, kb + k0:kb + k1],
                         lambda h, kc, kb=kb: VB[:, kb // P + kc, P * (h // 2):P * (h // 2) + P],
                         lambda b, h: b[:, :])
                for s in sets:
                    for h in range(HQ):
                        pe.wait_ge(*me.read(((i, s), "O", h)))
                    for g in range(2):
                        pe.wait_ge(*me.read((i, "pw", s), g))
                        pe.wait_ge(*me.read((i, "f3", s), g))
                for t in range(4):
                    w = tile((i, "out", t), DC, 256)
                    for j in range(2):
                        for k, s in enumerate(sets):
                            dense(((i, "out", t), len(sets) * j + k), w, P * j, P, hx if s == "x" else hc,
                                  width=SET[s]["tok"])
                    spent.append(((i, "out", t),))
                for s in sets:
                    norm((i, "n2" + s), SET[s]["tok"], DC, hx if s == "x" else hc)
                pe.wait_ge(*me.next("h_ready", DC * len(sets)))
                na = AC if i == 0 else TC
                for bank_free, count in me.free((i, "lg")):
                    pe.wait_ge(bank_free, count)
                b = me.bank((i, "lg"))
                for k in range(na):
                    for kc in range(DC):
                        last = mm(b[:, k * NE:(k + 1) * NE], HT[:, kc, k * P:(k + 1) * P], wr[:, i, kc, :],
                                  kc == 0, kc == DC - 1)
                last.then_inc(me.fills((i, "lg")), 1)
                for k in range(na):
                    for q in range(2):
                        for bank_free, count in me.free((i, "ht"), 2 * k + q):
                            pe.wait_ge(bank_free, count)
                        b = me.bank((i, "ht"), 2 * k + q)
                        for c in range(4):
                            last = nc.tensor.transpose(b[:, c * P:(c + 1) * P],
                                                       HT[:, 4 * q + c, k * P:(k + 1) * P], ident[:, :])
                        last.then_inc(me.fills((i, "ht"), 2 * k + q), 1)
                pe.wait_ge(*me.next("aff_ready"))
                for j, s in enumerate(sets):
                    o = SET[s]
                    for bank_free, count in me.free((i, "aT"), j):
                        pe.wait_ge(bank_free, count)
                    b = me.bank((i, "aT"), j)
                    for k in range(o["tc"]):
                        last = nc.tensor.transpose(b[0:NE, k * P:(k + 1) * P], LG[:, o["t0"] + k, :], ident[:, :])
                    last.then_inc(me.fills((i, "aT"), j), 1)
                pe.wait_ge(*me.next("a_ready", len(sets)))
                for bank_free, count in me.free((i, "posT")):
                    pe.wait_ge(bank_free, count)
                b = me.bank((i, "posT"))
                for k in range(na):
                    last = nc.tensor.transpose(b[:, k * NE:(k + 1) * NE], RK[:, k * P:(k + 1) * P],
                                               ident[0:NE, 0:NE])
                last.then_inc(me.fills((i, "posT")), 1)
                pe.wait_ge(*me.next("tok_ready"))

                def token_parts(s, bank, lhs, rhs, first, last_):
                    o = SET[s]
                    n, w = o["n"], o["w"]
                    for q in range(o["parts"]):
                        last = mm(bank[n * q:n * q + n, 0:w], lhs, rhs[:, q * w:(q + 1) * w], first, last_)
                    return last

                def gather(e):
                    for s in sets:
                        pe.wait_ge(*me.next("sel_ready"))
                        o = SET[s]
                        for bank_free, count in me.free((i, e, "XG", s)):
                            pe.wait_ge(bank_free, count)
                        b = me.bank((i, e, "XG", s))
                        pt = E["P" + s].rearrange("p (t c) -> p t c", t=o["tc"])
                        for k in range(o["tc"]):
                            last = token_parts(s, b, pt[:, k, :], HTOK[:, o["t0"] + k, :], k == 0, k == o["tc"] - 1)
                        last.then_inc(me.fills((i, e, "XG", s)), 1)

                def turn(e, what, src):
                    for s in sets:
                        for bank_free, count in me.free((i, e, what, s), after=[((i, e, src, s), 0, False)]):
                            pe.wait_ge(bank_free, count)
                        b = me.bank((i, e, what, s))
                        buf = E["XG" + s] if what == "XT" else E["ACT" + s]
                        for k in range(SBX[s]):
                            last = nc.tensor.transpose(b[:, k * P:(k + 1) * P], buf[:, k * P:(k + 1) * P], ident[:, :])
                        last.then_inc(me.fills((i, e, what, s)), 1)

                def share(s, buf, kc):
                    n = SET[s]["n"]
                    q, k = kc // SBX[s], kc % SBX[s]
                    return buf[:, k * P + q * n:k * P + q * n + n]

                def expert_product(e, m, what, src, after):
                    views = {}
                    for j, s in enumerate(sets):
                        for bank_free, count in me.free((i, e, what, s), after=after(s)):
                            pe.wait_ge(bank_free, count)
                        b = me.bank((i, e, what, s))
                        for kc in range(DC):
                            if j == 0 and kc % 2 == 0:
                                views[kc // 2] = tile((i, e, "w"), 2, D, 4 * m + kc // 2)
                            last = token_parts(s, b, share(s, src(s), kc), views[kc // 2][:, kc % 2, :],
                                               kc == 0, kc == DC - 1)
                            if j == len(sets) - 1 and kc % 2 == 1 and kc < DC - 1:
                                last.then_inc(me.used_up((i, e, "w"), 4 * m + kc // 2), 1)
                        last.then_inc(me.fills((i, e, what, s)), 1)
                    spent.append(((i, e, "w"), 4 * m + 3))

                def scatter(e, par, after):
                    for s in sets:
                        o = SET[s]
                        n, tw = o["n"], o["tc"] * P
                        for c in range(DC):
                            q, k = c % o["parts"], c // o["parts"]
                            r = slice(q * n, q * n + n)
                            for bank_free, count in me.free((i, e, "S", s), c, after(s) if c == 0 else ()):
                                pe.wait_ge(bank_free, count)
                            b = me.bank((i, e, "S", s), c)
                            mm(b[:, 0:tw], E["Y" + s][r, k * P:(k + 1) * P],
                                         E["PT" + s][r, par * tw:(par + 1) * tw], True, True)\
                                .then_inc(me.fills((i, e, "S", s), c), 1)

                gather("first")
                turn("first", "XT", "XG")
                for s in sets:
                    pe.wait_ge(*me.read((i, "first", "XT", s)))
                assert not spent
                with pe.Fori(0, NE // 2) as it:
                    me.begin(it, {"sel_ready": 2 * len(sets)})
                    for e in range(2):
                        xs = lambda s: E["XS" + s][:, e * SET[s]["w"]:(e + 1) * SET[s]["w"]]
                        expert_product(e, 0, "G", xs, lambda s: [((i, 1 - e, "XT", s), 0, e == 0)])
                        expert_product(e, 1, "U", xs, lambda s: ())
                        gather(e)
                        turn(e, "XT", "XG")
                        turn(e, "T", "U")
                        scatter(e, 1 - e, lambda s: [((i, 1 - e, "Y", s), 0, e == 0),
                                                     ((i, 1 - e, "PT", s), 0, e == 0)])
                        expert_product(e, 2, "Y", lambda s: E["AT" + s], lambda s: [((i, e, "T", s), 0, False)])
                        for s in sets:
                            o = SET[s]
                            for bank_free, count in me.free((i, e, "PT", s)):
                                pe.wait_ge(bank_free, count)
                            b = me.bank((i, e, "PT", s))
                            tw = o["tc"] * P
                            for k in range(o["tc"]):
                                last = tr(b[:, k * P:(k + 1) * P],
                                          E["Pg" + s][:, e * tw + k * P:e * tw + (k + 1) * P],
                                          ident[:, :], k == 0)
                            last.then_inc(me.fills((i, e, "PT", s)), 1)
                    assert not spent
                    me.end(NE // 2)
                for s in sets:
                    pe.wait_ge(*me.read((i, 1, "Y", s), after=NE // 2))
                    pe.wait_ge(*me.read((i, 1, "PT", s), after=NE // 2))
                scatter("last", 1, lambda s: ())
            pe.wait_ge(S["x_ready"], 2 + LAYERS)
            for t in range(TC):
                for k in range(2):
                    for bank_free, count in me.free("yout", 2 * t + k):
                        pe.wait_ge(bank_free, count)
                    b = me.bank("yout", 2 * t + k)
                    for c in range(4):
                        last = nc.tensor.transpose(b[:, c * P:(c + 1) * P], XC[:, 4 * k + c, t * P:(t + 1) * P],
                                                   ident[:, :])
                    last.then_inc(me.fills("yout", 2 * t + k), 1)


_DATA = ["x", "c", "positions", "rel_bias", "w_ada", "b_ada", "g_mix", "w_in", "g_q_lora", "w_uq", "g_kv_lora",
         "w_ukv", "w_up_a", "w_up_b", "w_o", "g_ffn", "w_gate", "w_up", "w_down", "g_final", "c_2", "ctx_2",
         "c_ctx_2", "ada_w_2", "ada_b_2", "norm1_g_2", "norm2_g_2", "w_in_2", "w_fourier_2", "w_pool_2",
         "pool_scale_2", "q_norm_g_2", "k_norm_g_2", "w_out_2", "w_router_2", "w_gate_2", "w_up_2", "w_down_2"]


def kernel(**inputs):
    import numpy as _np
    import concourse.bacc as _bacc
    from concourse import mybir as _mybir
    from concourse.bass_utils import run_bass_kernel_spmd as _run

    nc = _bacc.Bacc("TRN2", target_bir_lowering=False, num_devices=1)
    rows = {name for name, _ in ROWS}
    arrays, args = {}, {}
    for name in _DATA:
        a = _np.ascontiguousarray(inputs[name])
        if name in rows:
            a = a.reshape(-1, P)
        arrays[f"in_{name}"] = a
    for name, a in constants().items():
        arrays[f"in_{name}"] = _np.ascontiguousarray(a)
    for name, a in arrays.items():
        args[name[3:]] = nc.dram_tensor(name, a.shape, _mybir.dt.from_np(a.dtype), kind="ExternalInput").ap()
    out = nc.dram_tensor("out_0", (1, T, D), _mybir.dt.float32, kind="ExternalOutput").ap()
    build(nc, args, out)
    r = _run(nc, [arrays], core_ids=[0])
    return r.results[0]["out_0"]
```

```python
from contextlib import ExitStack

import numpy as np

import concourse.bass as bass
from concourse import mybir

NCONST = 11
P = 128
D = 1024
DC = D // P
T, TC = 512, 4
C, CC = 256, 2
A = T + C
AC = TC + CC
EPS = 1e-6
NEG = -1e30
HA, HD = 8, 64
HM, NOPE, ROPE, MV = 8, 64, 32, 64
QK = NOPE + ROPE
QL, KVL = 768, 256
FF = 2816
FC = FF // P
BUCKETS = 32
RL = 640
LAYERS = 2
HQ, HKV, HB = 4, 2, 128
NE = 16
CAPX, CAPC = 2 * T // NE, 2 * C // NE
SLOTS = 6
SLOT = 2048
BANKS = 8

F32 = mybir.dt.float32
I32 = mybir.dt.int32
ALU = mybir.AluOpType
ACT = mybir.ActivationFunctionType
AX = mybir.AxisListType.X

PCOL = {}
ROWS = []
for _name, _n in (("g_mix", 8), ("g_q_lora", 6), ("g_kv_lora", 2), ("g_ffn", 8), ("g_final", 8),
                  ("norm1_g_2", 16), ("norm2_g_2", 16), ("pool_scale_2", 4), ("q_norm_g_2", 2), ("k_norm_g_2", 2),
                  ("b_ada", 48), ("c", 8), ("ada_b_2", 96), ("c_2", 8), ("c_ctx_2", 8)):
    PCOL[_name] = sum(n for _, n in ROWS)
    ROWS.append((_name, _n))
NPAR = sum(n for _, n in ROWS)

VECTORS = [("b1", v, 1) for v in range(2, 6)] + [(0, v, 2) for v in range(6)] \
    + [(1, v, 2 if v < 2 else 1) for v in range(6)]
SIDE = [(n, j) for n in range(len(VECTORS)) for j in range(4)]
SIDE_AT = {}


def _place_sides():
    left = list(range(len(SIDE)))
    for stage, tiles, each in (("qk", 4, 1), ("va", 2, 1), ("cq", 3, 1), ("ckv", 1, 1), ("kr", 1, 1),
                               ("uq", 4, 1), ("ukv", 1, 1), ("wo", 4, 1), ("ffn", 22, 2)):
        for t in range(tiles):
            SIDE_AT[(stage, t)] = [left.pop(0) for _ in range(each) if left]
    assert not left


_place_sides()


class Ring:

    def __init__(self, slots):
        self.slots, self.at, self.pos = slots, {}, 0
        self.used = [0] * slots
        self.body = None

    def add(self, stage, n=1):
        for i in range(n):
            s = self.pos % self.slots
            self.at[(stage, i)] = [s, self.used[s], 0]
            if self.body is not None:
                self.body.append((stage, i))
            self.used[s] += 1
            self.pos += 1

    def next_step(self):
        self.add("rest")
        return self.at[("rest", 0)]

    def loop(self):
        self.body, self.before = [], list(self.used)

    def end(self, trips):
        per = [u - b for u, b in zip(self.used, self.before)]
        for key in self.body:
            self.at[key][2] = per[self.at[key][0]]
        self.used = [b + trips * p for b, p in zip(self.before, per)]
        self.body = None


HT_FIRST = 4
IN_ORDER = (2, 3, 4, 0, 1, 5)
SETS = {0: ("x", "c"), 1: ("x",)}
SET = {"x": dict(n=CAPX, parts=P // CAPX, w=D * CAPX // P, tok=T, tc=TC, t0=0, at=0),
       "c": dict(n=CAPC, parts=P // CAPC, w=D * CAPC // P, tok=C, tc=CC, t0=TC, at=T)}


def plan():
    b, r = Ring(BANKS), Ring(SLOTS)

    def side(stage, t):
        for s in SIDE_AT.get((stage, t), ()):
            n, j = SIDE[s]
            if j == 0 and n > 0:
                b.add(("mod", n - 1))
            r.add(("side", s))

    b.add("par", 2)
    b.add("xin", 2 * DC)
    b.add("n1")
    for v in (0, 1):
        r.add(("ada", v), 4)
        b.add(("adamod", v))
    b.add("rel", 2)
    for t in range(4):
        r.add(("qk", t)); b.add(("qk", t), 2); side("qk", t)
    for t in range(2):
        r.add(("va", t)); b.add(("va", t), TC); side("va", t)

    def attn(tag, heads, qi, segs, kc):
        b.add((tag, "S", 0), qi * segs)
        for h in range(heads):
            if h + 1 < heads:
                b.add((tag, "S", h + 1), qi * segs)
            b.add((tag, "T", h), kc)
            b.add((tag, "O", h))

    attn("A", HA, TC, 1, TC)
    for t in range(3):
        r.add(("cq", t)); b.add(("cq", t), 2); side("cq", t)
    r.add(("ckv", 0)); b.add(("ckv", 0), 2); side("ckv", 0)
    b.add("nq")
    r.add(("kr", 0)); b.add(("kr", 0)); side("kr", 0)
    b.add("nkv")
    b.add("krr")
    for t in range(4):
        r.add(("uq", t)); b.add(("uq", t), 2); side("uq", t)
    b.add("qr", HM)
    r.add(("ukv", 0)); b.add("kn", HM); b.add("vm", TC); side("ukv", 0)
    attn("M", HM, TC, 1, TC)
    for half in range(2):
        r.add(("upa", half)); r.add(("upb", half))
        for t in (2 * half, 2 * half + 1):
            r.add(("ga", t)); r.add(("gb", t))
            b.add(("merge", t), 8)
    for t in range(4):
        r.add(("wo", t)); b.add(("wo", t), 2); side("wo", t)
    b.add("n2")
    for t in range(FC // 2):
        for k in range(2):
            r.add(("ffn", 2 * t + k))
            side("ffn", 2 * t + k)
        b.add(("ffn", t), 4)
    b.add(("mod", len(VECTORS) - 1))
    r.add("down", FC // 2); b.add("down", DC)
    b.add("nf")
    for i in range(LAYERS):
        sets = SETS[i]
        b.add((i, "n1x")); b.add((i, "n1c"))
        for t in IN_ORDER:
            if t == 1:
                b.add((i, "qkn"), len(qk_units(i)))
            r.add((i, "in", t))
            b.add((i, "in", t), in_banks(i, t))
        b.add((i, "rot"), HQ + HKV)
        for s in sets:
            b.add((i, "f1", s), SET[s]["tc"])
            r.add((i, "dft", s), 2 if s == "x" else 1)
            b.add((i, "f2", s), 2)
            b.add((i, "f3", s), 2)
            b.add((i, "pw", s), 2)
        for s in sets:
            nk = A if s == "x" else C
            attn((i, s), HQ, SET[s]["tc"], 2 if s == "x" else 1, nk // P)
        for t in range(4):
            r.add((i, "out", t)); b.add((i, "out", t), 2 * len(sets))
        for s in sets:
            b.add((i, "n2" + s))
        na = AC if i == 0 else TC
        b.add((i, "lgT"), len(sets))
        b.add((i, "lg"))
        b.add((i, "ht"), HT_FIRST)
        b.add((i, "aT"), len(sets))
        for k in range(HT_FIRST, 2 * na):
            b.at[((i, "ht"), k)] = b.next_step()
        b.add((i, "posT"))

        def gather(e):
            for s in sets:
                b.add((i, e, "XG", s))

        def turn(e):
            for s in sets:
                b.add((i, e, "XT", s))

        gather("first"); turn("first")
        b.loop(); r.loop()
        for e in range(2):
            r.add((i, e, "w"), 12)
            for m in ("G", "U"):
                for s in sets:
                    b.add((i, e, m, s))
            gather(e)
            turn(e)
            for s in sets:
                b.add((i, e, "T", s))
            if e == 0:
                for s in sets:
                    b.add((i, "S", s), DC)
            for s in sets:
                b.add((i, e, "Y", s))
            for s in sets:
                b.add((i, e, "PT", s))
        b.end(NE // 2); r.end(NE // 2)
        for s in sets:
            b.add((i, "lastS", s), DC)
    b.add("yout", 2 * TC)
    return b, r


def qk_units(i):
    return [(ch, a0, n) for ch in range(HQ + HKV) for a0, n in ((0, T), (T, C)) if a0 == 0 or i == 0 or ch >= HQ]


def in_banks(i, t):
    return AC if t == 5 else 4 if (i == 0 or t == 4) else 2


def constants():
    k = {}
    k["ident"] = np.eye(P, dtype=np.float32)
    k["flip"] = np.eye(P, dtype=np.float32)[::-1].copy()
    r = np.arange(RL)
    delta = 511 - r
    dist = np.maximum(delta, 0)
    logb = 16 + np.floor(np.maximum(np.log(np.maximum(dist, 1) / 16) / np.log(128) * 16, 0) + 1e-9).astype(int)
    bucket = np.where(dist < 16, dist, np.minimum(logb, BUCKETS - 1))
    k["onehot"] = (bucket[None, :] == np.arange(BUCKETS)[:, None]).astype(np.float32)
    count = (delta >= 0) * ((delta <= 128) * 1 + (delta % 4 == 0) * 1 + (delta % 16 == 0) * 1)
    lnc = np.where(count > 0, np.log(np.maximum(count, 1)), NEG).astype(np.float32)
    k["lncount"] = np.broadcast_to(lnc, (HA, RL)).copy()
    u = np.arange(512)
    k["causal"] = np.where(np.arange(P)[:, None] - u[None, :] + 384 >= 0, 0.0, NEG).astype(np.float32)
    half = ROPE // 2
    f = (10000.0 ** (-np.arange(half) / half)).astype(np.float32)
    k["ropecol"] = np.stack([np.concatenate([f, f]), np.concatenate([-np.ones(half), np.ones(half)])], 1)\
        .astype(np.float32)
    perm = np.zeros((P, P), np.float32)
    for p in range(NOPE, QK):
        j = p - NOPE
        perm[NOPE + (j + half) % ROPE, p] = 1
    k["perm1"] = perm
    perm = np.zeros((P, P), np.float32)
    for p in range(P):
        perm[(p // 64) * 64 + (p + 32) % 64, p] = 1
    k["perm2"] = perm
    inv = (10000.0 ** (-np.arange(0, 64, 2) / 64)).astype(np.float32)
    n = np.arange(T)
    row, col = (n // 64).astype(np.float32), (n % 64).astype(np.float32)
    ar, ac = inv[:, None] * row[None], inv[:, None] * col[None]
    ang = np.concatenate([ar, ar, ac, ac], 0).astype(np.float32).astype(np.float64)
    sign = np.where(np.arange(P) % 64 < 32, -1.0, 1.0)[:, None]
    k["axial"] = np.concatenate([np.cos(ang), np.sin(ang) * sign], 1).astype(np.float32)
    d = np.arange(64)
    a = 2 * np.pi * (np.outer(d, d) % 64) / 64
    blk = np.zeros((P, 2, P), np.float64)
    for g in range(2):
        blk[64 * g:64 * g + 64, 0, 64 * g:64 * g + 64] = np.cos(a)
        blk[64 * g:64 * g + 64, 1, 64 * g:64 * g + 64] = np.sin(a)
    k["dft64"] = blk.reshape(P, 2 * P).astype(np.float32)
    for name, m in (("x", T), ("c", C)):
        t = np.arange(m)
        a = 2 * np.pi * (np.outer(t, t) % m) / m
        s = 1 / np.sqrt(m * 64)
        k["dft" + name] = np.concatenate([np.cos(a) * s, -np.sin(a) * s], 0).astype(np.float32)
    ic = np.zeros((P, 2, A), np.float64)
    for g, win in enumerate((2, 4, 8, 16)):
        for m, at in ((T, 0), (C, T)):
            t = np.arange(m)
            cnt = np.clip(t + win // 2, 0, m) - np.clip(t - win // 2, 0, m)
            ic[64 * (g % 2):64 * (g % 2) + 64, g // 2, at:at + m] = 1.0 / cnt
    k["invcount"] = ic.reshape(P, 2 * A).astype(np.float32)
    k["iota"] = np.broadcast_to(np.arange(CAPX, dtype=np.float32), (P, CAPX)).copy()
    return k


def build(nc, I, out):
    bank_plan, ring_plan = plan()
    with ExitStack() as ctx:
        def sb(name, shape, dt=F32):
            return ctx.enter_context(nc.sbuf_tensor(name, shape, dt))

        def sem(name):
            return ctx.enter_context(nc.semaphore(name))

        ps = [ctx.enter_context(nc.psum_tensor(f"ps{i}", [P, 512], F32)) for i in range(BANKS)]
        ring = sb("ring", [P, SLOTS, SLOT])
        XC = sb("XC", [P, DC, A])
        HT = sb("HT", [P, DC, A])
        WN = 22016
        W = sb("W", [P, WN])
        acc = sb("acc", [P, 2, D])
        inv = sb("inv", [P, 512])
        ident, ones = sb("ident", [P, P]), sb("ones", [P, 512])
        iota = sb("iota", [P, CAPX])
        perm, flip = sb("perm", [P, P]), sb("flip", [P, P])
        rope = sb("rope", [P, 2, T])
        dft64 = sb("dft64", [P, 2 * P])
        wp = sb("wp", [P, LAYERS, 2, 64])
        wr = sb("wr", [P, LAYERS, DC, NE])
        prow = sb("prow", [P, 2, P])
        pcol = sb("pcol", [P, NPAR])
        cond = sb("cond", [P, 24])
        mod1 = sb("mod1", [P, 6, DC])
        mod2 = sb("mod2", [P, LAYERS, 2, 6, DC])
        acol = sb("acol", [P, 2, DC])
        ac2 = sb("ac2", [P, LAYERS, 2, 2, DC])
        stat = sb("stat", [P, 6, 2, TC])
        freq = sb("freq", [P, 2])
        relT = sb("relT", [P, HA])
        rev_dram = nc.dram_tensor("rev_bias", (HA, RL), F32).ap()

        full = [sem(f"bank_full{i}") for i in range(BANKS)]
        free = [sem(f"bank_free{i}") for i in range(BANKS)]
        loaded = [sem(f"tile_loaded{i}") for i in range(SLOTS)]
        used = [sem(f"tile_used{i}") for i in range(SLOTS)]
        names = ("rows_loaded tok_loaded ctx_loaded consts_loaded pos_loaded axial_loaded rev_stored bias_loaded0 "
                 "bias_loaded1 mask_loaded ones_ready pcol_ready cond_ready x_ready rev_ready ang_ready sincos_ready "
                 "sq_ready lat_ready ms_ready inv_ready scaled h_ready acol_ready qn_ready "
                 "q_ready smax_ready p_ready merged pd_ready lg_ready ex_ready aff_ready "
                 "a_ready tok_ready sel_ready fin_ready out_stored dve_step kb_ready").split()
        S = {n: sem(n) for n in names}

        xtok = HT[:, :, :].rearrange("p c t -> p (c t)").rearrange("p (t d) -> p t d", d=D)

        class Counts:

            def __init__(self, own=None):
                self.own, self.n = own, 0
                self.seen, self.it, self.per, self.given = {}, None, {}, {}

            def grown(self, value, per):
                return value if self.it is None else self.it * per + value

            def next(self, name, k=1):
                self.seen[name] = self.seen.get(name, 0) + k
                return S[name], self.grown(self.seen[name], self.per.get(name, 0))

            def stepped(self):
                self.n += 1
                return S[self.own]

            def steps(self):
                return S[self.own], self.grown(self.n, self.per.get(self.own, 0))

            def signs(self, name):
                self.given[name] = self.given.get(name, 0) + 1
                return S[name]

            def own_signs(self, name):
                return S[name], self.given[name]

            def begin(self, it, per):
                self.it, self.per = it, per
                self.base, self.base_n = dict(self.seen), self.n

            def end(self, trips):
                for name, value in self.seen.items():
                    base = self.base.get(name, 0)
                    assert value - base == self.per.get(name, 0), (name, value - base)
                    self.seen[name] = base + trips * (value - base)
                if self.own is not None:
                    assert self.n - self.base_n == self.per.get(self.own, 0), self.n - self.base_n
                    self.n = self.base_n + trips * (self.n - self.base_n)
                self.it = None

            def bank(self, stage, i=0):
                return ps[bank_plan.at[(stage, i)][0]]

            def fills(self, stage, i=0):
                return full[bank_plan.at[(stage, i)][0]]

            def freed(self, stage, i=0):
                return free[bank_plan.at[(stage, i)][0]]

            def full(self, stage, i=0):
                s, u, per = bank_plan.at[(stage, i)]
                return full[s], self.grown(u + 1, per)

            def read(self, stage, i=0, before=False, after=0):
                s, u, per = bank_plan.at[(stage, i)]
                v = u + 1 - (per if before else 0) + (per * (after - 1) if after else 0)
                assert v > 0
                return free[s], self.grown(v, per)

            def free(self, stage, i=0, after=()):
                s, u, per = bank_plan.at[(stage, i)]
                want = {s: (u, per)}
                for stage2, i2, before in after:
                    s2, u2, per2 = bank_plan.at[(stage2, i2)]
                    u2 += 1 - (per2 if before else 0)
                    want[s2] = (max(u2, want.get(s2, (0, 0))[0]), per2)
                return [(free[s2], self.grown(u2, per2)) for s2, (u2, per2) in want.items() if u2 > 0]

            def landed(self, stage, i=0):
                s, u, per = ring_plan.at[(stage, i)]
                return loaded[s], self.grown(u, per) * 16 + 16

            def slot(self, stage, i=0):
                return ring[:, ring_plan.at[(stage, i)][0], :]

            def vacant(self, stage, i=0):
                s, u, per = ring_plan.at[(stage, i)]
                return [(used[s], self.grown(u, per))] if u > 0 else []

            def used_up(self, stage, i=0):
                return used[ring_plan.at[(stage, i)][0]]

            def spent(self, stage, i=0):
                s, u, per = ring_plan.at[(stage, i)]
                return used[s], self.grown(u + 1, per)

        block = ctx.enter_context(nc.Block())

        def wv(at, n, m):
            return W[:, at:at + n * m].rearrange("p (n m) -> p n m", n=n)

        OA, OB = wv(0, 4, T), wv(2048, 4, T)
        QKA, VA = wv(4096, 8, T), wv(8192, TC, 512)
        QM, KM, VM = wv(4096, HM, T), wv(8192, HM, T), wv(12288, TC, 512)
        CQ, CKV = wv(14336, 6, T), wv(17408, 2, T)
        P1 = wv(14336, 8, 512)
        PT1 = wv(18432, 4, 512)
        MB = wv(20480, 2, 512)
        MASK = MB[:, 0:1, :]
        MERGED = wv(4096, DC, T)
        GS = wv(14336, 4, 512)
        ACTF = wv(0, FC, T)
        SG = wv(11264, 4, T)
        ONEHOT, REV = W[0:BUCKETS, 0:RL], W[0:HA, RL:2 * RL]
        LNC = W[0:HA, 2 * RL:3 * RL]
        ctok = W[:, 4096:4096 + 2 * D].rearrange("p (t d) -> p t d", d=D)
        POSI = W[:, 8192:8192 + T].bitcast(I32)
        ANG = wv(8704, 4, T)
        SQ6, KRT = wv(4096, 6, T), wv(18432, 2, T)
        RTMP = wv(19456, 2, T)
        invcount = wv(20480, 2, A)
        wf = W[:, 18432:19456].rearrange("p (l k n) -> p l k n", l=LAYERS, k=2)
        FB, PB = wv(0, 2, A), wv(1536, 2, A)
        QKB = wv(3072, 6, A)
        VB = wv(7680, AC, 256)
        UB = wv(9216, AC, 512)
        FR = wv(12288, 2, A)
        ZX, ZC = 8 + T + 1 + 8, 8 + C + 1 + 8
        Z = wv(13824, 2, ZX + ZC)
        PD = wv(13824 + 2 * (ZX + ZC), 2, A)
        SQB, INVB = wv(9216, 6, A), wv(13824, 6, A)
        SQX = wv(9216, DC, A)
        P2 = wv(9216, 2 * TC, A)
        PT2 = wv(15360, AC, 512)
        HTOK = wv(0, AC, D)
        LG = wv(6144, AC, NE)
        L1 = W[:, 6240:6240 + 3 * AC].rearrange("p (a b) -> p a b", a=3)
        PA = W[:, 6300:6300 + 18 * 2 * AC].rearrange("p (e k) -> p e k", e=18)
        CUR = W[:, 6520:6520 + 2 * 2 * AC].rearrange("p (e k) -> p e k", e=2)
        TOP = W[0:NE, 6560:6568]
        AT = W[0:NE, 6656:6656 + A]
        MK = W[0:NE, 7424:7424 + A]
        RK = W[0:NE, 8192:8192 + A]
        at = 9472
        E = {}
        for s, o in SET.items():
            n, w, tc = o["n"], o["w"], o["tc"]
            for key, size in (("P", tc * n), ("Pg", 2 * tc * P), ("XG", w), ("XS", 2 * w), ("SG", w), ("ACT", w),
                              ("AT", w), ("Y", 2 * w), ("PT", 2 * tc * P)):
                if (key, s) in (("Y", "c"), ("PT", "c")):
                    a = 19456 if key == "Y" else 19968
                    E[key + s] = W[:, a:a + size]
                    continue
                E[key + s] = W[:, at:at + size]
                at += size
        assert at <= 18432, at
        SBX = {s: SET[s]["w"] // P for s in SET}

        def sect(name, v, n=DC):
            return pcol[:, PCOL[name] + v * n:PCOL[name] + (v + 1) * n]

        @block.sync
        def _(sp):
            me = Counts()

            def put(stage, i, src, dst):
                for tile_used, count in me.vacant(stage, i):
                    sp.wait_ge(tile_used, count)
                sp.dma_start(dst(me.slot(stage, i)), src).then_inc(me.landed(stage, i)[0], 16)

            def cols(w, c0, n, k=DC):
                return w[:, c0:c0 + n].rearrange("(k p) n -> p k n", p=P), \
                    (lambda t: t[:, 0:k * n].rearrange("p (k n) -> p k n", k=k))

            def rows(w, k0, c0=0, n=D):
                return w[k0 * P:(k0 + 2) * P, c0:c0 + n].rearrange("(k p) n -> p k n", p=P), \
                    (lambda t: t[:, 0:2 * n].rearrange("p (k n) -> p k n", k=2))

            def side(stage, t):
                for s in SIDE_AT.get((stage, t), ()):
                    n, j = SIDE[s]
                    blk, v, _ = VECTORS[n]
                    w = I["w_ada"][0] if blk == "b1" else I["ada_w_2"][blk]
                    put(("side", s), 0, *rows(w, 2 * j, v * D))

            sp.wait_ge(S["rows_loaded"], 16 * (len(ROWS) + 1))
            sp.wait_ge(S["tok_loaded"], 16 * TC)
            for v in (0, 1):
                for j in range(4):
                    put(("ada", v), j, *rows(I["w_ada"][0], 2 * j, v * D))
            w_in = I["w_in"][0]
            for t in range(4):
                put(("qk", t), 0, *cols(w_in, t * 256, 256)); side("qk", t)
            for t in range(2):
                put(("va", t), 0, *cols(w_in, 1024 + t * 256, 256)); side("va", t)
            for t in range(3):
                put(("cq", t), 0, *cols(w_in, 1536 + t * 256, 256)); side("cq", t)
            put(("ckv", 0), 0, *cols(w_in, 1536 + QL, 256)); side("ckv", 0)
            g0 = 1536 + QL + KVL
            put(("kr", 0), 0, *cols(w_in, g0, ROPE)); side("kr", 0)
            w_uq = I["w_uq"][0].rearrange("l h d -> l (h d)")
            for t in range(4):
                put(("uq", t), 0, *cols(w_uq, t * 2 * QK, 2 * QK, 6)); side("uq", t)
            put(("ukv", 0), 0, *cols(I["w_ukv"][0].rearrange("l h d -> l (h d)"), 0, 1024, 2)); side("ukv", 0)
            for half in range(2):
                put(("upa", half), 0, *cols(I["w_up_a"][0], 512 * half, 512, 4))
                put(("upb", half), 0, *cols(I["w_up_b"][0], 512 * half, 512, 4))
                for t in (2 * half, 2 * half + 1):
                    put(("ga", t), 0, *cols(w_in, g0 + ROPE + 256 * t, 256))
                    put(("gb", t), 0, *cols(w_in, g0 + ROPE + D + 256 * t, 256))
            for t in range(4):
                put(("wo", t), 0, *cols(I["w_o"][0], 256 * t, 256)); side("wo", t)
            for t in range(FC // 2):
                for k, name in enumerate(("w_gate", "w_up")):
                    put(("ffn", 2 * t + k), 0, *cols(I[name][0], 256 * t, 256)); side("ffn", 2 * t + k)
            for t in range(FC // 2):
                put("down", t, *rows(I["w_down"][0], 2 * t))
            for i in range(LAYERS):
                for t in IN_ORDER:
                    put((i, "in", t), 0, *cols(I["w_in_2"][i], 256 * t, 256))
                for s in SETS[i]:
                    k = SET[s]["tok"]
                    if s == "x":
                        for j in range(2):
                            put((i, "dft", s), j, *cols(I["dftx"][j * T:(j + 1) * T, :], 0, T, TC))
                    else:
                        put((i, "dft", s), 0, *cols(I["dftc"], 0, C, 4))
                for t in range(4):
                    put((i, "out", t), 0, *cols(I["w_out_2"][i], 256 * t, 256))
                flat = {m: I[m][i].rearrange("e k n -> (e k) n") for m in ("w_gate_2", "w_up_2", "w_down_2")}
                with sp.Fori(0, NE // 2) as it:
                    me.it = it
                    for e in range(2):
                        for m, name in enumerate(("w_gate_2", "w_up_2", "w_down_2")):
                            for j in range(4):
                                src = flat[name][bass.ds(it * (2 * D) + (e * D + 2 * j * P), 2 * P), :]
                                put((i, e, "w"), 4 * m + j, src.rearrange("(k p) n -> p k n", p=P),
                                    lambda t: t[:, 0:2 * D].rearrange("p (k n) -> p k n", k=2))
                    me.it = None
            for t in range(TC):
                sp.wait_ge(*me.next("fin_ready", 1))
                sp.dma_start(out[0, t * P:(t + 1) * P, :], HTOK[:, t, :]).then_inc(S["out_stored"], 16)
            sp.wait_ge(S["out_stored"], 16 * TC)

        @block.gpsimd
        def _(pool):
            me = Counts()
            k = 0
            pool.wait_ge(S["rows_loaded"], 16 * (len(ROWS) + 1))
            for t in range(TC):
                pool.dma_start(xtok[:, t, :], I["x"][0, t * P:(t + 1) * P, :]).then_inc(S["tok_loaded"], 16)
            for t in range(CC):
                pool.dma_start(ctok[:, t, :], I["ctx_2"][0, t * P:(t + 1) * P, :]).then_inc(S["ctx_loaded"], 16)
            for dst, src in ((perm[:, :], I["perm1"]), (iota[:, :], I["iota"]), (flip[:, :], I["flip"]), (ONEHOT, I["onehot"]),
                             (LNC, I["lncount"]), (freq[NOPE:QK, :], I["ropecol"]), 
                             (dft64[:, :], I["dft64"]),
                             (wp[:, 0], I["w_pool_2"][0].rearrange("(g h) c d -> (h c) g d", h=2)),
                             (wp[:, 1], I["w_pool_2"][1].rearrange("(g h) c d -> (h c) g d", h=2)),
                             (wr[:, 0], I["w_router_2"][0].rearrange("(k p) n -> p k n", p=P)),
                             (wr[:, 1], I["w_router_2"][1].rearrange("(k p) n -> p k n", p=P))):
                pool.dma_start(dst, src).then_inc(S["consts_loaded"], 16)
                k += 1
            assert k == NCONST
            pool.wait_ge(*me.next("rev_ready"))
            pool.dma_start(rev_dram, REV).then_inc(S["rev_stored"], 16)
            pool.wait_ge(S["rev_stored"], 16)
            for h in range(HA):
                if h >= 2:
                    pool.wait_ge(S["smax_ready"], TC * (h - 1))
                src = bass.AP(rev_dram.tensor, h * RL, [[1, P], [1, 512]])
                pool.dma_start(MB[:, h % 2, :], src).then_inc(S[f"bias_loaded{h % 2}"], 16)
            pool.wait_ge(S["smax_ready"], TC * HA)
            pool.dma_start(MASK[:, 0, :], I["causal"]).then_inc(S["mask_loaded"], 16)
            pool.wait_ge(S["merged"], 1)
            pool.dma_start(rope[:, :, :].rearrange("p a b -> p (a b)"), I["axial"]).then_inc(S["axial_loaded"], 16)
            pool.dma_start(perm[:, :], I["perm2"]).then_inc(S["axial_loaded"], 16)
            pool.dma_start(invcount[:, :, :].rearrange("p a b -> p (a b)"), I["invcount"])\
                .then_inc(S["axial_loaded"], 16)
            for i in range(LAYERS):
                pool.dma_start(wf[:, i], I["w_fourier_2"][i].rearrange("(k p) n -> p k n", p=P))\
                    .then_inc(S["axial_loaded"], 16)

        NROWS = len(ROWS)

        @block.scalar
        def _(act):
            me = Counts()
            act.dma_start(ident[:, :], I["ident"]).then_inc(S["rows_loaded"], 16)
            r = 0
            for name, n in ROWS:
                src = I[name]
                dst = prow[r % P:r % P + n, r // P, :]
                act.dma_start(dst, src).then_inc(S["rows_loaded"], 16)
                r += n
            act.dma_start(POSI[NOPE:QK, :], I["positions"].to_broadcast([ROPE, T])).then_inc(S["pos_loaded"], 16)
            act.dma_start(relT[0:BUCKETS, :], I["rel_bias"].rearrange("h b -> b h"),
                          allow_slow_non_contiguous=True).then_inc(S["pos_loaded"], 16)

            def norm(*streams):
                for n, cnt, src, sq, iv, b, dst, stands in streams:
                    for c in range(cnt):
                        act.wait_ge(*stands(c))
                        act.activation(sq(c), src(c), ACT.Square).then_inc(S["sq_ready"], 1)
                for n, cnt, src, sq, iv, b, dst, stands in streams:
                    act.wait_ge(*me.next("ms_ready"))
                    act.activation(iv, iv, ACT.Sqrt).then_inc(S["inv_ready"], 1)
                    if b is not None:
                        for c in range(cnt):
                            act.wait_ge(*me.next("scaled"))
                            act.activation(dst(c), dst(c), ACT.Identity, bias=b(c)).then_inc(S["h_ready"], 1)

            def attn(tag, heads, qi_n, nk, kc_n, pbuf, ptbuf, causal, scale):
                segs = 2 if nk > 512 else 1

                def exps(h):
                    for qi in range(qi_n):
                        act.wait_ge(*me.next("smax_ready"))
                        n = P * (qi + 1) if causal else nk
                        for sg in range(segs):
                            k0, k1 = 512 * sg, min(n, 512 * sg + 512)
                            b = me.bank((tag, "S", h), qi * segs + sg)
                            act.activation(pbuf[:, TC * (h % 2) + qi, k0:k1], b[:, 0:k1 - k0], ACT.Exp,
                                           bias=stat[:, 0, h % 2, qi:qi + 1], scale=scale,
                                           accum_out=stat[:, (1, 4)[sg], h % 2, qi:qi + 1]).then_inc(
                                me.freed((tag, "S", h), qi * segs + sg), 1)

                exps(0)
                for h in range(heads):
                    if h + 1 < heads:
                        exps(h + 1)
                    for kc in range(kc_n):
                        q0 = P * kc if causal else 0
                        act.wait_ge(*me.full((tag, "T", h), kc))
                        b = me.bank((tag, "T", h), kc)
                        act.activation(ptbuf[:, kc, q0:P * qi_n], b[:, q0:P * qi_n], ACT.Copy).then_inc(
                            me.freed((tag, "T", h), kc), 1)

            act.wait_ge(*me.next("pcol_ready"))
            act.activation(cond[:, 0:8], sect("c", 0), ACT.Silu).then_inc(S["cond_ready"], 1)
            act.activation(cond[:, 8:24], pcol[:, PCOL["c_2"]:PCOL["c_2"] + 16], ACT.Silu)\
                .then_inc(S["cond_ready"], 1)
            for c in range(DC):
                act.wait_ge(*me.full("xin", 2 * c))
                b = me.bank("xin", 2 * c)
                act.activation(XC[:, c, 0:T], b[:, :], ACT.Copy).then_inc(me.freed("xin", 2 * c), 1)
                act.wait_ge(*me.full("xin", 2 * c + 1))
                b = me.bank("xin", 2 * c + 1)
                act.activation(XC[:, c, T:A], b[:, 0:C], ACT.Copy).then_inc(me.freed("xin", 2 * c + 1), 1)
            h1 = lambda c: HT[:, c, 0:T]
            x1 = lambda c: XC[:, c, 0:T]
            norm((T, DC, x1, h1, inv[:, :], lambda c: mod1[:, 0, c:c + 1], h1,
                  lambda c: me.read("xin", 2 * DC - 1)))
            act.wait_ge(*me.next("ang_ready"))
            act.activation(rope[NOPE:QK, 1, :], ANG[NOPE:QK, 2, :], ACT.Sin).then_inc(S["sincos_ready"], 1)
            act.wait_ge(*me.next("ang_ready"))
            act.activation(rope[NOPE:QK, 0, :], ANG[NOPE:QK, 3, :], ACT.Sin).then_inc(S["sincos_ready"], 1)
            attn("A", HA, TC, T, TC, P1, PT1, True, 1.0)
            norm((T, 6, lambda c: CQ[:, c, :], lambda c: SQ6[:, c, :], inv[:, :], None, None,
                  lambda c: me.read(("cq", c // 2), c % 2)))
            norm((T, 2, lambda c: CKV[:, c, :], lambda c: SQ6[:, c, :], inv[:, :], None, None,
                  lambda c: me.read(("ckv", 0), c)))
            for t in range(4):
                for j in range(2):
                    act.wait_ge(*me.full(("uq", t), j))
                    b = me.bank(("uq", t), j)
                    act.activation(QM[0:QK, 2 * t + j, :], b[0:QK, :], ACT.Copy,
                                              scale=float(np.float32(QK ** -0.5)))\
                        .then_inc(me.freed(("uq", t), j), 1)
            attn("M", HM, TC, T, TC, P1, PT1, True, 1.0)
            for t in range(4):
                for j in range(2):
                    if t or j:
                        act.wait_ge(*me.next("merged"))
                    for k in range(2):
                        act.wait_ge(*me.full(("merge", t), 4 * j + 2 * k + 1))
                        b = me.bank(("merge", t), 4 * j + 2 * k + 1)
                        act.activation(GS[:, k, :], b[:, :], ACT.Sigmoid).then_inc(
                            me.freed(("merge", t), 4 * j + 2 * k + 1), 1)
            act.wait_ge(*me.next("merged"))
            norm((T, DC, x1, h1, inv[:, :], lambda c: mod1[:, 3, c:c + 1], h1,
                  lambda c: me.read(("wo", c // 2), c % 2)))
            for t in range(FC // 2):
                for j in range(2):
                    if t:
                        act.wait_ge(*me.read(("ffn", t - 1), 2 + j))
                    act.wait_ge(*me.full(("ffn", t), j))
                    b = me.bank(("ffn", t), j)
                    act.activation(SG[:, j, :], b[:, :], ACT.Silu).then_inc(me.freed(("ffn", t), j), 1)
            norm((T, DC, x1, h1, inv[:, :], None, None, lambda c: me.read("down", c)))

            for i in range(LAYERS):
                sets = SETS[i]
                hx = lambda c: HT[:, c, 0:T]
                hc = lambda c: HT[:, c, T:A]
                xc = lambda c: XC[:, c, T:A]
                ivc = RTMP[:, 1, 0:C]
                norm((T, DC, x1, hx, inv[:, :], lambda c: mod2[:, i, 0, 0, c:c + 1], hx,
                      lambda c: me.read((i - 1, "lastS", "x"), c) if i else me.next("x_ready")),
                     (C, DC, xc, hc, ivc, lambda c: mod2[:, i, 1, 0, c:c + 1], hc,
                      lambda c: me.read((i - 1, "lastS", "c"), c) if i else me.read("xin", 2 * c + 1)))
                units = iter(qk_units(i))
                for t in (2, 3, 4):
                    for k in range(in_banks(i, t)):
                        ch, a0, n = next(units)
                        act.wait_ge(*me.read((i, "in", t), k))
                        act.activation(SQB[:, ch, a0:a0 + n], QKB[:, ch, a0:a0 + n], ACT.Square).then_inc(
                            S["sq_ready"], 1)

                def take(t, dst):
                    both = in_banks(i, t) == 4
                    for k in range(in_banks(i, t)):
                        j, c = (k // 2, k % 2) if both else (k, 0)
                        act.wait_ge(*me.full((i, "in", t), k))
                        b = me.bank((i, "in", t), k)
                        act.activation(dst[:, j, T if c else 0:A if c else T], b[:, 0:C if c else T], ACT.Copy)\
                            .then_inc(me.freed((i, "in", t), k), 1)

                take(0, FB)
                for ch, a0, n in qk_units(i):
                    act.wait_ge(*me.next("ms_ready"))
                    iv = INVB[:, ch, a0:a0 + n]
                    act.activation(iv, iv, ACT.Sqrt).then_inc(S["inv_ready"], 1)
                take(1, PB)
                for k in range(AC):
                    act.wait_ge(*me.full((i, "in", 5), k))
                    b = me.bank((i, "in", 5), k)
                    act.activation(VB[:, k, :], b[:, 0:256], ACT.Copy).then_inc(me.freed((i, "in", 5), k), 1)
                for s in sets:
                    n, a0 = SET[s]["tok"], SET[s]["at"]
                    for k in range(SET[s]["tc"]):
                        act.wait_ge(*me.full((i, "f1", s), k))
                        b = me.bank((i, "f1", s), k)
                        act.activation(UB[:, k, :], b[:, :], ACT.Copy).then_inc(me.freed((i, "f1", s), k), 1)
                    for f in range(2):
                        act.wait_ge(*me.full((i, "f2", s), f))
                        b = me.bank((i, "f2", s), f)
                        act.activation(FR[:, f, a0:a0 + n], b[:, 0:n], ACT.Copy).then_inc(me.freed((i, "f2", s), f), 1)
                    for f in range(2):
                        act.wait_ge(*me.full((i, "f3", s), f))
                        b = me.bank((i, "f3", s), f)
                        act.activation(HT[:, f, a0:a0 + n], b[:, 0:n], ACT.Copy).then_inc(me.freed((i, "f3", s), f), 1)
                for s in sets:
                    attn((i, s), HQ, SET[s]["tc"], A if s == "x" else C, (A if s == "x" else C) // P, P2, PT2, False,
                         float(np.float32(HB ** -0.5)))
                out_of = lambda c, k: me.read((i, "out", c // 2), len(sets) * (c % 2) + k)
                streams = [(T, DC, x1, lambda c: SQX[:, c, 0:T], inv[:, :], lambda c: mod2[:, i, 0, 3, c:c + 1], hx,
                            lambda c: out_of(c, 0)),
                           (C, DC, xc, lambda c: SQX[:, c, T:A], ivc, lambda c: mod2[:, i, 1, 3, c:c + 1], hc,
                            lambda c: out_of(c, 1))]
                norm(*streams[:len(sets)])
                for j, s in enumerate(sets):
                    a0, n = SET[s]["at"], SET[s]["tok"]
                    act.wait_ge(*me.full((i, "lgT"), j))
                    b = me.bank((i, "lgT"), j)
                    act.activation(AT[:, a0:a0 + n], b[0:NE, 0:n], ACT.Copy).then_inc(me.freed((i, "lgT"), j), 1)
                act.wait_ge(*me.next("lg_ready"))
                na = AC if i == 0 else TC
                lg = LG[:, 0:na, :].rearrange("p a b -> p (a b)")
                act.activation(lg, lg, ACT.Exp).then_inc(S["ex_ready"], 1)
                for k in range(2 * na):
                    act.wait_ge(*me.full((i, "ht"), k))
                    b = me.bank((i, "ht"), k)
                    act.activation(HTOK[:, k // 2, 512 * (k % 2):512 * (k % 2) + 512], b[:, :], ACT.Copy).then_inc(
                        me.freed((i, "ht"), k), 1)

                def turn(e, par):
                    for s in sets:
                        act.wait_ge(*me.full((i, e, "XT", s)))
                        b = me.bank((i, e, "XT", s))
                        w = SET[s]["w"]
                        act.activation(E["XS" + s][:, par * w:(par + 1) * w], b[:, 0:w], ACT.Copy).then_inc(
                            me.freed((i, e, "XT", s)), 1)

                turn("first", 0)
                with act.Fori(0, NE // 2) as it:
                    me.begin(it, {})
                    for e in range(2):
                        for s in sets:
                            w = SET[s]["w"]
                            act.wait_ge(*me.full((i, e, "G", s)))
                            b = me.bank((i, e, "G", s))
                            act.activation(E["SG" + s], b[:, 0:w], ACT.Silu).then_inc(me.freed((i, e, "G", s)), 1)
                        turn(e, (e + 1) % 2)
                        for s in sets:
                            w = SET[s]["w"]
                            act.wait_ge(*me.full((i, e, "T", s)))
                            b = me.bank((i, e, "T", s))
                            act.activation(E["AT" + s], b[:, 0:w], ACT.Copy).then_inc(me.freed((i, e, "T", s)), 1)
                        for s in sets:
                            w, n = SET[s]["w"], SET[s]["n"]
                            act.wait_ge(*me.full((i, e, "Y", s)))
                            b = me.bank((i, e, "Y", s))
                            for q in range(SET[s]["parts"]):
                                r, ab = slice(q * n, q * n + n), (q + e) % 2
                                last = act.activation(E["Y" + s][r, ab * w:(ab + 1) * w], b[r, 0:w], ACT.Copy)
                            last.then_inc(me.freed((i, e, "Y", s)), 1)
                    me.end(NE // 2)

        @block.vector
        def _(dve):
            v = nc.vector
            me = Counts("dve_step")
            v.memset(ones[:, :], 1.0).then_inc(S["ones_ready"], 1)
            v.memset(rope[0:NOPE, 0, :], 1.0).then_inc(me.stepped(), 1)
            v.memset(rope[0:NOPE, 1, :], 0.0).then_inc(me.stepped(), 1)
            for k in range(2):
                n = min(P, NPAR - P * k)
                dve.wait_ge(*me.full("par", k))
                b = me.bank("par", k)
                v.tensor_copy(pcol[:, P * k:P * k + n], b[:, 0:n]).then_inc(me.freed("par", k), 1)
            dve.wait_ge(*me.read("par", 0))
            dve.wait_ge(*me.read("par", 1))
            dve.sem_inc(S["pcol_ready"], 1)

            def mod_take(n):
                blk, vec, sets = VECTORS[n]
                dve.wait_ge(*me.full(("mod", n)))
                b = me.bank(("mod", n))
                if blk == "b1":
                    last = v.tensor_tensor(mod1[:, vec, :], b[:, 0:DC], sect("b_ada", vec), ALU.add)
                else:
                    for s in range(sets):
                        last = v.tensor_tensor(mod2[:, blk, s, vec, :], b[:, s * DC:(s + 1) * DC],
                                               sect("ada_b_2", 6 * blk + vec), ALU.add)
                last.then_inc(me.freed(("mod", n)), 1)
                if vec in (1, 4):
                    dve.wait_ge(*me.read(("mod", n)))
                    base = PCOL["norm1_g_2" if vec == 1 else "norm2_g_2"]
                    if blk == "b1":
                        v.scalar_tensor_tensor(acol[:, 1, :], mod1[:, 4, :], 1.0, sect("g_ffn", 0),
                                                       ALU.add, ALU.mult).then_inc(me.stepped(), 1)
                    else:
                        for s in range(sets):
                            g = pcol[:, base + blk * DC:base + (blk + 1) * DC]
                            v.scalar_tensor_tensor(ac2[:, blk, s, vec // 4, :], mod2[:, blk, s, vec, :], 1.0,
                                                           g, ALU.add, ALU.mult).then_inc(me.stepped(), 1)

            def ada(stage, j_tile, j, csets):
                dve.wait_ge(*me.landed(stage, j_tile))
                tile = me.slot(stage, j_tile).rearrange("p (k n) -> p k n", k=2)
                for kk in range(2):
                    kc = 2 * j + kk
                    for s, c0 in enumerate(csets):
                        col = cond[:, c0 + kc:c0 + kc + 1]
                        if kc == 0:
                            ins = v.tensor_scalar(acc[:, s, :], tile[:, kk, :], col, None, ALU.mult)
                        else:
                            dve.wait_ge(*me.steps())
                            ins = v.scalar_tensor_tensor(acc[:, s, :], tile[:, kk, :], col, acc[:, s, :],
                                                         ALU.mult, ALU.add)
                        if kk == 1 and s == len(csets) - 1:
                            ins.then_inc(me.used_up(stage, j_tile), 1)
                        else:
                            ins.then_inc(me.stepped(), 1)
                dve.wait_ge(*me.spent(stage, j_tile))

            def side(stage, t):
                for sd in SIDE_AT.get((stage, t), ()):
                    n, j = SIDE[sd]
                    if j == 0 and n > 0:
                        mod_take(n - 1)
                    blk, vec, sets = VECTORS[n]
                    ada(("side", sd), 0, j, (0,) if blk == "b1" else (8, 16)[:sets])

            def mean_square(bankname, n, width, iv):
                dve.wait_ge(*me.full(bankname))
                b = me.bank(bankname)
                v.tensor_scalar(iv, b[:, 0:n], 1.0 / width, EPS, ALU.mult, ALU.add).then_inc(me.freed(bankname), 1)

            def inverse(bankname, iv):
                dve.wait_ge(*me.read(bankname))
                v.reciprocal(iv, iv).then_inc(S["ms_ready"], 1)

            def scale(cnt, src, a, dst, iv, sig):
                dve.wait_ge(*me.next("inv_ready"))
                for c in range(cnt):
                    v.scalar_tensor_tensor(dst(c), src(c), a(c), iv, ALU.mult, ALU.mult).then_inc(me.signs(sig), 1)

            def norm(*streams):
                bankname, n, cnt, width, src, a, dst, iv, sig = streams[0]
                mean_square(bankname, n, width, iv)
                inverse(bankname, iv)
                dve.wait_ge(*me.steps())
                for stream in streams[1:]:
                    mean_square(stream[0], stream[1], stream[3], stream[7])
                scale(cnt, src, a, dst, iv, sig)
                for bankname, n, cnt, width, src, a, dst, iv, sig in streams[1:]:
                    inverse(bankname, iv)
                    scale(cnt, src, a, dst, iv, sig)

            dve.wait_ge(*me.next("cond_ready", 2))
            for vec in (0, 1):
                for j in range(4):
                    ada(("ada", vec), j, j, (0,))
                if vec == 0:
                    mean_square("n1", T, D, inv[:, :])
                    inverse("n1", inv[:, :])
                dve.wait_ge(*me.full(("adamod", vec)))
                b = me.bank(("adamod", vec))
                v.tensor_tensor(mod1[:, vec, :], b[:, 0:DC], sect("b_ada", vec), ALU.add).then_inc(
                    me.freed(("adamod", vec)), 1)
                dve.wait_ge(*me.read(("adamod", vec)))
            v.scalar_tensor_tensor(acol[:, 0, :], mod1[:, 1, :], 1.0, sect("g_mix", 0), ALU.add, ALU.mult)\
                .then_inc(S["acol_ready"], 1)
            dve.wait_ge(S["acol_ready"], 1)

            h1 = lambda c: HT[:, c, 0:T]
            x1 = lambda c: XC[:, c, 0:T]
            scale(DC, x1, lambda c: acol[:, 0, c:c + 1], h1, inv[:, :], "scaled")
            dve.wait_ge(S["consts_loaded"], 16 * NCONST)
            dve.wait_ge(*me.full("rel", 0))
            b = me.bank("rel", 0)
            v.tensor_tensor(REV[:, 0:512], b[0:HA, :], LNC[:, 0:512], ALU.add).then_inc(me.freed("rel", 0), 1)
            dve.wait_ge(*me.full("rel", 1))
            b = me.bank("rel", 1)
            v.tensor_tensor(REV[:, 512:RL], b[0:HA, 0:RL - 512], LNC[:, 512:RL], ALU.add).then_inc(
                me.freed("rel", 1), 1)
            dve.wait_ge(*me.read("rel", 0))
            dve.wait_ge(*me.read("rel", 1))
            dve.sem_inc(S["rev_ready"], 1)
            R_ = slice(NOPE, QK)
            dve.wait_ge(S["pos_loaded"], 32)
            v.tensor_copy(ANG[R_, 1, :], POSI[R_, :]).then_inc(me.stepped(), 1)
            dve.wait_ge(*me.steps())
            v.tensor_scalar(ANG[R_, 0, :], ANG[R_, 1, :], freq[R_, 0:1], None, ALU.mult).then_inc(me.stepped(), 1)
            dve.wait_ge(*me.steps())
            C1, C2 = 6.28125, float(np.float32(2 * np.pi - 6.28125) )
            C2 = float(np.float32(int((2 * np.pi - 6.28125) * 2 ** 20) / 2 ** 20))
            C3 = float(2 * np.pi - C1 - C2)
            MAGIC = float(1.5 * 2 ** 23)
            for dst, turn_, shift in ((2, 0.0, 0.0), (3, 0.25, float(np.pi / 2))):
                v.tensor_scalar(ANG[R_, 1, :], ANG[R_, 0, :], float(1 / (2 * np.pi)), turn_,
                                         ALU.mult, ALU.add).then_inc(me.stepped(), 1)
                dve.wait_ge(*me.steps())
                v.tensor_scalar(ANG[R_, 1, :], ANG[R_, 1, :], MAGIC, None, ALU.add).then_inc(me.stepped(), 1)
                dve.wait_ge(*me.steps())
                v.tensor_scalar(ANG[R_, 1, :], ANG[R_, 1, :], MAGIC, None, ALU.subtract).then_inc(me.stepped(), 1)
                dve.wait_ge(*me.steps())
                v.scalar_tensor_tensor(ANG[R_, dst, :], ANG[R_, 1, :], -C1, ANG[R_, 0, :],
                                                ALU.mult, ALU.add).then_inc(me.stepped(), 1)
                dve.wait_ge(*me.steps())
                v.scalar_tensor_tensor(ANG[R_, dst, :], ANG[R_, 1, :], -C2, ANG[R_, dst, :],
                                                ALU.mult, ALU.add).then_inc(me.stepped(), 1)
                dve.wait_ge(*me.steps())
                v.scalar_tensor_tensor(ANG[R_, dst, :], ANG[R_, 1, :], -C3, ANG[R_, dst, :],
                                                ALU.mult, ALU.add).then_inc(me.stepped(), 1)
                dve.wait_ge(*me.steps())
                v.tensor_scalar(ANG[R_, dst, :], ANG[R_, dst, :], shift, 3.1415925, ALU.add, ALU.min).then_inc(me.stepped(), 1)
                dve.wait_ge(*me.steps())
                v.tensor_scalar(ANG[R_, dst, :], ANG[R_, dst, :], -3.1415925, None, ALU.max)\
                    .then_inc(S["ang_ready"], 1)
            dve.wait_ge(*me.next("sincos_ready", 2))
            v.tensor_scalar(rope[R_, 1, :], rope[R_, 1, :], freq[R_, 1:2], None, ALU.mult).then_inc(me.stepped(), 1)
            for t in range(4):
                for j in range(2):
                    dve.wait_ge(*me.full(("qk", t), j))
                    b = me.bank(("qk", t), j)
                    ins = v.tensor_scalar(QKA[:, 2 * t + j, :], b[:, :], HD ** -0.5, None, ALU.mult) if t < 2 \
                        else v.tensor_copy(QKA[:, 2 * t + j, :], b[:, :])
                    ins.then_inc(me.freed(("qk", t), j), 1)
                side("qk", t)
            for t in range(2):
                for k in range(TC):
                    dve.wait_ge(*me.full(("va", t), k))
                    b = me.bank(("va", t), k)
                    v.tensor_copy(VA[:, k, 256 * t:256 * t + 256], b[:, 0:256]).then_inc(me.freed(("va", t), k), 1)
                side("va", t)

            def attn(tag, heads, qi_n, nk, kc_n, pbuf, causal, scale, dst):
                segs = 2 if nk > 512 else 1

                def maxima(h):
                    for qi in range(qi_n):
                        n = P * (qi + 1) if causal else nk
                        part = lambda k: stat[:, k, h % 2, qi:qi + 1]
                        for sg in range(segs):
                            dve.wait_ge(*me.full((tag, "S", h), qi * segs + sg))
                            b = me.bank((tag, "S", h), qi * segs + sg)
                            w = min(n, 512 * sg + 512) - 512 * sg
                            if scale == 1.0:
                                v.reduce_max(part(0), b[:, 0:w], AX, negate=True).then_inc(S["smax_ready"], 1)
                            else:
                                v.reduce_max(part((3, 5)[sg]), b[:, 0:w], AX).then_inc(me.stepped(), 1)
                        if scale != 1.0:
                            dve.wait_ge(*me.steps())
                            other = part(5) if segs == 2 else part(3)
                            v.tensor_scalar(part(0), part(3), other, -scale, ALU.max, ALU.mult).then_inc(
                                S["smax_ready"], 1)

                def divide(h):
                    for qi in range(qi_n):
                        n = P * (qi + 1) if causal else nk
                        row = pbuf[:, TC * (h % 2) + qi, 0:n]
                        for sg in range(segs):
                            dve.wait_ge(*me.read((tag, "S", h), qi * segs + sg))
                        if segs == 2:
                            v.tensor_tensor(stat[:, 1, h % 2, qi:qi + 1], stat[:, 1, h % 2, qi:qi + 1],
                                            stat[:, 4, h % 2, qi:qi + 1], ALU.add).then_inc(me.stepped(), 1)
                            dve.wait_ge(*me.steps())
                        v.reciprocal(stat[:, 2, h % 2, qi:qi + 1], stat[:, 1, h % 2, qi:qi + 1]).then_inc(
                            me.stepped(), 1)
                        dve.wait_ge(*me.steps())
                        v.tensor_scalar(row, row, stat[:, 2, h % 2, qi:qi + 1], None, ALU.mult)\
                            .then_inc(S["p_ready"], 1)

                def rows(h):
                    maxima(h)
                    divide(h)

                rows(0)
                for h in range(heads):
                    if h + 1 < heads:
                        rows(h + 1)
                    dve.wait_ge(*me.full((tag, "O", h)))
                    b = me.bank((tag, "O", h))
                    d, p0, pn = dst(h)
                    v.tensor_copy(d, b[p0:p0 + pn, 0:P * qi_n]).then_inc(me.freed((tag, "O", h)), 1)

            attn("A", HA, TC, T, TC, P1, True, 1.0,
                 lambda h: (OA[(h % 2) * 64:(h % 2) * 64 + 64, h // 2, :], (h % 2) * 64, 64))
            for t in range(3):
                for j in range(2):
                    dve.wait_ge(*me.full(("cq", t), j))
                    b = me.bank(("cq", t), j)
                    v.tensor_copy(CQ[:, 2 * t + j, :], b[:, :]).then_inc(me.freed(("cq", t), j), 1)
                side("cq", t)
            for j in range(2):
                dve.wait_ge(*me.full(("ckv", 0), j))
                b = me.bank(("ckv", 0), j)
                v.tensor_copy(CKV[:, j, :], b[:, :]).then_inc(me.freed(("ckv", 0), j), 1)
            norm(("nq", T, 6, QL, lambda c: CQ[:, c, :],
                  lambda c: pcol[:, PCOL["g_q_lora"] + c:PCOL["g_q_lora"] + c + 1], lambda c: CQ[:, c, :], inv[:, :],
                  "lat_ready"))
            dve.wait_ge(*me.full(("kr", 0)))
            b = me.bank(("kr", 0))
            v.tensor_copy(KRT[NOPE:QK, 0, :], b[NOPE:QK, :]).then_inc(me.freed(("kr", 0)), 1)
            dve.wait_ge(*me.own_signs("lat_ready"))
            norm(("nkv", T, 2, KVL, lambda c: CKV[:, c, :],
                  lambda c: pcol[:, PCOL["g_kv_lora"] + c:PCOL["g_kv_lora"] + c + 1], lambda c: CKV[:, c, :],
                  inv[:, :], "lat_ready"))

            def rotate(rng, src, dst, bankname, i, n, sig):
                dve.wait_ge(*me.full(bankname, i))
                b = me.bank(bankname, i)
                v.tensor_tensor(RTMP[rng, 0, 0:n], src, rope[rng, 0, 0:n], ALU.mult).then_inc(me.stepped(), 1)
                v.tensor_tensor(RTMP[rng, 1, 0:n], b[rng, 0:n], rope[rng, 1, 0:n], ALU.mult).then_inc(
                    me.freed(bankname, i), 1)
                dve.wait_ge(*me.steps())
                dve.wait_ge(*me.read(bankname, i))
                ins = v.tensor_tensor(dst, RTMP[rng, 0, 0:n], RTMP[rng, 1, 0:n], ALU.add)
                if sig is None:
                    ins.then_inc(me.stepped(), 1)
                    dve.wait_ge(*me.steps())
                else:
                    ins.then_inc(me.signs(sig), 1)
                    dve.wait_ge(*me.own_signs(sig))

            side("ckv", 0)
            side("kr", 0)
            dve.wait_ge(*me.read(("kr", 0)))
            rotate(slice(NOPE, QK), KRT[NOPE:QK, 0, :], KRT[NOPE:QK, 1, :], "krr", 0, T, None)
            v.tensor_copy(KM[NOPE:QK, :, :], KRT[NOPE:QK, 1:2, :].to_broadcast([ROPE, HM, T]))\
                .then_inc(S["kb_ready"], 1)
            for t in range(4):
                side("uq", t)
            for h in range(HM):
                rotate(slice(0, QK), QM[0:QK, h, :], QM[0:QK, h, :], "qr", h, T, "q_ready")
            for h in range(HM):
                dve.wait_ge(*me.full("kn", h))
                b = me.bank("kn", h)
                v.tensor_copy(KM[0:NOPE, h, :], b[0:NOPE, :]).then_inc(me.freed("kn", h), 1)
            for k in range(TC):
                dve.wait_ge(*me.full("vm", k))
                b = me.bank("vm", k)
                v.tensor_copy(VM[:, k, :], b[:, :]).then_inc(me.freed("vm", k), 1)
            side("ukv", 0)
            attn("M", HM, TC, T, TC, P1, True, 1.0,
                 lambda h: (OB[(h % 2) * 64:(h % 2) * 64 + 64, h // 2, :], (h % 2) * 64, 64))
            for t in range(4):
                for j in range(2):
                    for k in range(2):
                        dve.wait_ge(*me.full(("merge", t), 4 * j + 2 * k))
                        b = me.bank(("merge", t), 4 * j + 2 * k)
                        dve.wait_ge(*me.read(("merge", t), 4 * j + 2 * k + 1))
                        v.tensor_tensor(GS[:, 2 + k, :], b[:, :], GS[:, k, :], ALU.mult).then_inc(
                            me.freed(("merge", t), 4 * j + 2 * k), 1)
                    for k in range(2):
                        dve.wait_ge(*me.read(("merge", t), 4 * j + 2 * k))
                    v.tensor_tensor(MERGED[:, 2 * t + j, :], GS[:, 2, :], GS[:, 3, :], ALU.add)\
                        .then_inc(S["merged"], 1)
                    dve.wait_ge(S["merged"], 2 * t + j + 1)

            def add_back(stage, i, c, gate, s):
                o = SET[s]
                xs = XC[:, c, o["at"]:o["at"] + o["tok"]]
                dve.wait_ge(*me.full(stage, i))
                b = me.bank(stage, i)
                v.scalar_tensor_tensor(xs, b[:, 0:o["tok"]], gate[:, c:c + 1], xs, ALU.mult, ALU.add).then_inc(
                    me.freed(stage, i), 1)

            for t in range(4):
                for j in range(2):
                    add_back(("wo", t), j, 2 * t + j, mod1[:, 2, :], "x")
                side("wo", t)
            norm(("n2", T, DC, D, x1, lambda c: acol[:, 1, c:c + 1], h1, inv[:, :], "scaled"))
            for t in range(FC // 2):
                side("ffn", 2 * t)
                side("ffn", 2 * t + 1)
                for j in range(2):
                    dve.wait_ge(*me.read(("ffn", t), j))
                    dve.wait_ge(*me.full(("ffn", t), 2 + j))
                    b = me.bank(("ffn", t), 2 + j)
                    v.tensor_tensor(ACTF[:, 2 * t + j, :], b[:, :], SG[:, j, :], ALU.mult).then_inc(
                        me.freed(("ffn", t), 2 + j), 1)
            mod_take(len(VECTORS) - 1)
            for c in range(DC):
                add_back("down", c, c, mod1[:, 5, :], "x")
            norm(("nf", T, DC, D, x1, lambda c: pcol[:, PCOL["g_final"] + c:PCOL["g_final"] + c + 1], x1, inv[:, :],
                  "x_ready"))

            for i in range(LAYERS):
                sets = SETS[i]
                hx = lambda c: HT[:, c, 0:T]
                hc = lambda c: HT[:, c, T:A]
                xc = lambda c: XC[:, c, T:A]
                ivc = RTMP[:, 1, 0:C]
                norm(((i, "n1x"), T, DC, D, x1, lambda c: ac2[:, i, 0, 0, c:c + 1], hx, inv[:, :], "scaled"),
                     ((i, "n1c"), C, DC, D, xc, lambda c: ac2[:, i, 1, 0, c:c + 1], hc, ivc, "scaled"))
                units = iter(qk_units(i))
                for t in (2, 3, 4):
                    for k in range(in_banks(i, t)):
                        ch, a0, n = next(units)
                        dve.wait_ge(*me.full((i, "in", t), k))
                        b = me.bank((i, "in", t), k)
                        v.tensor_copy(QKB[:, ch, a0:a0 + n], b[:, 0:n]).then_inc(me.freed((i, "in", t), k), 1)
                for k, (ch, a0, n) in enumerate(qk_units(i)):
                    iv = INVB[:, ch, a0:a0 + n]
                    dve.wait_ge(*me.full((i, "qkn"), k))
                    b = me.bank((i, "qkn"), k)
                    v.tensor_scalar(iv, b[:, 0:n], 1.0 / HB, EPS, ALU.mult, ALU.add).then_inc(
                        me.freed((i, "qkn"), k), 1)
                    dve.wait_ge(*me.read((i, "qkn"), k))
                    v.reciprocal(iv, iv).then_inc(S["ms_ready"], 1)
                for k, (ch, a0, n) in enumerate(qk_units(i)):
                    g = pcol[:, PCOL["q_norm_g_2" if ch < HQ else "k_norm_g_2"] + i:][:, 0:1]
                    view = QKB[:, ch, a0:a0 + n]
                    dve.wait_ge(*me.next("inv_ready"))
                    v.scalar_tensor_tensor(view, view, g, INVB[:, ch, a0:a0 + n], ALU.mult, ALU.mult).then_inc(
                        me.signs("qn_ready"), 1)
                dve.wait_ge(*me.own_signs("qn_ready"))
                if i == 0:
                    dve.wait_ge(S["axial_loaded"], 80)
                for ch in range(HQ + HKV):
                    rotate(slice(0, P), QKB[:, ch, 0:T], QKB[:, ch, 0:T], (i, "rot"), ch, T, "q_ready")
                for s in sets:
                    o = SET[s]
                    n, a0 = o["tok"], o["at"]
                    for k in range(in_banks(i, 1)):
                        dve.wait_ge(*me.read((i, "in", 1), k))
                    zat = 0 if s == "x" else ZX
                    zl = ZX if s == "x" else ZC
                    for g in range(2):
                        z = Z[:, g, zat:zat + zl]
                        v.memset(z[:, 0:9], 0.0).then_inc(me.stepped(), 1)
                        dve.wait_ge(*me.steps())
                        v.tensor_tensor_scan(z[:, 9:9 + n], ones[:, 0:n], PB[:, g, a0:a0 + n], 0.0,
                                                      ALU.mult, ALU.add).then_inc(me.stepped(), 1)
                        dve.wait_ge(*me.steps())
                        v.tensor_copy(z[:, 9 + n:zl], z[:, 8 + n:9 + n].to_broadcast([P, zl - 9 - n])).then_inc(me.stepped(), 1)
                        dve.wait_ge(*me.steps())
                        d = PD[:, g, a0:a0 + n]
                        for k in range(2):
                            hw = (2, 4, 8, 16)[2 * g + k] // 2
                            r = slice(64 * k, 64 * k + 64)
                            v.tensor_tensor(d[r, :], z[r, 8 + hw:8 + hw + n], z[r, 8 - hw:8 - hw + n],
                                                    ALU.subtract).then_inc(me.stepped(), 1)
                        dve.wait_ge(*me.steps())
                        v.tensor_tensor(d, d, invcount[:, g, a0:a0 + n], ALU.mult).then_inc(me.stepped(), 1)
                        dve.wait_ge(*me.steps())
                        v.tensor_tensor(d, d, PB[:, g, a0:a0 + n], ALU.subtract).then_inc(S["pd_ready"], 1)
                    for g in range(2):
                        dve.wait_ge(*me.full((i, "pw", s), g))
                        b = me.bank((i, "pw", s), g)
                        c0 = PCOL["pool_scale_2"] + 2 * i + g
                        v.tensor_scalar(HT[:, 2 + g, a0:a0 + n], b[:, 0:n], pcol[:, c0:c0 + 1], None,
                                                   ALU.mult)\
                            .then_inc(me.freed((i, "pw", s), g), 1)
                for s in sets:
                    for g in range(2):
                        dve.wait_ge(*me.read((i, "pw", s), g))
                        dve.wait_ge(*me.read((i, "f3", s), g))
                        dve.wait_ge(*me.read((i, "f2", s), g))
                for s in sets:
                    o = SET[s]
                    attn((i, s), HQ, o["tc"], A if s == "x" else C, (A if s == "x" else C) // P, P2, False,
                         float(np.float32(HB ** -0.5)),
                         lambda h, a0=o["at"], n=o["tok"]: (HT[:, 4 + h, a0:a0 + n], 0, P))
                for t in range(4):
                    for j in range(2):
                        for k, s in enumerate(sets):
                            add_back((i, "out", t), len(sets) * j + k, 2 * t + j, mod2[:, i, k, 2, :], s)
                norm(*[((i, "n2x"), T, DC, D, x1, lambda c: ac2[:, i, 0, 1, c:c + 1], hx, inv[:, :], "scaled"),
                       ((i, "n2c"), C, DC, D, xc, lambda c: ac2[:, i, 1, 1, c:c + 1], hc, ivc, "scaled")][:len(sets)])
                dve.wait_ge(*me.own_signs("scaled"))
                v.memset(PA[:, :, :], -1.0).then_inc(me.stepped(), 1)
                for s in sets:
                    v.memset(E["Y" + s], 0.0).then_inc(me.stepped(), 1)
                    v.memset(E["PT" + s], 0.0).then_inc(me.stepped(), 1)
                na = AC if i == 0 else TC
                dve.wait_ge(*me.full((i, "lg")))
                b = me.bank((i, "lg"))
                v.tensor_copy(LG[:, 0:na, :], b[:, 0:na * NE].rearrange("p (a b) -> p a b", a=na)).then_inc(
                    me.freed((i, "lg")), 1)
                dve.wait_ge(*me.read((i, "lg")))
                v.reduce_max(L1[:, 0, 0:na], LG[:, 0:na, :], AX).then_inc(me.stepped(), 1)
                dve.wait_ge(*me.steps())
                bc = lambda k: L1[:, k, 0:na].unsqueeze(2).to_broadcast([P, na, NE])
                v.tensor_tensor(LG[:, 0:na, :], LG[:, 0:na, :], bc(0), ALU.subtract).then_inc(S["lg_ready"], 1)
                dve.wait_ge(*me.next("ex_ready"))
                v.reduce_sum(L1[:, 1, 0:na], LG[:, 0:na, :], AX).then_inc(me.stepped(), 1)
                dve.wait_ge(*me.steps())
                v.reciprocal(L1[:, 2, 0:na], L1[:, 1, 0:na]).then_inc(me.stepped(), 1)
                dve.wait_ge(*me.steps())
                v.tensor_tensor(LG[:, 0:na, :], LG[:, 0:na, :], bc(2), ALU.mult).then_inc(me.stepped(), 1)
                dve.wait_ge(*me.steps())
                v.tensor_copy(PA[:, 0:NE, AC:AC + na], LG[:, 0:na, :].rearrange("p a e -> p e a"))\
                    .then_inc(S["aff_ready"], 1)
                for k, s in enumerate(sets):
                    o = SET[s]
                    a0, n = o["at"], o["tok"]
                    dve.wait_ge(*me.full((i, "aT"), k))
                    b = me.bank((i, "aT"), k)
                    v.tensor_copy(AT[:, a0:a0 + n], b[0:NE, 0:n]).then_inc(me.freed((i, "aT"), k), 1)
                    dve.wait_ge(*me.read((i, "aT"), k))
                    for _ in range(o["n"] // 8):
                        v.max(TOP, AT[:, a0:a0 + n]).then_inc(me.stepped(), 1)
                        dve.wait_ge(*me.steps())
                        v.match_replace(AT[:, a0:a0 + n], TOP, AT[:, a0:a0 + n], -1.0).then_inc(me.stepped(), 1)
                        dve.wait_ge(*me.steps())
                    v.tensor_scalar(MK[:, a0:a0 + n], AT[:, a0:a0 + n], 0.0, None, ALU.is_lt).then_inc(me.stepped(), 1)
                    dve.wait_ge(*me.steps())
                    v.tensor_tensor_scan(RK[:, a0:a0 + n], ones[0:NE, 0:n], MK[:, a0:a0 + n], 0.0,
                                                  ALU.mult, ALU.add).then_inc(me.stepped(), 1)
                    dve.wait_ge(*me.steps())
                    v.tensor_tensor(RK[:, a0:a0 + n], RK[:, a0:a0 + n], MK[:, a0:a0 + n], ALU.mult).then_inc(me.stepped(), 1)
                    dve.wait_ge(*me.steps())
                    v.tensor_scalar(RK[:, a0:a0 + n], RK[:, a0:a0 + n], 1.0, None, ALU.subtract)\
                        .then_inc(S["a_ready"], 1)
                dve.wait_ge(*me.full((i, "posT")))
                b = me.bank((i, "posT"))
                v.tensor_copy(PA[:, 0:NE, 0:na],
                                         b[:, 0:na * NE].rearrange("p (a e) -> p e a", a=na))\
                    .then_inc(me.freed((i, "posT")), 1)
                dve.wait_ge(*me.read((i, "posT")))
                dve.wait_ge(S["aff_ready"], i + 1)
                for k in range(2 * na):
                    dve.wait_ge(*me.read((i, "ht"), k))
                dve.wait_ge(*me.steps())
                dve.sem_inc(S["tok_ready"], 1)

                def select(e_expr, par):
                    v.tensor_copy(CUR[:, par:par + 1, :], PA[:, e_expr, :]).then_inc(me.stepped(), 1)
                    dve.wait_ge(*me.steps())
                    for k, s in enumerate(sets):
                        o = SET[s]
                        n, tc, q = o["n"], o["tc"], o["parts"]
                        pos = CUR[:, par, o["t0"]:o["t0"] + tc]
                        aff = CUR[:, par, AC + o["t0"]:AC + o["t0"] + tc]
                        pt = E["P" + s].rearrange("p (t c) -> p t c", t=tc)
                        io = iota[:, 0:n].unsqueeze(1).to_broadcast([P, tc, n])
                        v.tensor_tensor(pt, io, pos.unsqueeze(2).to_broadcast([P, tc, n]), ALU.is_equal).then_inc(me.stepped(), 1)
                        dve.wait_ge(*me.steps())
                        pg = E["Pg" + s][:, par * tc * P:(par + 1) * tc * P].rearrange("p (t q c) -> p t q c",
                                                                                      t=tc, q=q)
                        for r in range(q):
                            last = v.tensor_tensor(pg[:, :, r, :], pt, aff.unsqueeze(2).to_broadcast([P, tc, n]),
                                                   ALU.mult)
                            if r == q - 1:
                                last.then_inc(S["sel_ready"], 1)

                def take_gather(e):
                    for s in sets:
                        w = SET[s]["w"]
                        dve.wait_ge(*me.full((i, e, "XG", s)))
                        b = me.bank((i, e, "XG", s))
                        v.tensor_copy(E["XG" + s], b[:, 0:w]).then_inc(me.freed((i, e, "XG", s)), 1)

                def add_experts(stage):
                    for k, s in enumerate(sets):
                        for c in range(DC):
                            add_back((i, stage, s), c, c, mod2[:, i, k, 5, :], s)

                select(slice(0, 1), 0)
                take_gather("first")
                per = (2 * (1 + len(sets)))
                with dve.Fori(0, NE // 2) as it:
                    me.begin(it, {"dve_step": per})
                    for e in range(2):
                        select(bass.ds(it * 2 + (e + 1), 1), (e + 1) % 2)
                        for s in sets:
                            w = SET[s]["w"]
                            dve.wait_ge(*me.read((i, e, "G", s)))
                            dve.wait_ge(*me.full((i, e, "U", s)))
                            b = me.bank((i, e, "U", s))
                            v.tensor_tensor(E["ACT" + s], b[:, 0:w], E["SG" + s], ALU.mult).then_inc(
                                me.freed((i, e, "U", s)), 1)
                        take_gather(e)
                        if e == 0:
                            dve.wait_ge(*me.read((i, "S", sets[-1]), DC - 1, before=True))
                            add_experts("S")
                        for s in sets:
                            w, n = SET[s]["tc"] * P, SET[s]["n"]
                            dve.wait_ge(*me.full((i, e, "PT", s)))
                            b = me.bank((i, e, "PT", s))
                            for q in range(SET[s]["parts"]):
                                r, ab = slice(q * n, q * n + n), (q + e) % 2
                                last = v.tensor_copy(E["PT" + s][r, ab * w:(ab + 1) * w], b[r, 0:w])
                            last.then_inc(me.freed((i, e, "PT", s)), 1)
                    me.end(NE // 2)
                dve.wait_ge(*me.read((i, "S", sets[-1]), DC - 1, after=NE // 2))
                add_experts("lastS")
            for t in range(TC):
                for k in range(2):
                    dve.wait_ge(*me.full("yout", 2 * t + k))
                    b = me.bank("yout", 2 * t + k)
                    v.tensor_copy(HTOK[:, t, 512 * k:512 * k + 512], b[:, :]).then_inc(me.freed("yout", 2 * t + k), 1)
                dve.wait_ge(*me.read("yout", 2 * t))
                dve.wait_ge(*me.read("yout", 2 * t + 1))
                dve.sem_inc(S["fin_ready"], 1)

        @block.tensor
        def _(pe):
            me = Counts()

            spent = []

            def mm(o, l, r, start, stop):
                ins = nc.tensor.matmul(o, l, r, start=start, stop=stop)
                if spent and not stop:
                    ins.then_inc(me.used_up(*spent.pop(0)), 1)
                return ins

            def tr(o, src, idt, inner=False):
                ins = nc.tensor.transpose(o, src, idt)
                if spent and inner:
                    ins.then_inc(me.used_up(*spent.pop(0)), 1)
                return ins

            pe.wait_ge(S["rows_loaded"], 16 * (NROWS + 1))
            for k in range(2):
                n = min(P, NPAR - P * k)
                for bank_free, count in me.free("par", k):
                    pe.wait_ge(bank_free, count)
                b = me.bank("par", k)
                nc.tensor.transpose(b[:, 0:n], prow[0:n, k, :], ident[0:n, 0:n]).then_inc(me.fills("par", k), 1)
            pe.wait_ge(*me.next("ones_ready"))

            def mod_mm(stage, sets):
                for bank_free, count in me.free(stage):
                    pe.wait_ge(bank_free, count)
                b = me.bank(stage)
                for s in range(sets):
                    for c in range(DC):
                        last = mm(b[:, s * DC + c:s * DC + c + 1], acc[:, s, c * P:(c + 1) * P], ones[:, 0:1],
                                  True, True)
                last.then_inc(me.fills(stage), 1)

            def side(stage, t):
                for sd in SIDE_AT.get((stage, t), ()):
                    n, j = SIDE[sd]
                    if j == 0 and n > 0:
                        pe.wait_ge(*me.spent(("side", 4 * n - 1)))
                        mod_mm(("mod", n - 1), VECTORS[n - 1][2])

            def norm(stage, n, cnt, sq):
                for bank_free, count in me.free(stage):
                    pe.wait_ge(bank_free, count)
                b = me.bank(stage)
                for c in range(cnt):
                    pe.wait_ge(*me.next("sq_ready"))
                    last = mm(b[:, 0:n], ones[:, 0:P], sq(c), c == 0, c == cnt - 1)
                last.then_inc(me.fills(stage), 1)

            def tile(stage, k, n, i=0):
                pe.wait_ge(*me.landed(stage, i))
                return me.slot(stage, i)[:, 0:k * n].rearrange("p (k n) -> p k n", k=k)

            def dense(stage, t, c0, m, rhs, k=DC, width=None, o=None, fresh=None):
                for bank_free, count in me.free(*stage):
                    pe.wait_ge(bank_free, count)
                b = me.bank(*stage)
                width = width or T
                for kc in range(k):
                    if fresh is not None:
                        pe.wait_ge(*me.next(fresh))
                    r = rhs(kc)
                    oo = b[0:m, 0:width] if o is None else o(b)
                    last = mm(oo, t[:, kc, c0:c0 + m], r, kc == 0, kc == k - 1)
                last.then_inc(me.fills(*stage), 1)
                return last

            pe.wait_ge(S["tok_loaded"], 16 * TC)
            pe.wait_ge(S["ctx_loaded"], 16 * CC)
            for c in range(DC):
                for bank_free, count in me.free("xin", 2 * c):
                    pe.wait_ge(bank_free, count)
                b = me.bank("xin", 2 * c)
                for t in range(TC):
                    last = nc.tensor.transpose(b[:, t * P:(t + 1) * P], xtok[:, t, c * P:(c + 1) * P], ident[:, :])
                last.then_inc(me.fills("xin", 2 * c), 1)
                for bank_free, count in me.free("xin", 2 * c + 1):
                    pe.wait_ge(bank_free, count)
                b = me.bank("xin", 2 * c + 1)
                for t in range(CC):
                    last = nc.tensor.transpose(b[:, t * P:(t + 1) * P], ctok[:, t, c * P:(c + 1) * P], ident[:, :])
                last.then_inc(me.fills("xin", 2 * c + 1), 1)
            h1 = lambda c: HT[:, c, 0:T]
            norm("n1", T, DC, h1)
            pe.wait_ge(*me.spent(("ada", 0), 3))
            mod_mm(("adamod", 0), 1)
            pe.wait_ge(*me.spent(("ada", 1), 3))
            mod_mm(("adamod", 1), 1)
            pe.wait_ge(S["consts_loaded"], 16 * NCONST)
            pe.wait_ge(S["pos_loaded"], 32)
            for k, (c0, n) in enumerate(((0, 512), (512, RL - 512))):
                for bank_free, count in me.free("rel", k):
                    pe.wait_ge(bank_free, count)
                b = me.bank("rel", k)
                mm(b[0:HA, 0:n], relT[0:BUCKETS, :], ONEHOT[:, c0:c0 + n], True, True).then_inc(me.fills("rel", k), 1)

            for t in range(4):
                w = tile(("qk", t), DC, 256)
                for j in range(2):
                    dense((("qk", t), j), w, P * j, P, h1, fresh="h_ready" if t + j == 0 else None)
                spent.append((("qk", t),))
                side("qk", t)
            for t in range(2):
                w = tile(("va", t), DC, 256)
                for k in range(TC):
                    for bank_free, count in me.free(("va", t), k):
                        pe.wait_ge(bank_free, count)
                    b = me.bank(("va", t), k)
                    for kc in range(DC):
                        last = mm(b[:, 0:256], HT[:, kc, k * P:(k + 1) * P], w[:, kc, :], kc == 0, kc == DC - 1)
                    last.then_inc(me.fills(("va", t), k), 1)
                spent.append((("va", t),))
                side("va", t)

            def attn(tag, heads, qi_n, nk, kc_n, pbuf, ptbuf, causal, q, k, v_, o, bias=None, mask=None):
                segs = 2 if nk > 512 else 1

                def scores(h):
                    if bias is not None:
                        pe.wait_ge(S[f"bias_loaded{h % 2}"], 16 * (h // 2 + 1))
                    for qi in range(qi_n):
                        n = P * (qi + 1) if causal else nk
                        for sg in range(segs):
                            k0, k1 = 512 * sg, min(n, 512 * sg + 512)
                            for bank_free, count in me.free((tag, "S", h), qi * segs + sg):
                                pe.wait_ge(bank_free, count)
                            b = me.bank((tag, "S", h), qi * segs + sg)
                            last = mm(b[:, 0:k1 - k0], q(h, qi), k(h, k0, k1), True, bias is None and mask is None)
                            if mask is not None:
                                last = mm(b[:, n - P:n], ident[:, :], mask, False, True)
                            if bias is not None:
                                last = mm(b[:, 0:n], flip[:, :], bias(h)[:, 512 - n:512], False, True)
                            last.then_inc(me.fills((tag, "S", h), qi * segs + sg), 1)

                scores(0)
                for h in range(heads):
                    if h + 1 < heads:
                        scores(h + 1)
                    pe.wait_ge(*me.next("p_ready", qi_n))
                    for kc in range(kc_n):
                        for bank_free, count in me.free((tag, "T", h), kc):
                            pe.wait_ge(bank_free, count)
                        b = me.bank((tag, "T", h), kc)
                        for qi in range(kc if causal else 0, qi_n):
                            last = nc.tensor.transpose(b[:, P * qi:P * qi + P],
                                                       pbuf[:, TC * (h % 2) + qi, P * kc:P * kc + P], ident[:, :])
                        last.then_inc(me.fills((tag, "T", h), kc), 1)
                    for bank_free, count in me.free((tag, "O", h)):
                        pe.wait_ge(bank_free, count)
                    b = me.bank((tag, "O", h))
                    for kc in range(kc_n):
                        q0 = P * kc if causal else 0
                        pe.wait_ge(*me.read((tag, "T", h), kc))
                        last = mm(o(b, h)[:, q0:P * qi_n], v_(h, kc), ptbuf[:, kc, q0:P * qi_n],
                                  kc == 0, kc == kc_n - 1)
                    last.then_inc(me.fills((tag, "O", h)), 1)

            def hp(h):
                return slice((h % 2) * 64, (h % 2) * 64 + 64)

            for t in range(4):
                for j in range(2):
                    pe.wait_ge(*me.read(("qk", t), j))
            for t in range(2):
                for k in range(TC):
                    pe.wait_ge(*me.read(("va", t), k))
            attn("A", HA, TC, T, TC, P1, PT1, True,
                 lambda h, qi: QKA[hp(h), h // 2, qi * P:(qi + 1) * P],
                 lambda h, k0, k1: QKA[hp(h), 4 + h // 2, k0:k1],
                 lambda h, kc: VA[:, kc, h * 64:h * 64 + 64],
                 lambda b, h: b[hp(h), :], lambda h: MB[:, h % 2, :])
            for t in range(3):
                w = tile(("cq", t), DC, 256)
                for j in range(2):
                    dense((("cq", t), j), w, P * j, P, h1)
                spent.append((("cq", t),))
                side("cq", t)
            w = tile(("ckv", 0), DC, 256)
            for j in range(2):
                dense((("ckv", 0), j), w, P * j, P, h1)
            spent.append((("ckv", 0),))
            side("ckv", 0)
            norm("nq", T, 6, lambda c: SQ6[:, c, :])
            w = tile(("kr", 0), DC, ROPE)
            dense((("kr", 0), 0), w, 0, ROPE, h1, o=lambda b: b[NOPE:QK, :])
            spent.append((("kr", 0),))
            side("kr", 0)
            norm("nkv", T, 2, lambda c: SQ6[:, c, :])
            pe.wait_ge(*me.read(("kr", 0)))
            for bank_free, count in me.free("krr"):
                pe.wait_ge(bank_free, count)
            b = me.bank("krr")
            mm(b[NOPE:QK, :], perm[NOPE:QK, NOPE:QK], KRT[NOPE:QK, 0, :], True, True).then_inc(me.fills("krr"), 1)
            for t in range(4):
                w = tile(("uq", t), 6, 2 * QK)
                for j in range(2):
                    dense((("uq", t), j), w, QK * j, QK, lambda kc: CQ[:, kc, :], 6,
                          fresh="lat_ready" if t + j == 0 else None)
                spent.append((("uq", t),))
                side("uq", t)
            for h in range(HM):
                for bank_free, count in me.free("qr", h):
                    pe.wait_ge(bank_free, count)
                b = me.bank("qr", h)
                pe.wait_ge(*me.read(("uq", h // 2), h % 2))
                mm(b[0:QK, :], perm[0:QK, 0:QK], QM[0:QK, h, :], True, True).then_inc(me.fills("qr", h), 1)
            w = tile(("ukv", 0), 2, 1024)
            pe.wait_ge(*me.next("lat_ready", 2))
            for h in range(HM):
                dense(("kn", h), w, P * h, NOPE, lambda kc: CKV[:, kc, :], 2)
            for k in range(TC):
                for bank_free, count in me.free("vm", k):
                    pe.wait_ge(bank_free, count)
                b = me.bank("vm", k)
                for kc in range(2):
                    last = mm(b[:, :], CKV[:, kc, k * P:(k + 1) * P],
                              w[:, kc, :].rearrange("p (h d) -> p h d", h=HM)[:, :, NOPE:P], kc == 0, kc == 1)
                last.then_inc(me.fills("vm", k), 1)
            spent.append((("ukv", 0),))
            side("ukv", 0)
            for h in range(HM):
                pe.wait_ge(*me.read("kn", h))
            for k in range(TC):
                pe.wait_ge(*me.read("vm", k))
            pe.wait_ge(*me.next("kb_ready"))
            pe.wait_ge(*me.next("q_ready", HM))
            pe.wait_ge(S["mask_loaded"], 16)
            attn("M", HM, TC, T, TC, P1, PT1, True,
                 lambda h, qi: QM[0:QK, h, qi * P:(qi + 1) * P],
                 lambda h, k0, k1: KM[0:QK, h, k0:k1],
                 lambda h, kc: VM[:, kc, h * 64:h * 64 + 64],
                 lambda b, h: b[hp(h), :], mask=MASK[:, 0, 384:512])
            for h in range(HM):
                pe.wait_ge(*me.read(("A", "O", h)))
                pe.wait_ge(*me.read(("M", "O", h)))
            for half in range(2):
                ua, ub = tile(("upa", half), 4, 512), tile(("upb", half), 4, 512)
                for t in (2 * half, 2 * half + 1):
                    ga, gb = tile(("ga", t), DC, 256), tile(("gb", t), DC, 256)
                    for j in range(2):
                        c = 2 * (t % 2) + j
                        dense((("merge", t), 4 * j), ua, P * c, P, lambda kc: OA[:, kc, :], 4)
                        if c == 3:
                            spent.append((("upa", half),))
                        dense((("merge", t), 4 * j + 1), ga, P * j, P, h1)
                        if j == 1:
                            spent.append((("ga", t),))
                        dense((("merge", t), 4 * j + 2), ub, P * c, P, lambda kc: OB[:, kc, :], 4)
                        if c == 3:
                            spent.append((("upb", half),))
                        dense((("merge", t), 4 * j + 3), gb, P * j, P, h1)
                    spent.append((("gb", t),))
            pe.wait_ge(*me.next("merged", DC))
            for t in range(4):
                w = tile(("wo", t), DC, 256)
                for j in range(2):
                    dense((("wo", t), j), w, P * j, P, lambda kc: MERGED[:, kc, :])
                spent.append((("wo", t),))
                side("wo", t)
            norm("n2", T, DC, h1)
            for t in range(FC // 2):
                side("ffn", 2 * t)
                side("ffn", 2 * t + 1)
                g = tile(("ffn", 2 * t), DC, 256)
                for j in range(2):
                    dense((("ffn", t), j), g, P * j, P, h1, fresh="h_ready" if t + j == 0 else None)
                spent.append((("ffn", 2 * t),))
                u = tile(("ffn", 2 * t + 1), DC, 256)
                for j in range(2):
                    dense((("ffn", t), 2 + j), u, P * j, P, h1)
                spent.append((("ffn", 2 * t + 1),))
            pe.wait_ge(*me.spent(("side", len(SIDE) - 1)))
            mod_mm(("mod", len(VECTORS) - 1), VECTORS[-1][2])
            for c in range(DC):
                for bank_free, count in me.free("down", c):
                    pe.wait_ge(bank_free, count)
            banks = [me.bank("down", c) for c in range(DC)]
            for t in range(FC // 2):
                w = tile("down", 2, D, t)
                for kk in range(2):
                    pe.wait_ge(*me.read(("ffn", t), 2 + kk))
                    for c in range(DC):
                        last = mm(banks[c][:, :], w[:, kk, c * P:(c + 1) * P], ACTF[:, 2 * t + kk, :],
                                  t + kk == 0, 2 * t + kk == FC - 1)
                        if 2 * t + kk == FC - 1:
                            last.then_inc(me.fills("down", c), 1)
                spent.append(("down", t))
            norm("nf", T, DC, h1)

            for i in range(LAYERS):
                sets = SETS[i]
                hx = lambda c: HT[:, c, 0:T]
                hc = lambda c: HT[:, c, T:A]
                norm((i, "n1x"), T, DC, hx)
                norm((i, "n1c"), C, DC, hc)
                for t in IN_ORDER[:-1]:
                    if t == 1:
                        for k, (ch, a0, n) in enumerate(qk_units(i)):
                            for bank_free, count in me.free((i, "qkn"), k):
                                pe.wait_ge(bank_free, count)
                            b = me.bank((i, "qkn"), k)
                            pe.wait_ge(*me.next("sq_ready"))
                            mm(b[:, 0:n], ones[:, 0:P], SQB[:, ch, a0:a0 + n], True, True).then_inc(
                                me.fills((i, "qkn"), k), 1)
                    w = tile((i, "in", t), DC, 256)
                    both = in_banks(i, t) == 4
                    for j in range(2):
                        dense(((i, "in", t), (2 if both else 1) * j), w, P * j, P, hx,
                              fresh="h_ready" if t == IN_ORDER[0] and j == 0 else None)
                        if both:
                            first_c = t == (IN_ORDER[0] if i == 0 else 4) and j == 0
                            dense(((i, "in", t), 2 * j + 1), w, P * j, P, hc, width=C,
                                  fresh="h_ready" if first_c else None)
                    spent.append(((i, "in", t),))
                w = tile((i, "in", 5), DC, 256)
                for k in range(AC):
                    for bank_free, count in me.free((i, "in", 5), k):
                        pe.wait_ge(bank_free, count)
                    b = me.bank((i, "in", 5), k)
                    for kc in range(DC):
                        last = mm(b[:, 0:256], HT[:, kc, k * P:(k + 1) * P], w[:, kc, :], kc == 0, kc == DC - 1)
                    last.then_inc(me.fills((i, "in", 5), k), 1)
                spent.append(((i, "in", 5),))
                pe.wait_ge(*me.next("qn_ready", len(qk_units(i))))
                if i == 0:
                    pe.wait_ge(S["axial_loaded"], 80)
                for ch in range(HQ + HKV):
                    for bank_free, count in me.free((i, "rot"), ch):
                        pe.wait_ge(bank_free, count)
                    b = me.bank((i, "rot"), ch)
                    mm(b[:, :], perm[:, :], QKB[:, ch, 0:T], True, True).then_inc(me.fills((i, "rot"), ch), 1)
                for k in range(in_banks(i, 0)):
                    pe.wait_ge(*me.read((i, "in", 0), k))
                for s in sets:
                    o = SET[s]
                    n, a0, tc = o["tok"], o["at"], o["tc"]
                    for k in range(tc):
                        for bank_free, count in me.free((i, "f1", s), k):
                            pe.wait_ge(bank_free, count)
                        b = me.bank((i, "f1", s), k)
                        for f in range(2):
                            last = mm(b[:, 256 * f:256 * f + 256], FB[:, f, a0 + k * P:a0 + (k + 1) * P],
                                      dft64[:, :], True, True)
                        last.then_inc(me.fills((i, "f1", s), k), 1)
                    for k in range(tc):
                        pe.wait_ge(*me.read((i, "f1", s), k))
                    if s == "x":
                        tabs = [tile((i, "dft", s), tc, n, j) for j in range(2)]
                    else:
                        tt = tile((i, "dft", s), 4, n)
                        tabs = [tt[:, 0:2, :], tt[:, 2:4, :]]
                    for f in range(2):
                        for bank_free, count in me.free((i, "f2", s), f):
                            pe.wait_ge(bank_free, count)
                        b = me.bank((i, "f2", s), f)
                        for m in range(2):
                            for k in range(tc):
                                last = mm(b[:, 0:n], UB[:, k, 256 * f + P * m:256 * f + P * m + P], tabs[m][:, k, :],
                                          m + k == 0, m == 1 and k == tc - 1)
                        last.then_inc(me.fills((i, "f2", s), f), 1)
                    for j in range(2 if s == "x" else 1):
                        spent.append(((i, "dft", s), j,))
                    for f in range(2):
                        pe.wait_ge(*me.read((i, "f2", s), f))
                    for f in range(2):
                        for bank_free, count in me.free((i, "f3", s), f):
                            pe.wait_ge(bank_free, count)
                        b = me.bank((i, "f3", s), f)
                        for k in range(2):
                            last = mm(b[:, 0:n], wf[:, i, k, P * f:P * f + P], FR[:, k, a0:a0 + n], k == 0, k == 1)
                        last.then_inc(me.fills((i, "f3", s), f), 1)
                    for g in range(2):
                        pe.wait_ge(*me.next("pd_ready"))
                        for bank_free, count in me.free((i, "pw", s), g):
                            pe.wait_ge(bank_free, count)
                        b = me.bank((i, "pw", s), g)
                        for k in range(2):
                            r = slice(64 * k, 64 * k + 64)
                            last = mm(b[r, 0:n], wp[r, i, g, :], PD[r, g, a0:a0 + n], True, True)
                        last.then_inc(me.fills((i, "pw", s), g), 1)
                pe.wait_ge(*me.next("q_ready", HQ + HKV))
                for k in range(AC):
                    pe.wait_ge(*me.read((i, "in", 5), k))
                for s in sets:
                    o = SET[s]
                    a0 = o["at"]
                    kb = 0 if s == "x" else T
                    attn((i, s), HQ, o["tc"], A if s == "x" else C, (A if s == "x" else C) // P, P2, PT2, False,
                         lambda h, qi, a0=a0: QKB[:, h, a0 + qi * P:a0 + (qi + 1) * P],
                         lambda h, k0, k1, kb=kb: QKB[:, HQ + h // 2, kb + k0:kb + k1],
                         lambda h, kc, kb=kb: VB[:, kb // P + kc, P * (h // 2):P * (h // 2) + P],
                         lambda b, h: b[:, :])
                for s in sets:
                    for h in range(HQ):
                        pe.wait_ge(*me.read(((i, s), "O", h)))
                    for g in range(2):
                        pe.wait_ge(*me.read((i, "pw", s), g))
                        pe.wait_ge(*me.read((i, "f3", s), g))
                for t in range(4):
                    w = tile((i, "out", t), DC, 256)
                    for j in range(2):
                        for k, s in enumerate(sets):
                            dense(((i, "out", t), len(sets) * j + k), w, P * j, P, hx if s == "x" else hc,
                                  width=SET[s]["tok"])
                    spent.append(((i, "out", t),))
                for s in sets:
                    a0, n = SET[s]["at"], SET[s]["tok"]
                    norm((i, "n2" + s), n, DC, lambda c: SQX[:, c, a0:a0 + n])
                na = AC if i == 0 else TC
                for j, s in enumerate(sets):
                    a0, n = SET[s]["at"], SET[s]["tok"]
                    for bank_free, count in me.free((i, "lgT"), j):
                        pe.wait_ge(bank_free, count)
                    b = me.bank((i, "lgT"), j)
                    for kc in range(DC):
                        pe.wait_ge(*me.next("h_ready"))
                        last = mm(b[0:NE, 0:n], wr[:, i, kc, :], HT[:, kc, a0:a0 + n], kc == 0, kc == DC - 1)
                    last.then_inc(me.fills((i, "lgT"), j), 1)
                for bank_free, count in me.free((i, "lg")):
                    pe.wait_ge(bank_free, count)
                b = me.bank((i, "lg"))
                for j, s in enumerate(sets):
                    pe.wait_ge(*me.read((i, "lgT"), j))
                for k in range(na):
                    last = nc.tensor.transpose(b[:, k * NE:(k + 1) * NE], AT[:, k * P:(k + 1) * P],
                                               ident[0:NE, 0:NE])
                last.then_inc(me.fills((i, "lg")), 1)

                def by_tokens(k):
                    for bank_free, count in me.free((i, "ht"), k):
                        pe.wait_ge(bank_free, count)
                    b = me.bank((i, "ht"), k)
                    for c in range(4):
                        last = nc.tensor.transpose(b[:, c * P:(c + 1) * P],
                                                   HT[:, 4 * (k % 2) + c, k // 2 * P:(k // 2 + 1) * P], ident[:, :])
                    last.then_inc(me.fills((i, "ht"), k), 1)

                for k in range(HT_FIRST):
                    by_tokens(k)
                pe.wait_ge(*me.next("aff_ready"))
                for j, s in enumerate(sets):
                    o = SET[s]
                    for bank_free, count in me.free((i, "aT"), j):
                        pe.wait_ge(bank_free, count)
                    b = me.bank((i, "aT"), j)
                    for k in range(o["tc"]):
                        last = nc.tensor.transpose(b[0:NE, k * P:(k + 1) * P], LG[:, o["t0"] + k, :], ident[:, :])
                    last.then_inc(me.fills((i, "aT"), j), 1)
                for k in range(HT_FIRST, 2 * na):
                    by_tokens(k)
                pe.wait_ge(*me.next("a_ready", len(sets)))
                for bank_free, count in me.free((i, "posT")):
                    pe.wait_ge(bank_free, count)
                b = me.bank((i, "posT"))
                for k in range(na):
                    last = nc.tensor.transpose(b[:, k * NE:(k + 1) * NE], RK[:, k * P:(k + 1) * P],
                                               ident[0:NE, 0:NE])
                last.then_inc(me.fills((i, "posT")), 1)
                pe.wait_ge(*me.next("tok_ready"))

                def token_parts(s, bank, lhs, rhs, first, last_, swap=0):
                    o = SET[s]
                    n, w = o["n"], o["w"]
                    for q in range(o["parts"]):
                        last = mm(bank[n * q:n * q + n, 0:w], lhs, rhs[:, (q ^ swap) * w:((q ^ swap) + 1) * w],
                                  first, last_)
                    return last

                def gather(e):
                    for s in sets:
                        pe.wait_ge(*me.next("sel_ready"))
                        o = SET[s]
                        for bank_free, count in me.free((i, e, "XG", s)):
                            pe.wait_ge(bank_free, count)
                        b = me.bank((i, e, "XG", s))
                        pt = E["P" + s].rearrange("p (t c) -> p t c", t=o["tc"])
                        for k in range(o["tc"]):
                            last = token_parts(s, b, pt[:, k, :], HTOK[:, o["t0"] + k, :], k == 0, k == o["tc"] - 1)
                        last.then_inc(me.fills((i, e, "XG", s)), 1)

                def turn(e, what, src):
                    for s in sets:
                        for bank_free, count in me.free((i, e, what, s), after=[((i, e, src, s), 0, False)]):
                            pe.wait_ge(bank_free, count)
                        b = me.bank((i, e, what, s))
                        buf = E["XG" + s] if what == "XT" else E["ACT" + s]
                        for k in range(SBX[s]):
                            last = nc.tensor.transpose(b[:, k * P:(k + 1) * P], buf[:, k * P:(k + 1) * P], ident[:, :])
                        last.then_inc(me.fills((i, e, what, s)), 1)

                def share(s, buf, kc):
                    n = SET[s]["n"]
                    q, k = kc // SBX[s], kc % SBX[s]
                    return buf[:, k * P + q * n:k * P + q * n + n]

                def expert_product(e, m, what, src, after, swap=0):
                    views = {}
                    for j, s in enumerate(sets):
                        for bank_free, count in me.free((i, e, what, s), after=after(s)):
                            pe.wait_ge(bank_free, count)
                        b = me.bank((i, e, what, s))
                        for kc in range(DC):
                            if j == 0 and kc % 2 == 0:
                                views[kc // 2] = tile((i, e, "w"), 2, D, 4 * m + kc // 2)
                            last = token_parts(s, b, share(s, src(s), kc), views[kc // 2][:, kc % 2, :],
                                               kc == 0, kc == DC - 1, swap)
                            if j == len(sets) - 1 and kc % 2 == 1 and kc < DC - 1:
                                last.then_inc(me.used_up((i, e, "w"), 4 * m + kc // 2), 1)
                        last.then_inc(me.fills((i, e, what, s)), 1)
                    spent.append(((i, e, "w"), 4 * m + 3))

                def scatter(stage, after):
                    for s in sets:
                        o = SET[s]
                        n, w, tw = o["n"], o["w"], o["tok"]
                        for c in range(DC):
                            q, k = c // SBX[s], c % SBX[s]
                            r = slice(q // 2 * 2 * n, (q // 2 + 1) * 2 * n)
                            for bank_free, count in me.free((i, stage, s), c, after(s) if c == 0 else ()):
                                pe.wait_ge(bank_free, count)
                            b = me.bank((i, stage, s), c)
                            mm(b[:, 0:tw], E["Y" + s][r, q % 2 * w + k * P:q % 2 * w + (k + 1) * P],
                               E["PT" + s][r, q % 2 * tw:(q % 2 + 1) * tw], True, True).then_inc(
                                me.fills((i, stage, s), c), 1)

                gather("first")
                turn("first", "XT", "XG")
                for s in sets:
                    pe.wait_ge(*me.read((i, "first", "XT", s)))
                assert not spent
                with pe.Fori(0, NE // 2) as it:
                    me.begin(it, {"sel_ready": 2 * len(sets)})
                    for e in range(2):
                        xs = lambda s: E["XS" + s][:, e * SET[s]["w"]:(e + 1) * SET[s]["w"]]
                        expert_product(e, 0, "G", xs, lambda s: [((i, 1 - e, "XT", s), 0, e == 0)])
                        expert_product(e, 1, "U", xs, lambda s: ())
                        gather(e)
                        turn(e, "XT", "XG")
                        turn(e, "T", "U")
                        if e == 0:
                            scatter("S", lambda s: [((i, k, what, s), 0, True) for k in (0, 1)
                                                    for what in ("Y", "PT")])
                        expert_product(e, 2, "Y", lambda s: E["AT" + s], lambda s: [((i, e, "T", s), 0, False)], e)
                        for s in sets:
                            o = SET[s]
                            for bank_free, count in me.free((i, e, "PT", s)):
                                pe.wait_ge(bank_free, count)
                            b = me.bank((i, e, "PT", s))
                            tw = o["tc"] * P
                            for k in range(o["tc"]):
                                last = tr(b[:, k * P:(k + 1) * P],
                                          E["Pg" + s][:, e * tw + k * P:e * tw + (k + 1) * P],
                                          ident[:, :], k == 0)
                            last.then_inc(me.fills((i, e, "PT", s)), 1)
                    assert not spent
                    me.end(NE // 2)
                for s in sets:
                    for k in (0, 1):
                        pe.wait_ge(*me.read((i, k, "Y", s), after=NE // 2))
                        pe.wait_ge(*me.read((i, k, "PT", s), after=NE // 2))
                scatter("lastS", lambda s: ())
            for c in range(DC):
                pe.wait_ge(*me.read((LAYERS - 1, "lastS", "x"), c))
            for t in range(TC):
                for k in range(2):
                    for bank_free, count in me.free("yout", 2 * t + k):
                        pe.wait_ge(bank_free, count)
                    b = me.bank("yout", 2 * t + k)
                    for c in range(4):
                        last = nc.tensor.transpose(b[:, c * P:(c + 1) * P], XC[:, 4 * k + c, t * P:(t + 1) * P],
                                                   ident[:, :])
                    last.then_inc(me.fills("yout", 2 * t + k), 1)


_DATA = ["x", "c", "positions", "rel_bias", "w_ada", "b_ada", "g_mix", "w_in", "g_q_lora", "w_uq", "g_kv_lora",
         "w_ukv", "w_up_a", "w_up_b", "w_o", "g_ffn", "w_gate", "w_up", "w_down", "g_final", "c_2", "ctx_2",
         "c_ctx_2", "ada_w_2", "ada_b_2", "norm1_g_2", "norm2_g_2", "w_in_2", "w_fourier_2", "w_pool_2",
         "pool_scale_2", "q_norm_g_2", "k_norm_g_2", "w_out_2", "w_router_2", "w_gate_2", "w_up_2", "w_down_2"]


def kernel(**inputs):
    import numpy as _np
    import concourse.bacc as _bacc
    from concourse import mybir as _mybir
    from concourse.bass_utils import run_bass_kernel_spmd as _run

    nc = _bacc.Bacc("TRN2", target_bir_lowering=False, num_devices=1)
    rows = {name for name, _ in ROWS}
    arrays, args = {}, {}
    for name in _DATA:
        a = _np.ascontiguousarray(inputs[name])
        if name in rows:
            a = a.reshape(-1, P)
        arrays[f"in_{name}"] = a
    for name, a in constants().items():
        arrays[f"in_{name}"] = _np.ascontiguousarray(a)
    for name, a in arrays.items():
        args[name[3:]] = nc.dram_tensor(name, a.shape, _mybir.dt.from_np(a.dtype), kind="ExternalInput").ap()
    out = nc.dram_tensor("out_0", (1, T, D), _mybir.dt.float32, kind="ExternalOutput").ap()
    build(nc, args, out)
    r = _run(nc, [arrays], core_ids=[0])
    return r.results[0]["out_0"]
```
